# Optimizing a Trainium2 kernel written in Bass

```python
import math
import jax, jax.numpy as jnp
from jax import lax
import numpy as np

D_MODEL = 1024
BATCH = 1
SEQ = 512
DEPTH = 2
DEC_BATCH = 8
DEC_SEQ = 1
PAST_LEN = 4096
PAGE_SIZE = 128

N_EVEN = (DEPTH + 1) // 2
N_ODD = DEPTH // 2
D_PLE = 256
D_FF = 4 * D_MODEL
RMS_EPS = 1e-6
GN_EPS = 1e-5
CHUNK = 128

A_HEADS = 8
A_HD = 64
A_W = A_HEADS * A_HD
A_DECAY_LORA = 64
A_AAA_LORA = 64
A_GATE_LORA = 128
A_SHIFT_W = 3 * A_W + A_DECAY_LORA + A_AAA_LORA + A_GATE_LORA
A_SPLITS = [A_W, 2 * A_W, 3 * A_W, 3 * A_W + A_DECAY_LORA, 3 * A_W + A_DECAY_LORA + A_AAA_LORA]
A_LN_EPS = 64e-5

B_HEADS = 4
B_HD = 128
B_W = B_HEADS * B_HD
B_CONV = 4
B_IN_W = 4 * B_W + 2 * B_HEADS
B_SPLITS = [B_W, 2 * B_W, 3 * B_W, 4 * B_W, 4 * B_W + B_HEADS]

MIX0_IN = A_SHIFT_W + B_IN_W
MIX0_OUT = A_W + B_W

C_HEADS = 4
C_DK = 256
C_DV = 512
C_OUT_W = C_HEADS * C_DV
C_IN_W = 2 * C_HEADS * C_DK + 2 * C_OUT_W
ROPE_BASE = 10000.0

kernel_name = 'rwkv7_mlstm_retention_hybrid_step'

def rmsnorm(x, g):
    xf = x.astype(jnp.float32)
    y = xf * lax.rsqrt(jnp.mean(xf * xf, axis=-1, keepdims=True) + RMS_EPS)
    return (y * g.astype(jnp.float32)).astype(x.dtype)

def head_norm(x, g, eps):
    xf = x.astype(jnp.float32)
    mu = jnp.mean(xf, axis=-1, keepdims=True)
    var = jnp.mean(jnp.square(xf - mu), axis=-1, keepdims=True)
    y = ((xf - mu) * lax.rsqrt(var + eps)).reshape(x.shape[:-2] + (-1,))
    return y * g.astype(jnp.float32)

def _chunks(t, L):
    Bsz, T = t.shape[:2]
    return jnp.moveaxis(t.reshape((Bsz, T // L, L) + t.shape[2:]), 1, 0)

def _unchunk(t):
    nc, Bsz, L = t.shape[:3]
    return jnp.moveaxis(t, 0, 1).reshape((Bsz, nc * L) + t.shape[3:])

def rope(x, pos):
    half = x.shape[-1] // 2
    inv = ROPE_BASE ** (-jnp.arange(half, dtype=jnp.float32) / half)
    ang = pos.astype(jnp.float32)[:, None] * inv[None, :]
    cos = jnp.cos(ang)[None, :, None, :]
    sin = jnp.sin(ang)[None, :, None, :]
    x1, x2 = x[..., :half], x[..., half:]
    return jnp.concatenate([x1 * cos - x2 * sin, x1 * sin + x2 * cos], axis=-1)

def rwkv7_recurrence(S0, r, w, k, v, a_vec, b_vec):
    def step(S, inp):
        r_t, w_t, k_t, v_t, a_t, b_t = inp
        sa = jnp.einsum('bhvk,bhk->bhv', S, a_t)
        S = S * w_t[:, :, None, :] + sa[..., None] * b_t[:, :, None, :] + v_t[..., None] * k_t[:, :, None, :]
        return S, jnp.einsum('bhvk,bhk->bhv', S, r_t)
    xs = tuple(jnp.moveaxis(t, 1, 0) for t in (r, w, k, v, a_vec, b_vec))
    S, y = lax.scan(step, S0, xs)
    return jnp.moveaxis(y, 0, 1), S

def mlstm_chunkwise(C0, n0, m0, q, k, v, i_pre, log_f):
    T = q.shape[1]
    L = math.gcd(T, CHUNK)
    causal = jnp.tril(jnp.ones((L, L), dtype=bool))

    def step(carry, inp):
        C, n, m = carry
        qc, kc, vc, ic, fc = inp
        b = jnp.cumsum(fc, axis=1)
        dlog = b[:, :, None, :] - b[:, None, :, :] + ic[:, None, :, :]
        dlog = jnp.where(causal[None, :, :, None], dlog, -jnp.inf)
        inter = b + m[:, None, :]
        m_t = jnp.maximum(inter, jnp.max(dlog, axis=2))
        s = jnp.einsum('bjhd,bihd->bjih', qc, kc) * jnp.exp(dlog - m_t[:, :, None, :])
        iw = jnp.exp(inter - m_t)
        num = jnp.einsum('bjih,bihe->bjhe', s, vc) + iw[..., None] * jnp.einsum('bjhd,bhde->bjhe', qc, C)
        den = jnp.sum(s, axis=2) + iw * jnp.einsum('bjhd,bhd->bjh', qc, n)
        h = num / jnp.maximum(jnp.abs(den), jnp.exp(-m_t))[..., None]
        bL = b[:, -1]
        gi = bL[:, None, :] - b + ic
        m_new = jnp.maximum(bL + m, jnp.max(gi, axis=1))
        wi = jnp.exp(gi - m_new[:, None, :])
        wc = jnp.exp(bL + m - m_new)
        C = wc[..., None, None] * C + jnp.einsum('blh,blhd,blhe->bhde', wi, kc, vc)
        n = wc[..., None] * n + jnp.einsum('blh,blhd->bhd', wi, kc)
        return (C, n, m_new), h

    xs = tuple(_chunks(t, L) for t in (q, k, v, i_pre, log_f))
    (C, n, m), h = lax.scan(step, (C0, n0, m0), xs)
    return _unchunk(h), C, n, m

def retention_chunkwise(S0, q, k, v):
    T, H = q.shape[1], q.shape[2]
    L = math.gcd(T, CHUNK)
    lg = jnp.log1p(-jnp.exp2(-5.0 - jnp.arange(H, dtype=jnp.float32)))
    idx = jnp.arange(L, dtype=jnp.float32)
    diff = idx[:, None] - idx[None, :]
    mask = jnp.where(diff[..., None] >= 0, jnp.exp(jnp.maximum(diff, 0.0)[..., None] * lg), 0.0)
    q_dec = jnp.exp((idx[:, None] + 1.0) * lg)
    k_dec = jnp.exp((L - 1.0 - idx)[:, None] * lg)
    c_dec = jnp.exp(L * lg)

    def step(S, inp):
        qc, kc, vc = inp
        s = jnp.einsum('bjhd,bihd->bjih', qc, kc) * mask[None]
        o = jnp.einsum('bjih,bihe->bjhe', s, vc) + jnp.einsum('bjhd,bhde->bjhe', qc * q_dec[None, :, :, None], S)
        S = c_dec[None, :, None, None] * S + jnp.einsum('bihd,bihe->bhde', kc * k_dec[None, :, :, None], vc)
        return S, o

    xs = tuple(_chunks(t, L) for t in (q, k, v))
    S, o = lax.scan(step, S0, xs)
    return _unchunk(o), S

def mix_even(xn, st, W, e):
    f32 = jnp.float32
    shift_buf, S_a, conv_buf, C, n, m = st
    Bsz, T, _ = xn.shape
    u = xn @ W['mix0_w_in'][e]
    ua, ub = u[..., :A_SHIFT_W], u[..., A_SHIFT_W:]

    ua_prev = jnp.concatenate([shift_buf[:, None, :].astype(ua.dtype), ua[:, :-1]], axis=1)
    ua_s = ua + (ua_prev - ua) * W['rw_mu'][e]
    r, k, v, wd, ad, gd = jnp.split(ua_s, A_SPLITS, axis=-1)
    w_log = -jax.nn.softplus(-(W['rw_w0'][e] + jnp.tanh(wd) @ W['rw_w2'][e])) - 0.5
    decay = jnp.exp(-jnp.exp(w_log.astype(f32)))
    a = jax.nn.sigmoid(W['rw_a0'][e] + ad @ W['rw_a2'][e])
    g = jax.nn.sigmoid(gd) @ W['rw_g2'][e]
    heads = lambda t: t.astype(f32).reshape(Bsz, T, A_HEADS, A_HD)
    kk = heads(k * W['rw_kk'][e])
    kk = kk / jnp.maximum(jnp.sqrt(jnp.sum(kk * kk, axis=-1, keepdims=True)), 1e-12)
    k = k * (1.0 + (a - 1.0) * W['rw_ka'][e])
    rh, kh, vh, ah = heads(r), heads(k), heads(v), heads(a)
    y, S_a = rwkv7_recurrence(S_a.astype(f32), rh, heads(decay), kh, vh, -kk, kk * ah)
    bonus = jnp.sum(rh * kh * W['rw_rk'][e].astype(f32), axis=-1, keepdims=True) * vh
    ya = (head_norm(y, W['rw_ln'][e], A_LN_EPS) + bonus.reshape(Bsz, T, A_W)) * g.astype(f32)

    q, kb, vb, ob, ip, fp = jnp.split(ub, B_SPLITS, axis=-1)
    full = jnp.concatenate([conv_buf.astype(q.dtype), jnp.concatenate([q, kb], axis=-1)], axis=1)
    cw = W['ml_conv_w'][e]
    qk = jax.nn.silu(W['ml_conv_b'][e] + sum(full[:, j:j + T] * cw[j] for j in range(B_CONV)))
    qb, kb = jnp.split(qk, 2, axis=-1)
    mh = lambda t: t.astype(f32).reshape(Bsz, T, B_HEADS, B_HD)
    i_pre = (ip + W['ml_i_bias'][e]).astype(f32)
    log_f = jax.nn.log_sigmoid((fp + W['ml_f_bias'][e]).astype(f32))
    hb, C, n, m = mlstm_chunkwise(C.astype(f32), n.astype(f32), m.astype(f32),
                                  mh(qb), mh(kb) * (B_HD ** -0.5), mh(vb), i_pre, log_f)
    hb = jax.nn.sigmoid(ob.astype(f32)) * hb.reshape(Bsz, T, B_W)
    yb = head_norm(hb.reshape(Bsz, T, B_HEADS, B_HD), W['ml_gn'][e], GN_EPS)

    out = jnp.concatenate([ya, yb], axis=-1).astype(xn.dtype) @ W['mix0_w_out'][e]
    new_st = (ua[:, -1].astype(f32), S_a, full[:, T:].astype(f32), C, n, m)
    return out, new_st

def mix_odd(xn, S, pos, W, o):
    f32 = jnp.float32
    Bsz, T, _ = xn.shape
    u = xn @ W['ret_w_in'][o]
    q, k, v, g = jnp.split(u, [C_HEADS * C_DK, 2 * C_HEADS * C_DK, 2 * C_HEADS * C_DK + C_OUT_W], axis=-1)
    q = rope(q.astype(f32).reshape(Bsz, T, C_HEADS, C_DK), pos)
    k = rope(k.astype(f32).reshape(Bsz, T, C_HEADS, C_DK), pos) * (C_DK ** -0.5)
    v = v.astype(f32).reshape(Bsz, T, C_HEADS, C_DV)
    y, S = retention_chunkwise(S.astype(f32), q, k, v)
    y = head_norm(y, W['ret_gn'][o], GN_EPS) * jax.nn.silu(g.astype(f32))
    return y.astype(xn.dtype) @ W['ret_w_out'][o], S

def trunk(x, p, pos, ev_states, od_states, W):
    new_ev = [[] for _ in ev_states]
    new_od = []
    h = x
    for li in range(DEPTH):
        g = W['norm_g'][li]
        xn = rmsnorm(h, g[0])
        if li % 2 == 0:
            e = li // 2
            mix, nst = mix_even(xn, tuple(s[e] for s in ev_states), W, e)
            for lst, s in zip(new_ev, nst):
                lst.append(s)
        else:
            o = li // 2
            mix, S = mix_odd(xn, od_states[o], pos, W, o)
            new_od.append(S)
        h = h + rmsnorm(mix, g[1])
        f = jnp.square(jax.nn.relu(rmsnorm(h, g[2]) @ W['ffn_up'][li])) @ W['ffn_down'][li]
        h = h + rmsnorm(f, g[3])
        h = h + jax.nn.sigmoid(h @ W['ple_gate'][li]) * (p[li] @ W['ple_proj'][li])
    return h, [jnp.stack(l) for l in new_ev], jnp.stack(new_od)

def setup_inputs(seed: int = 0) -> dict:
    key = jax.random.key(seed)
    ks = jax.random.split(key, 40)
    f32 = jnp.float32
    nrm = lambda i, shape, scale: scale * jax.random.normal(ks[i], shape, f32)
    gain = lambda i, shape: 1.0 + nrm(i, shape, 0.05)
    d = {}
    d['x_prompt'] = nrm(0, (BATCH, SEQ, D_MODEL), 1.0)
    d['x_sample'] = nrm(1, (DEC_BATCH, DEC_SEQ, D_MODEL), 1.0)
    d['state_rwkv_shift'] = nrm(2, (N_EVEN, DEC_BATCH, A_SHIFT_W), 1.0)
    d['state_rwkv_S'] = nrm(3, (N_EVEN, DEC_BATCH, A_HEADS, A_HD, A_HD), 0.3)
    d['state_mlstm_conv'] = nrm(4, (N_EVEN, DEC_BATCH, B_CONV - 1, 2 * B_W), 1.0)
    d['state_mlstm_C'] = nrm(5, (N_EVEN, DEC_BATCH, B_HEADS, B_HD, B_HD), 0.1)
    d['state_mlstm_n'] = nrm(6, (N_EVEN, DEC_BATCH, B_HEADS, B_HD), 0.3)
    d['state_mlstm_m'] = 1.0 + nrm(7, (N_EVEN, DEC_BATCH, B_HEADS), 1.0)
    d['state_ret_S'] = nrm(8, (N_ODD, DEC_BATCH, C_HEADS, C_DK, C_DV), 0.05)
    d['p_prompt'] = nrm(9, (DEPTH, BATCH, SEQ, D_PLE), 1.0)
    d['p_sample'] = nrm(10, (DEPTH, DEC_BATCH, DEC_SEQ, D_PLE), 1.0)
    d['norm_g'] = gain(11, (DEPTH, 4, D_MODEL))
    d['ffn_up'] = nrm(12, (DEPTH, D_MODEL, D_FF), D_MODEL ** -0.5)
    d['ffn_down'] = nrm(13, (DEPTH, D_FF, D_MODEL), D_FF ** -0.5)
    d['ple_gate'] = nrm(14, (DEPTH, D_MODEL, D_MODEL), D_MODEL ** -0.5)
    d['ple_proj'] = nrm(15, (DEPTH, D_PLE, D_MODEL), 0.5 * D_PLE ** -0.5)
    d['mix0_w_in'] = nrm(16, (N_EVEN, D_MODEL, MIX0_IN), D_MODEL ** -0.5)
    d['rw_mu'] = jax.random.uniform(ks[17], (N_EVEN, A_SHIFT_W), f32)
    d['rw_w0'] = jnp.linspace(-6.5, -1.5, A_W, dtype=f32)[None, :] + nrm(18, (N_EVEN, A_W), 0.1)
    d['rw_w2'] = nrm(19, (N_EVEN, A_DECAY_LORA, A_W), 0.5 * A_DECAY_LORA ** -0.5)
    d['rw_a0'] = nrm(20, (N_EVEN, A_W), 0.1)
    d['rw_a2'] = nrm(21, (N_EVEN, A_AAA_LORA, A_W), 0.5 * A_AAA_LORA ** -0.5)
    d['rw_g2'] = nrm(22, (N_EVEN, A_GATE_LORA, A_W), A_GATE_LORA ** -0.5)
    d['rw_kk'] = 0.85 + nrm(23, (N_EVEN, A_W), 0.05)
    d['rw_ka'] = 1.0 + nrm(24, (N_EVEN, A_W), 0.05)
    d['rw_rk'] = nrm(25, (N_EVEN, A_HEADS, A_HD), 0.1)
    d['rw_ln'] = gain(26, (N_EVEN, A_W))
    d['ml_conv_w'] = nrm(27, (N_EVEN, B_CONV, 2 * B_W), 0.5)
    d['ml_conv_b'] = nrm(28, (N_EVEN, 2 * B_W), 0.02)
    d['ml_i_bias'] = nrm(29, (N_EVEN, B_HEADS), 0.1)
    d['ml_f_bias'] = jnp.linspace(3.0, 6.0, B_HEADS, dtype=f32)[None, :] + nrm(30, (N_EVEN, B_HEADS), 0.1)
    d['ml_gn'] = gain(31, (N_EVEN, B_W))
    d['mix0_w_out'] = nrm(32, (N_EVEN, MIX0_OUT, D_MODEL), MIX0_OUT ** -0.5)
    d['ret_w_in'] = nrm(33, (N_ODD, D_MODEL, C_IN_W), D_MODEL ** -0.5)
    d['ret_gn'] = gain(34, (N_ODD, C_OUT_W))
    d['ret_w_out'] = nrm(35, (N_ODD, C_OUT_W, D_MODEL), C_OUT_W ** -0.5)
    return d

def reference(x_prompt, x_sample, state_rwkv_shift, state_rwkv_S, state_mlstm_conv, state_mlstm_C,
              state_mlstm_n, state_mlstm_m, state_ret_S, p_prompt, p_sample, norm_g, ffn_up, ffn_down,
              ple_gate, ple_proj, mix0_w_in, rw_mu, rw_w0, rw_w2, rw_a0, rw_a2, rw_g2, rw_kk, rw_ka,
              rw_rk, rw_ln, ml_conv_w, ml_conv_b, ml_i_bias, ml_f_bias, ml_gn, mix0_w_out,
              ret_w_in, ret_gn, ret_w_out):
    W = dict(norm_g=norm_g, ffn_up=ffn_up, ffn_down=ffn_down, ple_gate=ple_gate, ple_proj=ple_proj,
             mix0_w_in=mix0_w_in, rw_mu=rw_mu, rw_w0=rw_w0, rw_w2=rw_w2, rw_a0=rw_a0, rw_a2=rw_a2,
             rw_g2=rw_g2, rw_kk=rw_kk, rw_ka=rw_ka, rw_rk=rw_rk, rw_ln=rw_ln, ml_conv_w=ml_conv_w,
             ml_conv_b=ml_conv_b, ml_i_bias=ml_i_bias, ml_f_bias=ml_f_bias, ml_gn=ml_gn,
             mix0_w_out=mix0_w_out, ret_w_in=ret_w_in, ret_gn=ret_gn, ret_w_out=ret_w_out)
    f32 = jnp.float32
    Bp, Tp = x_prompt.shape[:2]
    Ts = x_sample.shape[1]
    ev0 = (jnp.zeros((N_EVEN, Bp, A_SHIFT_W), f32),
           jnp.zeros((N_EVEN, Bp, A_HEADS, A_HD, A_HD), f32),
           jnp.zeros((N_EVEN, Bp, B_CONV - 1, 2 * B_W), f32),
           jnp.zeros((N_EVEN, Bp, B_HEADS, B_HD, B_HD), f32),
           jnp.zeros((N_EVEN, Bp, B_HEADS, B_HD), f32),
           jnp.zeros((N_EVEN, Bp, B_HEADS), f32))
    od0 = jnp.zeros((N_ODD, Bp, C_HEADS, C_DK, C_DV), f32)
    y_prompt, ev_p, ret_p = trunk(x_prompt, p_prompt, jnp.arange(Tp), ev0, od0, W)
    ev_s_in = (state_rwkv_shift, state_rwkv_S, state_mlstm_conv, state_mlstm_C, state_mlstm_n, state_mlstm_m)
    y_sample, ev_s, ret_s = trunk(x_sample, p_sample, PAST_LEN + jnp.arange(Ts), ev_s_in, state_ret_S, W)
    p_shift, p_Sa, p_conv, p_C, p_n, p_m = ev_p
    s_shift, s_Sa, s_conv, s_C, s_n, s_m = ev_s
    return (y_prompt, y_sample, p_shift, p_Sa, p_conv, p_C, p_n, p_m, ret_p,
            s_shift, s_Sa, s_conv, s_C, s_n, s_m, ret_s)


_drawn_inputs = setup_inputs


def setup_inputs(seed=0):
    import zlib

    import numpy as np

    out = dict(_drawn_inputs(seed))
    spreads = {}
    factors = {'rw_w2': 2.996}
    for name, (base, spread) in spreads.items():
        noise = np.random.default_rng([zlib.crc32(name.encode()), seed]).standard_normal(out[name].shape)
        drawn = base * np.exp(spread * noise) if base else spread * noise
        out[name] = __import__('jax').numpy.asarray(drawn.astype(out[name].dtype))
    for name, factor in factors.items():
        out[name] = (out[name] * factor).astype(out[name].dtype)
    return out
```

```python
from contextlib import ExitStack

import numpy as np

import concourse.bass as bass
from concourse import mybir

F32 = mybir.dt.float32
ALU = mybir.AluOpType
ACT = mybir.ActivationFunctionType

P = 128
D = 1024
KD = D // P
TP = 512
NS = 8
T = TP + NS
HALF = T // 2
FF = 4 * D
KF = FF // P
PLE = 256
KP = PLE // P
L = 128
NG = TP // L
SUB = 64
AH, AHD = 8, 64
BH, BHD = 4, 128
CH, CDK, CDV = 4, 256, 512
NA = 14
NB = 16
RMS_EPS = 1e-6
GN_EPS = 1e-5
A_LN_EPS = 64e-5
C0 = float(np.exp(-0.5))
SLAB = 32 * P
NEG = -1e30


def columns(parts):
    at, out = 0, {}
    for name, n in parts:
        out[name] = (at, n)
        at += n
    return out, at


VEC, NVEC = columns([
    ("norm_g", 64), ("mu", NA), ("w0", 4), ("a0", 4), ("kk", 4), ("ka", 4), ("rk", 4), ("rln", 4),
    ("cw", 32), ("cb", 8), ("mgn", 4), ("rgn", 16), ("ib", 1), ("fb", 1), ("m", NS),
    ("shift", NA * NS), ("conv", 8 * 3 * NS), ("n", BH * NS), ("wif", KD * 36), ("w2a2", 512), ("g2", 512)])
CON, NCON = columns([
    ("ident", P), ("ones", P), ("mean_d", P), ("ones64", P), ("mean64", P), ("mean128", P), ("mean512", P),
    ("gram", 2 * P), ("bd16", P), ("n1t", P), ("n2", P), ("reset", P), ("neg", P), ("sel", 4 * P),
    ("cos", T), ("sin", T), ("rmask", CH * P), ("qdec", CH * P), ("kdec", CH), ("cdec", CH)])


def shape_constants():
    f = np.float32
    c = np.zeros((P, NCON), f)

    def put(name, a):
        at, n = CON[name]
        c[:a.shape[0], at:at + n] = a.reshape(a.shape[0], n)

    i = np.arange(P)
    row, col = i[:, None], i[None, :]
    put("ident", np.eye(P, dtype=f))
    put("ones", np.ones((P, P), f))
    put("mean_d", np.full((P, P), 1.0 / D, f))
    same64 = row // 64 == col // 64
    put("ones64", same64.astype(f))
    put("mean64", same64.astype(f) / f(64))
    put("mean128", np.full((P, P), 1.0 / 128, f))
    put("mean512", np.full((P, P), 1.0 / 512, f))
    put("gram", np.concatenate([same64 & (row < col), same64 & (row <= col)], 1).astype(f))
    put("bd16", (row // 16 == col // 16).astype(f))
    put("n1t", ((col // 16 % 2 == 1) & (row // 16 == col // 16 - 1)).astype(f))
    put("n2", ((row // 32 % 2 == 1) & (col // 32 == row // 32 - 1)).astype(f))
    put("reset", np.broadcast_to((col % SUB != 0).astype(f), (P, P)))
    put("neg", np.where(row <= col, 0.0, NEG).astype(f))
    sel = np.zeros((4, 4, P), f)
    for h in range(4):
        sel[h, h] = 1.0
    put("sel", sel.reshape(4, -1))
    half = CDK // 2
    pos = np.concatenate([np.arange(TP), np.full(NS, 4096)]).astype(f)
    inv = (f(10000.0) ** (-np.arange(half, dtype=f) / f(half))).astype(f)
    ang = (pos[None, :] * inv[:, None]).astype(f)
    put("cos", np.cos(ang))
    put("sin", np.sin(ang))
    lg = np.log1p(-np.exp2(-5.0 - np.arange(CH)))
    put("rmask", np.stack([np.where(row <= col, np.exp(np.maximum(col - row, 0) * g), 0.0) for g in lg], 1))
    put("qdec", np.broadcast_to(np.stack([np.exp((i + 1) * g) for g in lg])[None], (P, CH, P)))
    put("kdec", np.stack([np.exp((L - 1 - i) * g) for g in lg], 1))
    put("cdec", np.broadcast_to(np.exp(lg)[None], (P, CH)))
    return c


CDEC_CHUNK = [float(np.exp(L * np.log1p(-np.exp2(-5.0 - h)))) for h in range(CH)]
CDEC_ONE = [float(np.exp(np.log1p(-np.exp2(-5.0 - h)))) for h in range(CH)]


class Steps:

    def __init__(self, sem, names, base=0):
        self.sem, self.names, self.base, self.at_now = sem, names, base, 0

    def at(self, name, it=0):
        return self.sem, it * len(self.names) + (self.base + self.names.index(name) + 1)

    def step(self, name):
        want = self.names[self.at_now % len(self.names)]
        assert name == want, (name, want)
        self.at_now += 1
        return self.sem, 1


class Space:

    def __init__(self, stretches):
        self.free = [[ap, ap.shape[1], 0] for ap in stretches]

    def take(self, *dims):
        n = int(np.prod(dims))
        for s in self.free:
            if s[2] + n <= s[1]:
                ap = s[0][:, s[2]:s[2] + n]
                s[2] += n
                if len(dims) == 1:
                    return ap
                names = "abcd"[:len(dims)]
                return ap.rearrange(f"p ({' '.join(names)}) -> p {' '.join(names)}",
                                    **{k: d for k, d in zip(names[1:], dims[1:])})
        raise AssertionError(f"no room for {dims}: {[(s[1], s[2]) for s in self.free]}")


GEMMS, _s, _t = {}, 0, 0
for _name, _slabs, _tiles, _per in [
        ("in0", 8, NA + NB, 4), ("out0", 2, 8, 4), ("up0", 8, KF, 4), ("down0", 8, 8, 1), ("gate0", 2, 8, 4),
        ("qkv", 8, 32, 4), ("g", 4, 16, 4), ("out1", 4, 8, 2), ("up1", 8, KF, 4), ("down1", 8, 8, 1),
        ("gate1", 2, 8, 4)]:
    GEMMS[_name] = (_s, _t, _slabs, _tiles, _per)
    _s, _t = _s + _slabs, _t + _tiles
NSLAB = _s

RW_DVE = ["kkr", "cum0", "cum1", "prev", "floor", "rinv", "kk", "ka0", "ka1", "kp", "at", "rt", "kka", "bt", "kt",
          "bh", "kh", "bon", "ad0", "ad1", "me0", "me1", "d0", "n2", "t1", "d2t", "t2", "d4t", "t4", "t8", "z",
          "t16", "zz", "tt", "qp", "gh0", "gh1", "s0a", "s0b", "mid", "s1a", "s1b", "end", "yc", "vinv", "yn",
          "yg0", "yg1", "out"]
RW_ACT = ["v", "sq", "p", "q", "pm", "norm", "ar", "br", "vr", "mv", "d2", "d4", "d8t", "t8t", "t16t", "w",
          "y", "ysq", "ysd"]
RW_POOL = ["rk", "rkw", "d0t", "n1t"]
RW_PE = ["norm", "bonus", "rows", "gram_b", "gram_k", "a", "mv", "d2", "d2t", "t2", "d4", "d4t", "t4", "d8t",
         "t8", "t8t", "z", "t16", "t16t", "zz", "tt", "w", "qp", "gh", "s0", "s1", "y", "mean", "var"]


def program(nc, stop=None, **dram):
    with ExitStack() as ctx:
        def sb(name, n):
            return ctx.enter_context(nc.sbuf_tensor(name, [P, n], F32))

        def sem(name):
            return ctx.enter_context(nc.semaphore(name))

        con, vec = sb("con", NCON), sb("vec", NVEC)
        hbuf = [sb("h_a", KD * T), sb("h_b", KD * T)]
        xg_t = sb("xg", KD * T)
        big = sb("big", KF * T)
        slot = [sb("slot0", SLAB), sb("slot1", SLAB)]
        pjw = sb("pjw", KP * KD * P)
        rb_t = sb("rb", T)
        free = sb("free", 6400)
        ps = ctx.enter_context(nc.psum_tensor("ps", [P, 8, 512], F32))

        def tiles(t, n=KD, w=T):
            return t[:, 0:n * w].rearrange("p (k t) -> p k t", t=w)

        hb = [tiles(t) for t in hbuf]
        xg, hid = tiles(xg_t), tiles(big, KF)
        ua = big[:, 0:NA * (T + 1)].rearrange("p (k t) -> p k t", t=T + 1)
        ub = big[:, NA * (T + 1):NA * (T + 1) + NB * T].rearrange("p (k t) -> p k t", t=T)
        rb = rb_t[:, :]
        tail = Space([free[:, :]])
        sqr = [tail.take(T), tail.take(T)]
        ss = tail.take(T)
        rt = tail.take(T)
        tmp = [tail.take(T), tail.take(T)]
        pt = tail.take(KP, T)

        def C(name, i=0, n=None):
            a, w = CON[name]
            n = w if n is None else n
            return con[:, a + i:a + i + n]

        def V(name, i=0, n=1):
            a, _ = VEC[name]
            return vec[:, a + i:a + i + n]

        def two(ap):
            return ap.rearrange("p (a n) -> p a n", a=2)

        def bank(par):
            return ps[:, 2 * par:2 * par + 2, 0:HALF]

        s_vec, s_con, s_x = sem("vec_loaded"), sem("con_loaded"), sem("x_loaded")
        s_w = [sem("slab_loaded0"), sem("slab_loaded1")]
        s_tile = sem("tile_done")
        s_bank = sem("bank_free")
        s_xg = sem("xg_ready")
        s_st = sem("stats_done")
        s_rt = sem("rms_ready")
        s_rb = sem("rinv_ready")
        s_sq = sem("square_ready")
        s_ss = sem("square_summed")
        s_h = sem("h_ready")
        s_res = sem("residual_step")
        s_relu = sem("relu_ready")
        s_hid = sem("hidden_ready")
        s_pj_w, s_pt = sem("proj_weights_loaded"), sem("p_loaded")
        s_pj = sem("proj_done")
        s_pjc = sem("proj_copied")
        s_e = sem("gate_exp")
        s_pl = sem("gate_step")
        s_hn = sem("next_h_ready")
        s_out = sem("stored")
        outs = [0]
        MIXER_STORES = 16 * 7

        def store(eng, dst, src):
            outs[0] += 16
            eng.dma_start(dst, src).then_inc(s_out, 16)
            return outs[0]

        def part(name, names_by_engine):
            return {k: Steps(sem(f"{name}_{k}"), v, int(k == "dve")) for k, v in names_by_engine.items()}

        def gemm(pe, name, nk, rhs, before=None):
            slab0, tile0, slabs, ntiles, per = GEMMS[name]

            def slab(i, s, count, waits):
                pe.wait_ge(s_w[s], 16 * (slab0 // 2 + 1) + 16 * i)
                for mt in range(count):
                    pe.wait_ge(s_bank, (tile0 + s * per + mt + 1) + 2 * per * i)
                    par = (s * per + mt) % 2
                    for kt in range(nk):
                        if waits and s == 0 and mt == 0:
                            pe.wait_ge(*waits(kt))
                        for hf in range(2):
                            at = (mt * nk + kt) * P
                            mm = pe.matmul(ps[:, 2 * par + hf, 0:HALF], slot[s][:, at:at + P], rhs(kt, hf),
                                           start=(kt == 0), stop=(kt == nk - 1))
                    mm.then_inc(s_tile, 1)

            whole = ntiles // (2 * per)
            with pe.Fori(0, whole) as i:
                for s in range(2):
                    slab(i, s, per, before)
            left = ntiles - whole * 2 * per
            if left:
                slab(whole, 0, per, None)
                slab(whole, 1, left - per, None)

        def tile_at(name, k, i=0, step=0):
            return (GEMMS[name][1] + k + 1) + step * i

        def pe_prenorm(pe, n):
            for kt in range(KD):
                pe.wait_ge(s_xg, 8 * n + kt + 1)
                for hf in range(2):
                    mm = pe.matmul(ps[:, 4 + hf, 0:HALF], C("mean_d"),
                                   hid[:, 24 + kt, hf * HALF:(hf + 1) * HALF], start=(kt == 0), stop=(kt == KD - 1))
            mm.then_inc(s_st, 1)

        def pe_postnorm(pe, n):
            pe.wait_ge(s_ss, 8 * n + 8)
            for hf in range(2):
                mm = pe.matmul(ps[:, 4 + hf, 0:HALF], C("mean_d"), ss[:, hf * HALF:(hf + 1) * HALF],
                               start=True, stop=True)
            mm.then_inc(s_st, 1)

        def act_rms(act, r):
            act.wait_ge(s_st, r + 1)
            if r:
                act.wait_ge(s_rb, r)
            nc.scalar.activation(two(rt), ps[:, 4:6, 0:HALF], ACT.Sqrt, bias=RMS_EPS).then_inc(s_rt, 1)

        def dve_rinv(dve, r):
            dve.wait_ge(s_rt, r + 1)
            nc.vector.reciprocal(rb, rt).then_inc(s_rb, 1)
            dve.wait_ge(s_rb, r + 1)

        def act_prenorm(act, n, h, gain, ready):
            for kt in range(KD):
                act.wait_ge(*ready(kt))
                nc.scalar.activation(xg[:, kt, :], h[:, kt, :], ACT.Copy, scale=V("norm_g", gain * 8 + kt))
                nc.scalar.activation(hid[:, 24 + kt, :], h[:, kt, :], ACT.Square).then_inc(s_xg, 1)


        def act_outproj(act, name, n, out):
            for mt in range(KD):
                act.wait_ge(s_tile, tile_at(name, mt))
                if 8 * n + mt >= 2:
                    act.wait_ge(s_ss, 8 * n + mt - 1)
                nc.scalar.activation(two(sqr[mt % 2]), bank(mt % 2), ACT.Square).then_inc(s_sq, 1)
                nc.scalar.activation(two(out[:, mt, :]), bank(mt % 2), ACT.Copy).then_inc(s_bank, 1)

        def pool_sum(pool, n):
            for mt in range(KD):
                pool.wait_ge(s_sq, 8 * n + mt + 1)
                if mt == 0:
                    nc.gpsimd.tensor_copy(ss, sqr[0]).then_inc(s_ss, 1)
                else:
                    pool.wait_ge(s_ss, 8 * n + mt)
                    nc.gpsimd.tensor_tensor(ss, ss, sqr[mt % 2], ALU.add).then_inc(s_ss, 1)

        def dve_residual(dve, n, out, h, gain):
            for kt in range(KD):
                nc.vector.scalar_tensor_tensor(tmp[0], out[:, kt, :], V("norm_g", gain * 8 + kt), rb,
                                               ALU.mult, ALU.mult).then_inc(s_res, 1)
                dve.wait_ge(s_res, 8 * n + kt + 1)
                nc.vector.tensor_tensor(h[:, kt, :], h[:, kt, :], tmp[0], ALU.add).then_inc(s_h, 1)
                dve.wait_ge(s_h, 8 * n + kt + 1)

        ds = bass.ds
        half_b, xg_q = 4 * T, 4 * T
        sig = tiles(hbuf[1], 4)
        aa = xg[:, 0:4, :]
        gg = xg[:, 4:8, :]
        used0 = tail.free[0][2]
        pieces = [hbuf[0][:, :], free[:, used0:], hbuf[1][:, half_b:], pjw[:, :],
                  big[:, NA * (T + 1) + NB * T:], free[:, 0:3 * T], free[:, 6 * T:6 * T + KP * T]]


        r0 = Space(pieces)
        sho = r0.take(NA, NS + 1)
        cvo = r0.take(8, 11)
        ct = r0.take(NG * BH)
        sr = r0.take(24)
        mo = r0.take(NS + 1)
        s_buf = [r0.take(2, P), r0.take(2, P)]
        crow, nmrow, nmtrow = tmp[0], tmp[1], rt

        pair = lambda ap: ap.rearrange("p (j t) -> p j t", j=2)
        RH = r0.take(2, 4, 64)
        rhf = RH.rearrange("p a h n -> p (a h n)")
        kkr, ksq = pair(rhf[:, 0:256]), pair(rhf[:, 256:512])
        knr, kkn, cum, pp, qq, pm, kp, tb = [r0.take(2, P) for _ in range(8)]
        AR = r0.take(2, 2, P)
        bt, kt_, bh, kh, vS = [r0.take(2, P) for _ in range(5)]
        bht, kht, vt = [r0.take(4, 64) for _ in range(3)]
        AD, ME = r0.take(4, 2 * P), r0.take(4, 2 * P)
        d0, d0t, n1t, n2, t1, d2, d2t, t2 = [r0.take(4, P) for _ in range(8)]
        GH = r0.take(2, 4, P)
        ghf = GH.rearrange("p c a n -> p (c a n)")
        d4, d4t = [ghf[:, i * 512:(i + 1) * 512].rearrange("p (h n) -> p h n", h=4) for i in range(2)]
        t4, d8t, t8, t8t, zb, t16, t16t, zz, tt = t1, d0t, t2, d2, d2t, d4, d4t, d0, t1
        Wb = t2.rearrange("p h n -> p (h n)")
        qp, yb_, yc, ysq, yr, sh_ = knr, kkn, cum, qq, pm, tb
        rkb = kkn

        def bk(b, n=4):
            return ps[:, b, 0:n * P].rearrange("p (h t) -> p h t", t=P)

        def bc(ap, n):
            return ap.unsqueeze(2).to_broadcast([ap.shape[0], ap.shape[1], n])

        def mid(ap, k):
            return ap.unsqueeze(1).to_broadcast([ap.shape[0], k, ap.shape[1]])

        rw = part("rwkv", dict(pe=RW_PE, dve=RW_DVE, act=RW_ACT, pool=RW_POOL))
        rp, rd, ra, rl = rw["pe"], rw["dve"], rw["act"], rw["pool"]
        s_zero, s_rs = sem("state_zeroed"), sem("rwkv_state_stored")

        def uah(arr, h, g):
            return ua[:, ds(2 * h + arr, 2), ds(L * g + 1, L)]

        def th(x, h, g):
            return x[:, ds(2 * h, 2), ds(L * g, L)]

        def dve_rwkv(dve):
            v = nc.vector
            with dve.Fori(0, 2) as h:
                dve.wait_ge(s_rs, 16 * h + 1)
                v.memset(s_buf[0], 0.0).then_inc(s_zero, 1)
                with dve.Fori(0, NG) as g:
                    it = 4 * h + g

                    def after(steps, name):
                        dve.wait_ge(*steps.at(name, it))
                    v.tensor_tensor(kkr, uah(4, h, g), bc(vec[:, ds(VEC["kk"][0] + 2 * h, 2)], L),
                                    ALU.mult).then_inc(*rd.step("kkr"))
                    for j in range(2):
                        v.tensor_tensor_scan(cum[:, j, :], C("reset"), sig[:, 2 * h + j, ds(L * g, L)], 0.0,
                                             ALU.mult, ALU.add).then_inc(*rd.step(f"cum{j}"))
                    after(rd, "cum1")
                    v.tensor_tensor(tb, cum, th(sig, h, g), ALU.subtract).then_inc(*rd.step("prev"))
                    after(rp, "norm")
                    v.tensor_scalar(knr, bk(0, 2), 1e-24, None, ALU.max).then_inc(*rd.step("floor"))
                    after(ra, "norm")
                    v.reciprocal(knr, knr).then_inc(*rd.step("rinv"))
                    after(rd, "rinv")
                    v.tensor_tensor(kkn, kkr, knr, ALU.mult).then_inc(*rd.step("kk"))
                    after(ra, "pm")
                    for j in range(2):
                        v.tensor_scalar(tb[:, j, :], aa[:, 2 * h + j, ds(L * g, L)], -1.0,
                                        vec[:, ds(VEC["ka"][0] + 2 * h + j, 1)], ALU.add,
                                        ALU.mult).then_inc(*rd.step(f"ka{j}"))
                    after(rd, "ka1")
                    v.scalar_tensor_tensor(kp, tb, 1.0, uah(4, h, g), ALU.add, ALU.mult).then_inc(*rd.step("kp"))
                    v.scalar_tensor_tensor(AR[:, :, 0, :], kkn, -1.0, pm, ALU.mult, ALU.mult).then_inc(*rd.step("at"))
                    v.tensor_tensor(AR[:, :, 1, :], uah(0, h, g), pp, ALU.mult).then_inc(*rd.step("rt"))
                    after(rd, "kp")
                    v.tensor_tensor(tb, kkn, th(aa, h, g), ALU.mult).then_inc(*rd.step("kka"))
                    after(rd, "kka")
                    v.tensor_tensor(bt, tb, qq, ALU.mult).then_inc(*rd.step("bt"))
                    v.tensor_tensor(kt_, kp, qq, ALU.mult).then_inc(*rd.step("kt"))
                    after(rd, "kt")
                    last = pp.rearrange("p j (c n) -> p (j c) n", n=SUB)[:, :, SUB - 1:SUB].to_broadcast([P, 4, SUB])
                    by_chunk = lambda ap: ap.rearrange("p j (c n) -> p (j c) n", n=SUB)
                    v.tensor_tensor(by_chunk(bh), by_chunk(bt), last, ALU.mult).then_inc(*rd.step("bh"))
                    v.tensor_tensor(by_chunk(kh), by_chunk(kt_), last, ALU.mult).then_inc(*rd.step("kh"))
                    after(rp, "bonus")
                    after(rp, "rows")
                    v.tensor_tensor(vS, ps[:, 0, 256:512].rearrange("p (j t) -> p j t", j=2), vS,
                                    ALU.mult).then_inc(*rd.step("bon"))
                    after(rp, "gram_b")
                    for par in range(2):
                        o = AD.rearrange("p (j q) n -> p q j n", q=2)[:, par]
                        v.tensor_tensor(o, ps[:, 3 + par, :].rearrange("p (j n) -> p j n", j=2),
                                        mid(C("gram"), 2), ALU.mult).then_inc(*rd.step(f"ad{par}"))
                    after(rp, "gram_k")
                    for par in range(2):
                        o = ME.rearrange("p (j q) n -> p q j n", q=2)[:, par]
                        v.tensor_tensor(o, ps[:, 5 + par, :].rearrange("p (j n) -> p j n", j=2),
                                        mid(C("gram"), 2), ALU.mult).then_inc(*rd.step(f"me{par}"))
                    after(rp, "a")
                    v.tensor_tensor(d0, bk(7), mid(C("bd16"), 4), ALU.mult).then_inc(*rd.step("d0"))
                    v.tensor_tensor(n2, bk(7), mid(C("n2"), 4), ALU.mult).then_inc(*rd.step("n2"))
                    after(rd, "d0")
                    v.tensor_tensor(t1, d0, mid(C("ident"), 4), ALU.add).then_inc(*rd.step("t1"))
                    after(rp, "d2t")
                    v.tensor_copy(d2t, bk(2)).then_inc(*rd.step("d2t"))
                    after(rp, "t2")
                    after(rd, "t1")
                    v.tensor_tensor(t2, bk(3), t1, ALU.add).then_inc(*rd.step("t2"))
                    after(rp, "d4t")
                    v.tensor_copy(d4t, bk(5)).then_inc(*rd.step("d4t"))
                    after(rp, "t4")
                    v.tensor_tensor(t4, bk(6), t2, ALU.add).then_inc(*rd.step("t4"))
                    after(rp, "t8")
                    after(rd, "t4")
                    v.tensor_tensor(t8, bk(2), t4, ALU.add).then_inc(*rd.step("t8"))
                    after(rp, "z")
                    v.tensor_copy(zb, bk(4)).then_inc(*rd.step("z"))
                    after(rp, "t16")
                    v.tensor_tensor(t16, bk(5), t8, ALU.add).then_inc(*rd.step("t16"))
                    after(rp, "zz")
                    v.tensor_copy(zz, bk(1)).then_inc(*rd.step("zz"))
                    after(rp, "tt")
                    v.tensor_tensor(tt, bk(2), t16t, ALU.add).then_inc(*rd.step("tt"))
                    after(rp, "qp")
                    v.tensor_tensor(qp, bk(4, 2), AR[:, :, 1, :], ALU.add).then_inc(*rd.step("qp"))
                    after(rp, "gh")
                    for c in range(2):
                        v.tensor_tensor(GH[:, c], bk(5 + c), mid(C("ones64"), 4),
                                        ALU.mult).then_inc(*rd.step(f"gh{c}"))
                    after(rd, "gh1")
                    dve.wait_ge(s_zero, h + 1)
                    for c in range(2):
                        for j in range(2):
                            v.scalar_tensor_tensor(sh_[:, j, :], s_buf[c][:, j, :],
                                                   pp[:, j, SUB * c + SUB - 1:SUB * c + SUB], GH[:, c, 2 + j],
                                                   ALU.mult, ALU.add).then_inc(*rd.step(f"s{c}{'ab'[j]}"))
                        after(rd, f"s{c}b")
                        after(rp, f"s{c}")
                        v.tensor_tensor(s_buf[1 - c], bk(c, 2), sh_, ALU.add).then_inc(*rd.step(["mid", "end"][c]))
                        after(rd, ["mid", "end"][c])
                    after(rp, "mean")
                    v.tensor_tensor(yc, yb_, bk(2, 2), ALU.subtract).then_inc(*rd.step("yc"))
                    after(ra, "ysd")
                    v.reciprocal(yr, yr).then_inc(*rd.step("vinv"))
                    after(rd, "vinv")
                    v.tensor_tensor(yc, yc, yr, ALU.mult).then_inc(*rd.step("yn"))
                    after(rd, "yn")
                    for j in range(2):
                        v.scalar_tensor_tensor(yc[:, j, :], yc[:, j, :], vec[:, ds(VEC["rln"][0] + 2 * h + j, 1)],
                                               vS[:, j, :], ALU.mult, ALU.add).then_inc(*rd.step(f"yg{j}"))
                    after(rd, "yg1")
                    v.tensor_tensor(uah(0, h, g), yc, th(gg, h, g), ALU.mult).then_inc(*rd.step("out"))
                    after(rd, "out")

        def act_rwkv(act):
            a = nc.scalar
            with act.Fori(0, 2) as h:
                with act.Fori(0, NG) as g:
                    it = 4 * h + g

                    def after(steps, name, back=0):
                        act.wait_ge(*steps.at(name, it - back))
                    after(rd, "out", 1)
                    a.activation(vS, uah(8, h, g), ACT.Copy).then_inc(*ra.step("v"))
                    after(rd, "kkr")
                    a.activation(ksq, kkr, ACT.Square).then_inc(*ra.step("sq"))
                    after(rd, "cum1")
                    a.activation(pp, cum, ACT.Exp, scale=-C0).then_inc(*ra.step("p"))
                    a.activation(qq, cum, ACT.Exp, scale=C0).then_inc(*ra.step("q"))
                    after(rd, "prev")
                    a.activation(pm, tb, ACT.Exp, scale=-C0).then_inc(*ra.step("pm"))
                    after(rd, "floor")
                    a.activation(knr, knr, ACT.Sqrt).then_inc(*ra.step("norm"))
                    after(rp, "rows")
                    r4 = lambda b, k: ps[:, b, 256 * k:256 * k + 256].rearrange("p (h n) -> p h n", h=4)
                    a.activation(RH[:, 0], r4(1, 0), ACT.Copy).then_inc(*ra.step("ar"))
                    a.activation(bht, r4(1, 1), ACT.Copy)
                    a.activation(kht, r4(2, 0), ACT.Copy).then_inc(*ra.step("br"))
                    a.activation(vt, r4(2, 1), ACT.Copy).then_inc(*ra.step("vr"))
                    after(rp, "mv")
                    a.activation(RH[:, 1], r4(0, 0), ACT.Copy).then_inc(*ra.step("mv"))
                    for name, out, b in [("d2", d2, 1), ("d4", d4, 4), ("d8t", d8t, 1), ("t8t", t8t, 3),
                                         ("t16t", t16t, 6)]:
                        after(rp, name)
                        a.activation(out, bk(b), ACT.Copy).then_inc(*ra.step(name))
                    after(rp, "w")
                    a.activation(Wb.rearrange("p (a h n) -> p h a n", a=2, h=4),
                                 bk(3).rearrange("p h (a n) -> p h a n", a=2), ACT.Copy).then_inc(*ra.step("w"))
                    after(rp, "y")
                    a.activation(yb_, bk(7, 2), ACT.Copy).then_inc(*ra.step("y"))
                    after(rd, "yc")
                    a.activation(ysq, yc, ACT.Square).then_inc(*ra.step("ysq"))
                    after(rp, "var")
                    a.activation(yr, bk(3, 2), ACT.Sqrt, bias=A_LN_EPS).then_inc(*ra.step("ysd"))

        def pool_rwkv(pool):
            with pool.Fori(0, 2) as h:
                with pool.Fori(0, NG) as g:
                    it = 4 * h + g
                    pool.wait_ge(*rd.at("kka", it))
                    nc.gpsimd.tensor_tensor(rkb, uah(0, h, g), kp, ALU.mult).then_inc(*rl.step("rk"))
                    pool.wait_ge(*rl.at("rk", it))
                    nc.gpsimd.tensor_tensor(rkb, rkb, bc(vec[:, ds(VEC["rk"][0] + 2 * h, 2)], L),
                                            ALU.mult).then_inc(*rl.step("rkw"))
                    pool.wait_ge(*rd.at("ad1", it))
                    nc.gpsimd.tensor_tensor(d0t, AD[:, :, 0:P], mid(C("bd16"), 4), ALU.mult).then_inc(*rl.step("d0t"))
                    nc.gpsimd.tensor_tensor(n1t, AD[:, :, 0:P], mid(C("n1t"), 4), ALU.mult).then_inc(*rl.step("n1t"))

        def pe_rwkv(pe):
            def mm4(b, lhs, rhs, step):
                for hh in range(4):
                    mm = pe.matmul(bk(b)[:, hh, :], lhs[:, hh, :], rhs[:, hh, :], start=True, stop=True)
                mm.then_inc(*rp.step(step))

            with pe.Fori(0, 2) as h:
                with pe.Fori(0, NG) as g:
                    it = 4 * h + g

                    def after(steps, name):
                        pe.wait_ge(*steps.at(name, it))
                    after(ra, "sq")
                    pe.matmul(ps[:, 0, 0:256], C("ones64"), ksq, start=True, stop=True).then_inc(*rp.step("norm"))
                    after(rl, "rkw")
                    after(rd, "floor")
                    pe.matmul(ps[:, 0, 256:512], C("ones64"), rkb, start=True, stop=True).then_inc(*rp.step("bonus"))
                    after(rd, "kh")
                    for j in range(2):
                        pe.transpose(ps[:, 1, j * P:(j + 1) * P], AR[:, j, 0, :], C("ident"))
                        pe.transpose(ps[:, 1, 256 + j * P:256 + (j + 1) * P], bh[:, j, :], C("ident"))
                        pe.transpose(ps[:, 2, j * P:(j + 1) * P], kh[:, j, :], C("ident"))
                        mm = pe.transpose(ps[:, 2, 256 + j * P:256 + (j + 1) * P], vS[:, j, :], C("ident"))
                    mm.then_inc(*rp.step("rows"))
                    for b, w, step in [(3, bt, "gram_b"), (5, kt_, "gram_k")]:
                        for par in range(2):
                            rows = slice(64 * par, 64 * par + 64)
                            for j in range(2):
                                mm = pe.matmul(ps[:, b + par, 256 * j:256 * j + 256], w[rows, j, :],
                                               AR[rows, j, :, :], start=True, stop=True)
                        mm.then_inc(*rp.step(step))
                    after(rd, "ad1")
                    for hh in range(4):
                        mm = pe.transpose(bk(7)[:, hh, :], AD[:, hh, 0:P], C("ident"))
                    mm.then_inc(*rp.step("a"))
                    after(rd, "me1")
                    after(rd, "bon")
                    after(ra, "vr")
                    for hh in range(4):
                        mm = pe.matmul(ps[:, 0, 64 * hh:64 * hh + 64], ME[:, hh, 0:P], vt[:, hh, :],
                                       start=True, stop=True)
                    mm.then_inc(*rp.step("mv"))
                    after(rl, "d0t")
                    after(rd, "d0")
                    mm4(1, d0t, d0, "d2")
                    mm4(2, d0, d0t, "d2t")
                    after(rd, "d2t")
                    after(rd, "t1")
                    mm4(3, d2t, t1, "t2")
                    after(ra, "d2")
                    mm4(4, d2t, d2, "d4")
                    mm4(5, d2, d2t, "d4t")
                    after(rd, "d4t")
                    after(rd, "t2")
                    mm4(6, d4t, t2, "t4")
                    after(ra, "d4")
                    mm4(1, d4, d4t, "d8t")
                    after(ra, "d8t")
                    after(rd, "t4")
                    mm4(2, d8t, t4, "t8")
                    after(rd, "t8")
                    for hh in range(4):
                        mm = pe.transpose(bk(3)[:, hh, :], t8[:, hh, :], C("ident"))
                    mm.then_inc(*rp.step("t8t"))
                    after(rl, "n1t")
                    mm4(4, n1t, t8, "z")
                    after(rd, "z")
                    after(ra, "t8t")
                    mm4(5, t8t, zb, "t16")
                    after(rd, "t16")
                    for hh in range(4):
                        mm = pe.transpose(bk(6)[:, hh, :], t16[:, hh, :], C("ident"))
                    mm.then_inc(*rp.step("t16t"))
                    after(ra, "t16t")
                    mm4(1, n2, t16t, "zz")
                    after(rd, "zz")
                    mm4(2, t16, zz, "tt")
                    after(rd, "tt")
                    after(ra, "mv")
                    for hh in range(4):
                        mm = pe.matmul(bk(3)[:, hh, :].rearrange("p (a n) -> p a n", a=2), tt[:, hh, :],
                                       RH[:, :, hh, :], start=True, stop=True)
                    mm.then_inc(*rp.step("w"))
                    after(ra, "w")
                    w1 = lambda hh: Wb[:, 64 * hh:64 * hh + 64]
                    u0 = lambda hh: Wb[:, 256 + 64 * hh:256 + 64 * hh + 64]
                    for hh in range(4):
                        j, par = hh // 2, hh % 2
                        mm = pe.matmul(ps[64 * par:64 * par + 64, 4, j * P:(j + 1) * P], w1(hh), AD[:, hh, P:2 * P],
                                       start=True, stop=True)
                    mm.then_inc(*rp.step("qp"))
                    for c in range(2):
                        rows = slice(64 * c, 64 * c + 64)
                        for j in range(2):
                            two_heads = slice(P * j, P * j + P)
                            bhj = bht.rearrange("p h n -> p (h n)")[rows, two_heads]
                            khj = kht.rearrange("p h n -> p (h n)")[rows, two_heads]
                            vtj = vt.rearrange("p h n -> p (h n)")[rows, two_heads]
                            pe.matmul(bk(5 + c)[:, j, :], Wb[rows, two_heads], bhj, start=True, stop=True)
                            pe.matmul(bk(5 + c)[:, 2 + j, :], bhj, Wb[rows, 256 + P * j:256 + P * j + P],
                                      start=True, stop=False)
                            mm = pe.matmul(bk(5 + c)[:, 2 + j, :], khj, vtj, start=False, stop=True)
                    mm.then_inc(*rp.step("gh"))
                    for hh in range(4):
                        j, par = hh // 2, hh % 2
                        o = ps[64 * par:64 * par + 64, 7, j * P:(j + 1) * P]
                        pe.matmul(o, u0(hh), AD[:, hh, P:2 * P], start=(j == 0), stop=False, skip_group_check=True)
                        pe.matmul(o, vt[:, hh, :], ME[:, hh, P:2 * P], start=False, stop=False, skip_group_check=True)
                    after(rd, "qp")
                    for c in range(2):
                        after(rd, ["gh1", "mid"][c])
                        for j in range(2):
                            mm = pe.matmul(bk(c)[:, j, :], GH[:, c, j, :], s_buf[c][:, j, :], start=True, stop=True)
                        mm.then_inc(*rp.step(f"s{c}"))
                        for j in range(2):
                            mm = pe.matmul(ps[:, 7, j * P + SUB * c:j * P + SUB * c + SUB], s_buf[c][:, j, :],
                                           qp[:, j, SUB * c:SUB * c + SUB], start=False, stop=(c == 1),
                                           skip_group_check=True)
                    mm.then_inc(*rp.step("y"))
                    after(ra, "y")
                    pe.matmul(bk(2, 2), C("mean64"), yb_, start=True, stop=True).then_inc(*rp.step("mean"))
                    after(ra, "ysq")
                    pe.matmul(bk(3, 2), C("mean64"), ysq, start=True, stop=True).then_inc(*rp.step("var"))

        r1 = Space([pieces[0][:, 1024:], *pieces[1:]])
        sst = r1.take(4, NS, 64)
        um, vm = r1.take(2, NS, 64), r1.take(2, NS, 64)
        rows3 = r1.take(3, 4, P)
        xk, xq, xn, xkk, xw, xa, xkp, xb, xan, xbo, xy, xyc, xr = [r1.take(4, NS) for _ in range(13)]
        RS_DVE = ["kkr", "floor", "rinv", "kk", "a1", "ka", "kp", "an", "b", "rk", "rkw", "bon"]
        RS_DVEJ = ["um", "vm", "sw", "s"]
        RS_DVE2 = ["yc", "rinv2", "yn", "yl", "yg", "out"]
        rs_sem = {k: sem(f"rwkv1_{k}") for k in ("pe", "dve", "act")}
        sd = Steps(rs_sem["dve"], RS_DVE)
        sdj = Steps(rs_sem["dve"], RS_DVEJ, len(RS_DVE))
        sd2 = Steps(rs_sem["dve"], RS_DVE2, len(RS_DVE) + 4 * len(RS_DVEJ))
        sa = Steps(rs_sem["act"], ["sq", "norm", "w", "rows", "y", "ysq", "ysd"])
        sp_ = Steps(rs_sem["pe"], ["norm", "bonus", "rows"])
        spj = Steps(rs_sem["pe"], ["sa", "outer"], 3)
        sp2 = Steps(rs_sem["pe"], ["y", "mean", "var"], 3 + 8)
        s_sst, s_cst = sem("rwkv_state_loaded"), sem("mlstm_state_loaded")
        uas = lambda arr: ua[:, arr:arr + 4, TP + 1:]
        smp = lambda x: x[:, :, TP:]
        eight = C("ident")[0:NS, 0:NS]

        def dve_rwkv1(dve):
            v = nc.vector

            def after(steps, name, it=0):
                dve.wait_ge(*steps.at(name, it))
            v.tensor_tensor(xk, uas(4), bc(V("kk", 0, 4), NS), ALU.mult).then_inc(*sd.step("kkr"))
            after(sp_, "norm")
            v.tensor_scalar(xn, ps[:, 0, 0:32].rearrange("p (j t) -> p j t", j=4), 1e-24, None,
                            ALU.max).then_inc(*sd.step("floor"))
            after(sa, "norm")
            v.reciprocal(xn, xn).then_inc(*sd.step("rinv"))
            after(sd, "rinv")
            v.tensor_tensor(xkk, xk, xn, ALU.mult).then_inc(*sd.step("kk"))
            v.tensor_scalar(xa, smp(aa), -1.0, None, ALU.add).then_inc(*sd.step("a1"))
            after(sd, "a1")
            v.tensor_tensor(xa, xa, bc(V("ka", 0, 4), NS), ALU.mult).then_inc(*sd.step("ka"))
            after(sd, "ka")
            v.scalar_tensor_tensor(xkp, xa, 1.0, uas(4), ALU.add, ALU.mult).then_inc(*sd.step("kp"))
            v.tensor_scalar(xan, xkk, -1.0, None, ALU.mult).then_inc(*sd.step("an"))
            v.tensor_tensor(xb, xkk, smp(aa), ALU.mult).then_inc(*sd.step("b"))
            after(sd, "kp")
            v.tensor_tensor(xbo, uas(0), xkp, ALU.mult).then_inc(*sd.step("rk"))
            after(sd, "rk")
            v.tensor_tensor(xbo, xbo, bc(V("rk", 0, 4), NS), ALU.mult).then_inc(*sd.step("rkw"))
            after(sp_, "bonus")
            v.tensor_tensor(xbo, ps[:, 0, 32:64].rearrange("p (j t) -> p j t", j=4), uas(8),
                            ALU.mult).then_inc(*sd.step("bon"))
            dve.wait_ge(s_sst, 16)
            after(sa, "rows")
            for j in range(4):
                after(spj, "sa", j)
                b = 2 * (j % 2)
                v.tensor_tensor(um[0:NS], ps[0:NS, b:b + 2, :].rearrange("p q (s n) -> p q s n", s=NS),
                                eight.unsqueeze(1).unsqueeze(3).to_broadcast([NS, 2, NS, 64]),
                                ALU.mult).then_inc(*sdj.step("um"))
                vr = rows3[0:NS, 2, j, :].rearrange("p (q n) -> p q n", q=2)
                v.tensor_tensor(vm[0:NS], vr.unsqueeze(2).to_broadcast([NS, 2, NS, 64]),
                                eight.unsqueeze(1).unsqueeze(3).to_broadcast([NS, 2, NS, 64]),
                                ALU.mult).then_inc(*sdj.step("vm"))
                v.tensor_tensor(sst[:, j], sst[:, j], bc(xw[:, j, :], 64), ALU.mult).then_inc(*sdj.step("sw"))
                after(sdj, "sw", j)
                after(spj, "outer", j)
                v.tensor_tensor(sst[:, j], sst[:, j], ps[:, 4 + j % 2, :].rearrange("p (s n) -> p s n", s=NS),
                                ALU.add).then_inc(*sdj.step("s"))
            after(sp2, "mean")
            v.tensor_tensor(xyc, xy, ps[:, 0, 0:32].rearrange("p (j t) -> p j t", j=4),
                            ALU.subtract).then_inc(*sd2.step("yc"))
            after(sa, "ysd")
            v.reciprocal(xr, xr).then_inc(*sd2.step("rinv2"))
            after(sd2, "rinv2")
            v.tensor_tensor(xyc, xyc, xr, ALU.mult).then_inc(*sd2.step("yn"))
            after(sd2, "yn")
            v.tensor_tensor(xyc, xyc, bc(V("rln", 0, 4), NS), ALU.mult).then_inc(*sd2.step("yl"))
            after(sd2, "yl")
            v.tensor_tensor(xyc, xyc, xbo, ALU.add).then_inc(*sd2.step("yg"))
            after(sd2, "yg")
            v.tensor_tensor(uas(0), xyc, smp(gg), ALU.mult).then_inc(*sd2.step("out"))
            after(sd2, "out")

        def act_rwkv1(act):
            a = nc.scalar

            def after(steps, name, it=0):
                act.wait_ge(*steps.at(name, it))
            after(sd, "kkr")
            a.activation(xq, xk, ACT.Square).then_inc(*sa.step("sq"))
            after(sd, "floor")
            a.activation(xn, xn, ACT.Sqrt).then_inc(*sa.step("norm"))
            a.activation(xw, smp(sig), ACT.Exp, scale=-C0).then_inc(*sa.step("w"))
            after(sp_, "rows")
            a.activation(rows3[0:NS].rearrange("p k j n -> p k (j n)"), ps[0:NS, 4:7, :],
                         ACT.Copy).then_inc(*sa.step("rows"))
            after(sp2, "y")
            a.activation(xy[0:64], ps[0:64, 6, 0:32].rearrange("p (j t) -> p j t", j=4), ACT.Copy)
            a.activation(xy[64:P], ps[64:P, 7, 0:32].rearrange("p (j t) -> p j t", j=4),
                         ACT.Copy).then_inc(*sa.step("y"))
            after(sd2, "yc")
            a.activation(xq, xyc, ACT.Square).then_inc(*sa.step("ysq"))
            after(sp2, "var")
            a.activation(xr, ps[:, 1, 0:32].rearrange("p (j t) -> p j t", j=4), ACT.Sqrt,
                         bias=A_LN_EPS).then_inc(*sa.step("ysd"))

        def pe_rwkv1(pe):
            def after(steps, name, it=0):
                pe.wait_ge(*steps.at(name, it))
            flat = lambda x: x.rearrange("p j t -> p (j t)")
            after(sa, "sq")
            pe.matmul(ps[:, 0, 0:32], C("ones64"), flat(xq), start=True, stop=True).then_inc(*sp_.step("norm"))
            after(sd, "rkw")
            pe.matmul(ps[:, 0, 32:64], C("ones64"), flat(xbo), start=True, stop=True).then_inc(*sp_.step("bonus"))
            for k, src in enumerate([xb, xkp, uas(8)]):
                for j in range(4):
                    mm = pe.transpose(ps[0:NS, 4 + k, j * P:(j + 1) * P], src[:, j, :], C("ident"))
            mm.then_inc(*sp_.step("rows"))
            after(sd, "bon")
            pe.wait_ge(s_sst, 16)
            for j in range(4):
                if j >= 2:
                    after(sdj, "um", j - 2)
                for par in range(2):
                    r = slice(64 * par, 64 * par + 64)
                    mm = pe.matmul(ps[0:NS, 2 * (j % 2) + par, :], xan[r, j, :],
                                   sst[r, j].rearrange("p s n -> p (s n)"), start=True, stop=True)
                mm.then_inc(*spj.step("sa"))
                after(sdj, "vm", j)
                if j >= 2:
                    after(sdj, "s", j - 2)
                after(sa, "rows")
                for par in range(2):
                    o = ps[64 * par:64 * par + 64, 4 + j % 2, :]
                    c = slice(64 * par, 64 * par + 64)
                    pe.matmul(o, rows3[0:NS, 0, j, c], um[0:NS, par].rearrange("p s n -> p (s n)"),
                              start=True, stop=False)
                    mm = pe.matmul(o, rows3[0:NS, 1, j, c], vm[0:NS, par].rearrange("p s n -> p (s n)"),
                                   start=False, stop=True)
                mm.then_inc(*spj.step("outer"))
            after(sdj, "s", 3)
            for j in range(4):
                for b in range(NS):
                    for par in range(2):
                        r = slice(64 * par, 64 * par + 64)
                        mm = pe.matmul(ps[r, 6 + par, NS * j + b:NS * j + b + 1], sst[r, j, b, :],
                                       ua[r, j, TP + 1 + b:TP + 2 + b], start=True, stop=True)
            mm.then_inc(*sp2.step("y"))
            after(sa, "y")
            pe.matmul(ps[:, 0, 0:32], C("mean64"), flat(xy), start=True, stop=True).then_inc(*sp2.step("mean"))
            after(sa, "ysq")
            pe.matmul(ps[:, 1, 0:32], C("mean64"), flat(xq), start=True, stop=True).then_inc(*sp2.step("var"))

        r2 = Space([pieces[0][:, 1024:], *pieces[1:]])
        kS, vS2, PT, IW, QI, EN, HD, HB, E, KH = [r2.take(4, P) for _ in range(10)]
        cn = r2.take(4, 2 * P)
        vo = r2.take(4, 2 * P)
        mprev, wia, wi, wca, wc = [r2.take(4) for _ in range(5)]
        ml = part("mlstm", dict(
            pe=["nm", "nb", "rows", "sc", "num", "den", "st", "mean", "var"],
            dve=["wia", "wca", "e0", "e1", "e2", "e3", "iwa", "mprev", "kh", "pt", "qi", "c0", "c1", "c2", "c3",
                 "hd", "hr", "hb", "ho", "yc", "rinv", "yn", "out"],
            act=["k", "v", "wi", "wc", "e", "iw", "en", "vo", "abs", "ysq", "ysd"]))
        mp, md, ma = ml["pe"], ml["dve"], ml["act"]
        s_mz = sem("mlstm_zeroed")
        ubg = lambda arr, g: ub[:, arr:arr + 4, ds(L * g, L)]

        def dve_mlstm(dve):
            v = nc.vector
            dve.wait_ge(s_st1, 16)
            v.memset(cn, 0.0).then_inc(s_mz, 1)
            v.memset(mprev, 0.0).then_inc(s_mz, 1)
            v.memset(vo[:, :, P:2 * P], 1.0).then_inc(s_mz, 1)
            dve.wait_ge(s_mz, 3)
            with dve.Fori(0, NG) as g:
                def after(steps, name):
                    dve.wait_ge(*steps.at(name, g))
                after(mp, "nm")
                nml = bk(0)[:, :, P - 1]
                v.tensor_tensor(wia, ct[:, ds(4 * g, 4)], nml, ALU.add).then_inc(*md.step("wia"))
                v.tensor_tensor(wca, mprev, nml, ALU.add).then_inc(*md.step("wca"))
                for h in range(4):
                    v.scalar_tensor_tensor(E[:, h, :], bk(0)[:, h, :], ct[:, ds(4 * g + h, 1)], C("neg"),
                                           ALU.add, ALU.min).then_inc(*md.step(f"e{h}"))
                v.tensor_tensor(IW, bk(0), bc(mprev, P), ALU.add).then_inc(*md.step("iwa"))
                after(md, "iwa")
                v.tensor_scalar(mprev, nml, -1.0, None, ALU.mult).then_inc(*md.step("mprev"))
                after(mp, "rows")
                after(ma, "wc")
                v.tensor_tensor(KH, bk(2), bc(wi, P), ALU.mult).then_inc(*md.step("kh"))
                after(mp, "sc")
                after(ma, "iw")
                v.tensor_tensor(PT, bk(4), E, ALU.mult).then_inc(*md.step("pt"))
                v.tensor_tensor(QI, ubg(0, g), IW, ALU.mult).then_inc(*md.step("qi"))
                after(mp, "st")
                for h in range(4):
                    v.scalar_tensor_tensor(cn[:, h, :], cn[:, h, :], wc[:, h:h + 1],
                                           ps[:, 2 + h // 2, 256 * (h % 2):256 * (h % 2) + 256],
                                           ALU.mult, ALU.add).then_inc(*md.step(f"c{h}"))
                after(ma, "abs")
                v.tensor_tensor(HD, HD, EN, ALU.max).then_inc(*md.step("hd"))
                after(md, "hd")
                v.reciprocal(HD, HD).then_inc(*md.step("hr"))
                after(md, "hr")
                v.tensor_tensor(HB, bk(5), HD, ALU.mult).then_inc(*md.step("hb"))
                after(md, "hb")
                v.tensor_tensor(HB, HB, ubg(12, g), ALU.mult).then_inc(*md.step("ho"))
                after(mp, "mean")
                v.tensor_tensor(HB, HB, bk(4), ALU.subtract).then_inc(*md.step("yc"))
                after(ma, "ysd")
                v.reciprocal(HD, HD).then_inc(*md.step("rinv"))
                after(md, "rinv")
                v.tensor_tensor(HB, HB, HD, ALU.mult).then_inc(*md.step("yn"))
                after(md, "yn")
                v.tensor_tensor(ubg(0, g), HB, bc(V("mgn", 0, 4), P), ALU.mult).then_inc(*md.step("out"))
                after(md, "out")

        def act_mlstm(act):
            a = nc.scalar
            with act.Fori(0, NG) as g:
                def after(steps, name, back=0):
                    act.wait_ge(*steps.at(name, g - back))
                after(md, "out", 1)
                a.activation(kS, ubg(4, g), ACT.Copy, scale=BHD ** -0.5).then_inc(*ma.step("k"))
                a.activation(vS2, ubg(8, g), ACT.Copy).then_inc(*ma.step("v"))
                after(md, "wca")
                a.activation(wi, wia, ACT.Exp).then_inc(*ma.step("wi"))
                a.activation(wc, wca, ACT.Exp).then_inc(*ma.step("wc"))
                after(md, "e3")
                a.activation(E, E, ACT.Exp).then_inc(*ma.step("e"))
                after(md, "iwa")
                a.activation(IW, IW, ACT.Exp).then_inc(*ma.step("iw"))
                after(mp, "nb")
                a.activation(EN, bk(1), ACT.Exp).then_inc(*ma.step("en"))
                after(mp, "rows")
                a.activation(vo[:, :, 0:P], bk(3), ACT.Copy).then_inc(*ma.step("vo"))
                after(mp, "den")
                a.activation(HD, bk(6), ACT.Abs).then_inc(*ma.step("abs"))
                after(md, "yc")
                a.activation(E, HB, ACT.Square).then_inc(*ma.step("ysq"))
                after(mp, "var")
                a.activation(HD, bk(7), ACT.Sqrt, bias=GN_EPS).then_inc(*ma.step("ysd"))

        def pe_mlstm(pe):
            sel = lambda h: C("sel", h * P, P)[0:4]
            pe.wait_ge(*sd2.at("out"))
            with pe.Fori(0, NG) as g:
                def after(steps, name, back=0):
                    pe.wait_ge(*steps.at(name, g - back))
                after(md, "out", 1)
                for h in range(4):
                    mm = pe.matmul(bk(0)[:, h, :], sel(h), nmrow[0:4, ds(L * g, L)], start=True, stop=True)
                mm.then_inc(*mp.step("nm"))
                for h in range(4):
                    mm = pe.matmul(bk(1)[:, h, :], sel(h), nmtrow[0:4, ds(L * g, L)], start=True, stop=True)
                mm.then_inc(*mp.step("nb"))
                after(ma, "v")
                for h in range(4):
                    pe.transpose(bk(2)[:, h, :], kS[:, h, :], C("ident"))
                    mm = pe.transpose(bk(3)[:, h, :], vS2[:, h, :], C("ident"))
                mm.then_inc(*mp.step("rows"))
                for h in range(4):
                    mm = pe.matmul(bk(4)[:, h, :], kS[:, h, :], ub[:, h, ds(L * g, L)], start=True, stop=True)
                mm.then_inc(*mp.step("sc"))
                after(md, "qi")
                after(ma, "vo")
                pe.wait_ge(s_mz, 3)
                for h in range(4):
                    pe.matmul(bk(5)[:, h, :], vo[:, h, 0:P], PT[:, h, :], start=True, stop=False)
                    mm = pe.matmul(bk(5)[:, h, :], cn[:, h, 0:P], QI[:, h, :], start=False, stop=True)
                mm.then_inc(*mp.step("num"))
                for h in range(4):
                    pe.matmul(bk(6)[:, h, :], C("ones"), PT[:, h, :], start=True, stop=False)
                    mm = pe.matmul(bk(6)[:, h, :], cn[:, h, P:2 * P], QI[:, h, :], start=False, stop=True)
                mm.then_inc(*mp.step("den"))
                for h in range(4):
                    mm = pe.matmul(ps[:, 2 + h // 2, 256 * (h % 2):256 * (h % 2) + 256], KH[:, h, :], vo[:, h, :],
                                   start=True, stop=True)
                mm.then_inc(*mp.step("st"))
                after(md, "ho")
                pe.matmul(bk(4), C("mean128"), HB, start=True, stop=True).then_inc(*mp.step("mean"))
                after(ma, "ysq")
                pe.matmul(bk(7), C("mean128"), E, start=True, stop=True).then_inc(*mp.step("var"))

        r3 = Space([pieces[0][:, 1024:], *pieces[1:]])
        vm3 = r3.take(NS, P)
        rows2 = r3.take(2, 4, P)
        n_new, khs, qn, hs, dn, ys = [r3.take(4, NS) for _ in range(6)]
        sb3 = r3.take(4, 24)
        cst = xg[:, :, :].rearrange("p k t -> p (k t)")[:, 0:4 * NS * P].rearrange("p (h s n) -> p h s n", h=4, s=NS)
        m1_sem = {k: sem(f"mlstm1_{k}") for k in ("pe", "dve", "act")}
        nd = Steps(m1_sem["dve"], ["kh", "nw", "n", "qn"])
        ndj = Steps(m1_sem["dve"], ["vm", "cw", "c"], 4)
        nd2 = Steps(m1_sem["dve"], ["dn", "dr", "h", "ho", "yc", "rinv", "yn", "out"], 4 + 12)
        na = Steps(m1_sem["act"], ["exp", "bc", "rows", "abs", "ysq", "ysd"])
        np_ = Steps(m1_sem["pe"], ["bc", "rows", "qn"])
        npj = Steps(m1_sem["pe"], ["outer"], 3)
        np2 = Steps(m1_sem["pe"], ["num", "mean", "var"], 3 + 4)
        ubs = lambda arr: ub[:, arr:arr + 4, TP:]
        p32 = lambda b: ps[:, b, 0:32].rearrange("p (h s) -> p h s", h=4)

        def dve_mlstm1(dve):
            v = nc.vector

            def after(steps, name, it=0):
                dve.wait_ge(*steps.at(name, it))
            after(na, "bc")
            iw, wi1, en1 = [sb3[:, :, 8 * k:8 * k + 8] for k in range(3)]
            v.scalar_tensor_tensor(khs, ubs(4), BHD ** -0.5, wi1, ALU.mult, ALU.mult).then_inc(*nd.step("kh"))
            v.tensor_tensor(n_new, V("n", 0, 32).rearrange("p (h s) -> p h s", h=4), iw,
                            ALU.mult).then_inc(*nd.step("nw"))
            after(nd, "nw")
            v.tensor_tensor(n_new, n_new, khs, ALU.add).then_inc(*nd.step("n"))
            after(nd, "n")
            v.tensor_tensor(qn, n_new, ubs(0), ALU.mult).then_inc(*nd.step("qn"))
            after(na, "rows")
            dve.wait_ge(s_cst, 16)
            for h in range(4):
                if h:
                    after(npj, "outer", h - 1)
                v.tensor_tensor(vm3[0:NS], mid(rows2[0:NS, 1, h, :], NS), bc(eight, P),
                                ALU.mult).then_inc(*ndj.step("vm"))
                v.tensor_tensor(cst[:, h], cst[:, h], bc(iw[:, h, :], P), ALU.mult).then_inc(*ndj.step("cw"))
                after(ndj, "cw", h)
                after(npj, "outer", h)
                b = 2 * (h % 2)
                v.tensor_tensor(cst[:, h], cst[:, h],
                                ps[:, b:b + 2, :].rearrange("p q (s n) -> p (q s) n", n=P),
                                ALU.add).then_inc(*ndj.step("c"))
            after(na, "abs")
            v.tensor_tensor(dn, dn, en1, ALU.max).then_inc(*nd2.step("dn"))
            after(nd2, "dn")
            v.reciprocal(dn, dn).then_inc(*nd2.step("dr"))
            after(nd2, "dr")
            after(np2, "num")
            v.tensor_tensor(hs, p32(7), dn, ALU.mult).then_inc(*nd2.step("h"))
            after(nd2, "h")
            v.tensor_tensor(hs, hs, ubs(12), ALU.mult).then_inc(*nd2.step("ho"))
            after(np2, "mean")
            v.tensor_tensor(hs, hs, p32(4), ALU.subtract).then_inc(*nd2.step("yc"))
            after(na, "ysd")
            v.reciprocal(dn, dn).then_inc(*nd2.step("rinv"))
            after(nd2, "rinv")
            v.tensor_tensor(hs, hs, dn, ALU.mult).then_inc(*nd2.step("yn"))
            after(nd2, "yn")
            v.tensor_tensor(ubs(0), hs, bc(V("mgn", 0, 4), NS), ALU.mult).then_inc(*nd2.step("out"))

        def act_mlstm1(act):
            a = nc.scalar

            def after(steps, name, it=0):
                act.wait_ge(*steps.at(name, it))
            act.wait_ge(*row_d.at("en"))
            a.activation(sr[0:4], sr[0:4], ACT.Exp).then_inc(*na.step("exp"))
            after(np_, "bc")
            a.activation(sb3, ps[:, 0, 0:96].rearrange("p (h n) -> p h n", h=4), ACT.Copy).then_inc(*na.step("bc"))
            after(np_, "rows")
            a.activation(rows2[0:NS].rearrange("p k h n -> p k (h n)"), ps[0:NS, 4:6, :],
                         ACT.Copy).then_inc(*na.step("rows"))
            after(np_, "qn")
            a.activation(dn, p32(6), ACT.Abs).then_inc(*na.step("abs"))
            after(nd2, "yc")
            a.activation(ys, hs, ACT.Square).then_inc(*na.step("ysq"))
            after(np2, "var")
            a.activation(dn, p32(5), ACT.Sqrt, bias=GN_EPS).then_inc(*na.step("ysd"))

        def pe_mlstm1(pe):
            def after(steps, name, it=0):
                pe.wait_ge(*steps.at(name, it))
            flat = lambda x: x.rearrange("p j t -> p (j t)")
            after(md, "out", NG - 1)
            after(na, "exp")
            for h in range(4):
                mm = pe.matmul(ps[:, 0, 24 * h:24 * h + 24], C("sel", h * P, P)[0:4], sr[0:4, :],
                               start=True, stop=True)
            mm.then_inc(*np_.step("bc"))
            after(nd, "kh")
            for h in range(4):
                pe.transpose(ps[0:NS, 4, h * P:(h + 1) * P], khs[:, h, :], C("ident"))
                mm = pe.transpose(ps[0:NS, 5, h * P:(h + 1) * P], ubs(8)[:, h, :], C("ident"))
            mm.then_inc(*np_.step("rows"))
            after(nd, "qn")
            pe.matmul(ps[:, 6, 0:32], C("ones"), flat(qn), start=True, stop=True).then_inc(*np_.step("qn"))
            after(na, "rows")
            for h in range(4):
                after(ndj, "vm", h)
                if h >= 2:
                    after(ndj, "c", h - 2)
                for q in range(2):
                    mm = pe.matmul(ps[:, 2 * (h % 2) + q, :], rows2[0:NS, 0, h, :],
                                   vm3[0:NS, 4 * q:4 * q + 4, :], start=True, stop=True)
                mm.then_inc(*npj.step("outer"))
            after(ndj, "c", 3)
            for h in range(4):
                for b in range(NS):
                    mm = pe.matmul(ps[:, 7, NS * h + b:NS * h + b + 1], cst[:, h, b, :],
                                   ub[:, h, TP + b:TP + b + 1], start=True, stop=True)
            mm.then_inc(*np2.step("num"))
            after(nd2, "ho")
            pe.matmul(ps[:, 4, 0:32], C("mean128"), flat(hs), start=True, stop=True).then_inc(*np2.step("mean"))
            after(na, "ysq")
            pe.matmul(ps[:, 5, 0:32], C("mean128"), flat(ys), start=True, stop=True).then_inc(*np2.step("var"))

        s_ev, s_sub, s_shf = sem("in_evacuated"), sem("shift_difference"), sem("shift_mixed")
        s_raw = sem("raw_saved")
        s_tn, s_lp, s_lc = sem("lora_inputs"), sem("lora_products"), sem("lora_outputs")
        s_cv, s_cvd = sem("convolution_step"), sem("silu_done")
        s_zc = sem("zero_column")
        acc = [sqr[0], sqr[1]]
        RD = ["i", "ib", "f", "fb", "abs", "lf", "zero", "b", "c", "m", "nm", "nmt", "mo", "t", "tm", "iw", "wi",
              "en", "ct"]
        row_d, row_a, row_p = (Steps(sem(f"rows_{k}"), n) for k, n in
                               [("dve", RD), ("act", ["gate", "exp", "ln"]), ("pe", ["if", "ct"])])

        def dve_in0(dve):
            v = nc.vector
            v.memset(ua[:, :, 0:1], 0.0).then_inc(s_zc, 1)
            dve.wait_ge(s_zc, 1)
            dve.wait_ge(s_vec, 16)
            with dve.Fori(0, NA // 2) as i:
                for s in range(2):
                    t = 2 * i + s
                    dve.wait_ge(s_tile, t + 1)
                    v.tensor_tensor(two(ua[:, ds(t, 1), 1:].squeeze(1)), bank(s), two(rb), ALU.mult).then_inc(s_bank, 1)
                    dve.wait_ge(s_bank, t + 3)
                    dve.wait_ge(s_shf, t + 1)
                    v.tensor_tensor(tmp[0][:, 0:TP], ua[:, ds(t, 1), 0:TP].squeeze(1),
                                    ua[:, ds(t, 1), 1:TP + 1].squeeze(1), ALU.subtract)
                    v.tensor_tensor(tmp[0][:, TP:], vec[:, ds(VEC["shift"][0] + NS * t, NS)],
                                    ua[:, ds(t, 1), TP + 1:].squeeze(1), ALU.subtract).then_inc(s_sub, 1)
                    dve.wait_ge(s_sub, t + 1)
                    dve.wait_ge(s_raw, t + 1)
                    v.scalar_tensor_tensor(ua[:, ds(t, 1), 1:].squeeze(1), tmp[0], vec[:, ds(VEC["mu"][0] + t, 1)],
                                           ua[:, ds(t, 1), 1:].squeeze(1), ALU.mult, ALU.add).then_inc(s_shf, 1)
            with dve.Fori(0, 4) as i:
                for s in range(2):
                    t = 2 * i + s
                    u = lambda a, b: ub[:, ds(t, 1), a:b].squeeze(1)
                    dve.wait_ge(s_tile, t + NA + 1)
                    v.tensor_tensor(two(u(0, T)), bank(s), two(rb), ALU.mult).then_inc(s_bank, 1)
                    dve.wait_ge(s_bank, t + NA + 3)
                    dve.wait_ge(s_cvd, t + 1)
                    w = lambda j: vec[:, ds(VEC["cw"][0] + 8 * j + t, 1)]
                    o = acc[s]
                    v.tensor_scalar(o, u(0, T), w(3), vec[:, ds(VEC["cb"][0] + t, 1)], ALU.mult,
                                    ALU.add).then_inc(s_cv, 1)
                    for k in range(1, 4):
                        dve.wait_ge(s_cv, 4 * t + k)
                        v.scalar_tensor_tensor(o[:, TP:], vec[:, ds(VEC["conv"][0] + 24 * t + 8 * (3 - k), 8)],
                                               w(3 - k), o[:, TP:], ALU.mult, ALU.add)
                        v.scalar_tensor_tensor(o[:, k:TP], u(0, TP - k), w(3 - k), o[:, k:TP],
                                               ALU.mult, ALU.add).then_inc(s_cv, 1)
            with dve.Fori(0, 4) as i:
                for s in range(2):
                    t = 2 * i + s
                    dve.wait_ge(s_tile, t + NA + 8 + 1)
                    v.tensor_tensor(two(ub[:, ds(t + 8, 1), :].squeeze(1)), bank(s), two(rb),
                                    ALU.mult).then_inc(s_bank, 1)
            def after(steps, name):
                dve.wait_ge(*steps.at(name))
            ir, fr, er, zr = hbuf[0][0:4, 1024:1024 + T], hbuf[0][0:4, 2048:2048 + T], hbuf[0][0:4, 3072:3072 + T], \
                hbuf[0][0:4, 3600:3600 + TP]
            cr, nr, tr = crow[0:4], nmrow[0:4], nmtrow[0:4]
            after(row_p, "if")
            v.tensor_tensor(two(ir), ps[0:4, 6:8, 0:HALF], two(rb[0:4]), ALU.mult).then_inc(*row_d.step("i"))
            after(row_d, "i")
            v.tensor_scalar(ir, ir, V("ib")[0:4], None, ALU.add).then_inc(*row_d.step("ib"))
            v.tensor_tensor(two(fr), ps[32:36, 6:8, 0:HALF], two(rb[32:36]), ALU.mult).then_inc(*row_d.step("f"))
            after(row_d, "f")
            v.tensor_scalar(fr, fr, V("fb")[0:4], None, ALU.add).then_inc(*row_d.step("fb"))
            after(row_d, "fb")
            v.scalar_tensor_tensor(er, fr, -1.0, fr, ALU.mult, ALU.max).then_inc(*row_d.step("abs"))
            after(row_a, "ln")
            v.scalar_tensor_tensor(fr, fr, 0.0, er, ALU.min, ALU.subtract).then_inc(*row_d.step("lf"))
            v.memset(zr, 0.0).then_inc(*row_d.step("zero"))
            after(row_d, "zero")
            v.tensor_tensor_scan(er[:, 0:TP], fr[:, 0:TP], zr, 0.0, ALU.add, ALU.add).then_inc(*row_d.step("b"))
            after(row_d, "b")
            v.tensor_tensor(cr[:, 0:TP], ir[:, 0:TP], er[:, 0:TP], ALU.subtract).then_inc(*row_d.step("c"))
            after(row_d, "c")
            v.tensor_tensor_scan(tr[:, 0:TP], cr[:, 0:TP], cr[:, 0:TP], 0.0, ALU.max,
                                 ALU.max).then_inc(*row_d.step("m"))
            after(row_d, "m")
            v.tensor_scalar(nr[:, 0:TP], tr[:, 0:TP], -1.0, None, ALU.mult).then_inc(*row_d.step("nm"))
            v.scalar_tensor_tensor(tr[:, 0:TP], er[:, 0:TP], -1.0, tr[:, 0:TP], ALU.mult,
                                   ALU.subtract).then_inc(*row_d.step("nmt"))
            after(row_d, "nmt")
            v.tensor_scalar(mo[0:4, 0:1], tr[:, TP - 1:TP], -1.0, None, ALU.mult).then_inc(*row_d.step("mo"))
            t_, m_ = zr[:, 0:NS], mo[0:4, 1:]
            v.tensor_tensor(t_, fr[:, TP:], V("m", 0, NS)[0:4], ALU.add).then_inc(*row_d.step("t"))
            after(row_d, "t")
            v.tensor_tensor(m_, t_, ir[:, TP:], ALU.max).then_inc(*row_d.step("tm"))
            after(row_d, "tm")
            v.tensor_tensor(sr[0:4, 0:8], t_, m_, ALU.subtract).then_inc(*row_d.step("iw"))
            v.tensor_tensor(sr[0:4, 8:16], ir[:, TP:], m_, ALU.subtract).then_inc(*row_d.step("wi"))
            v.tensor_scalar(sr[0:4, 16:24], m_, -1.0, None, ALU.mult).then_inc(*row_d.step("en"))
            after(row_d, "en")
            after(row_p, "ct")
            v.tensor_copy(ct, ps[:, 4, 0:16]).then_inc(*row_d.step("ct"))
            after(row_d, "ct")

        def pool_in0(pool):
            with pool.Fori(0, NA // 2) as i:
                for s in range(2):
                    t = 2 * i + s
                    pool.wait_ge(s_bank, t + 3)
                    nc.gpsimd.tensor_copy(sho[:, ds(t, 1), :].squeeze(1),
                                          ua[:, ds(t, 1), TP:].squeeze(1)).then_inc(s_raw, 1)
            with pool.Fori(0, 4) as i:
                for s in range(2):
                    t = 2 * i + s
                    pool.wait_ge(s_bank, t + NA + 3)
                    nc.gpsimd.tensor_copy(cvo[:, ds(t, 1), :].squeeze(1),
                                          ub[:, ds(t, 1), TP - 3:].squeeze(1)).then_inc(s_raw, 1)

        def act_in0(act):
            a = nc.scalar
            act.wait_ge(s_shf, NA + 1)
            a.activation(ua[0:64, 12, 1:], ua[0:64, 12, 1:], ACT.Tanh).then_inc(s_tn, 1)
            a.activation(ua[:, 13, 1:], ua[:, 13, 1:], ACT.Sigmoid).then_inc(s_tn, 1)
            with act.Fori(0, 4) as i:
                for s in range(2):
                    t = 2 * i + s
                    act.wait_ge(s_cv, 4 * t + 4)
                    act.wait_ge(s_raw, t + 15)
                    a.activation(ub[:, ds(t, 1), :].squeeze(1), acc[s], ACT.Silu).then_inc(s_cvd, 1)
            er = hbuf[0][0:4, 3072:3072 + T]
            act.wait_ge(s_bank, NA + NB + 2)
            a.activation(ub[:, 12:16, :], ub[:, 12:16, :], ACT.Sigmoid).then_inc(*row_a.step("gate"))
            for k in range(12):
                act.wait_ge(s_lp, k + 1)
                src = ps[:, 4 + 2 * (k % 2):6 + 2 * (k % 2), 0:HALF]
                j = k % 4
                if k < 4:
                    a.activation(two(sig[:, j, :]), src, ACT.Sigmoid, bias=V("w0", j)).then_inc(s_lc, 1)
                elif k < 8:
                    a.activation(two(aa[:, j, :]), src, ACT.Sigmoid, bias=V("a0", j)).then_inc(s_lc, 1)
                else:
                    a.activation(two(gg[:, j, :]), src, ACT.Copy).then_inc(s_lc, 1)
            act.wait_ge(*row_d.at("abs"))
            a.activation(er, er, ACT.Exp, scale=-1.0).then_inc(*row_a.step("exp"))
            act.wait_ge(*row_a.at("exp"))
            a.activation(er, er, ACT.Ln, bias=1.0).then_inc(*row_a.step("ln"))

        def pe_in0(pe):
            for kt in range(KD):
                for hf in range(2):
                    mm = pe.matmul(ps[0:36, 6 + hf, 0:HALF], V("wif", 36 * kt, 36), xg[:, kt, hf * HALF:(hf + 1) * HALF],
                                   start=(kt == 0), stop=(kt == KD - 1))
            mm.then_inc(*row_p.step("if"))
            pe.wait_ge(s_tn, 2)
            for k in range(12):
                j = k % 4
                if k == 0:
                    pe.wait_ge(s_rt, 1)
                if k == 1:
                    pe.wait_ge(*row_d.at("f"))
                if k >= 2:
                    pe.wait_ge(s_lc, k - 1)
                w = (V("w2a2", j * P, P)[0:64] if k < 4 else V("w2a2", j * P, P)[64:P] if k < 8 else V("g2", j * P, P))
                for hf in range(2):
                    cols = slice(1 + hf * HALF, 1 + hf * HALF + HALF)
                    x = ua[0:64, 12, cols] if k < 4 else ua[64:P, 12, cols] if k < 8 else ua[:, 13, cols]
                    mm = pe.matmul(ps[:, 4 + 2 * (k % 2) + hf, 0:HALF], w, x, start=True, stop=True)
                mm.then_inc(s_lp, 1)
            pe.wait_ge(s_lc, 11)
            pe.wait_ge(*row_d.at("c"))
            for g in range(NG):
                mm = pe.transpose(ps[:, 4, 4 * g:4 * g + 4], crow[0:4, g * P:(g + 1) * P], C("ident")[0:4, 0:4])
            mm.then_inc(*row_p.step("ct"))
            pe.wait_ge(s_lc, 12)

        h1 = hb[1]
        r4_ = Space([hbuf[0][:, :], free[:, used0:], pjw[:, :], free[:, 0:3 * T]])
        rS = r4_.take(4, 2, CDV)
        kR, QD = r4_.take(2, P), r4_.take(2, P)
        vR, YC, YQ, YB = [r4_.take(4, P) for _ in range(4)]
        kTk, vTk = r4_.take(2 * P), r4_.take(CDV)
        PR, RI = r4_.take(P), r4_.take(P)
        rp_x, s_rope, s_pair = [tmp[0], tmp[1], sqr[0], sqr[1]], sem("rope_step"), sem("rope_pair")
        re = part("ret", dict(
            pe=["kr", "vr", "sc", "o", "st", "mean", "var"],
            dve=["kt", "pt", "qd", "s", "yc", "ri", "yn", "out"],
            act=["k", "v", "vt", "y", "ysq", "sd"]))
        ep, ed, ea = re["pe"], re["dve"], re["act"]
        s_rz = sem("ret_zeroed")

        def dve_qkv(dve):
            v = nc.vector
            with dve.Fori(0, 8) as i:
                x1, x2, p1, p2 = rp_x
                t = GEMMS["qkv"][1]
                dve.wait_ge(s_tile, (t + 1) + 2 * i)
                dve.wait_ge(s_rope, 8 * i + 1)
                v.tensor_tensor(two(x1), bank(0), two(rb), ALU.mult).then_inc(s_bank, 1)
                dve.wait_ge(s_tile, (t + 2) + 2 * i)
                v.tensor_tensor(two(x2), bank(1), two(rb), ALU.mult).then_inc(s_bank, 1)
                dve.wait_ge(s_bank, (t + 4) + 2 * i)
                y = lambda k: hid[:, ds(2 * i + k, 1), :].squeeze(1)
                v.tensor_tensor(p1, x1, C("cos"), ALU.mult).then_inc(s_rope, 1)
                v.tensor_tensor(p2, x2, C("sin"), ALU.mult).then_inc(s_rope, 1)
                dve.wait_ge(s_rope, 8 * i + 3)
                v.tensor_tensor(y(0), p1, p2, ALU.subtract).then_inc(s_rope, 1)
                dve.wait_ge(s_rope, 8 * i + 4)
                v.tensor_tensor(p1, x1, C("sin"), ALU.mult).then_inc(s_rope, 1)
                v.tensor_tensor(p2, x2, C("cos"), ALU.mult).then_inc(s_rope, 1)
                dve.wait_ge(s_rope, 8 * i + 6)
                v.tensor_tensor(y(1), p1, p2, ALU.add).then_inc(s_rope, 1)
                dve.wait_ge(s_rope, 8 * i + 7)
                v.memset(PR[:, 0:1], 0.0).then_inc(s_rope, 2)
            with dve.Fori(0, 8) as i:
                for s in range(2):
                    dve.wait_ge(s_tile, (GEMMS["qkv"][1] + 17 + s) + 2 * i)
                    v.tensor_tensor(two(hid[:, ds(2 * i + 16 + s, 1), :].squeeze(1)), bank(s), two(rb),
                                    ALU.mult).then_inc(s_bank, 1)
            v.memset(rS, 0.0).then_inc(s_rz, 1)
            dve.wait_ge(s_rz, 1)

        def hg(tile, n, g):
            return hid[:, tile:tile + n, ds(L * g, L)]

        def dve_ret(dve):
            v = nc.vector
            with dve.Fori(0, NG) as g:
                for h in range(CH):
                    def after(steps, name):
                        dve.wait_ge(*steps.at(name, 4 * g + h))
                    after(ep, "kr")
                    v.tensor_scalar(kTk, ps[:, 0, 0:256], C("kdec", h, 1), None, ALU.mult).then_inc(*ed.step("kt"))
                    after(ep, "sc")
                    v.tensor_tensor(PR, ps[:, 2, 0:P], C("rmask", h * P, P), ALU.mult).then_inc(*ed.step("pt"))
                    v.tensor_tensor(QD, hg(2 * h, 2, g), mid(C("qdec", h * P, P), 2), ALU.mult).then_inc(*ed.step("qd"))
                    after(ep, "st")
                    v.scalar_tensor_tensor(rS[:, h], rS[:, h], CDEC_CHUNK[h], ps[:, 4:6, :], ALU.mult,
                                           ALU.add).then_inc(*ed.step("s"))
                    after(ep, "mean")
                    v.tensor_tensor(YC, YB, mid(ps[:, 6, 0:P], 4), ALU.subtract).then_inc(*ed.step("yc"))
                    after(ea, "sd")
                    v.reciprocal(RI, RI).then_inc(*ed.step("ri"))
                    after(ed, "ri")
                    v.tensor_tensor(YC, YC, mid(RI, 4), ALU.mult).then_inc(*ed.step("yn"))
                    after(ed, "yn")
                    v.tensor_tensor(hg(16 + 4 * h, 4, g), YC, bc(V("rgn", 4 * h, 4), P), ALU.mult).then_inc(*ed.step("out"))

        def act_ret(act):
            a = nc.scalar
            with act.Fori(0, NG) as g:
                for h in range(CH):
                    def after(steps, name, back=0):
                        act.wait_ge(*steps.at(name, 4 * g + h - back))
                    if h == 0:
                        act.wait_ge(s_bank, GEMMS["qkv"][1] + 34)
                        act.wait_ge(s_rope, 65)
                    after(ed, "out", 1)
                    a.activation(kR, hg(8 + 2 * h, 2, g), ACT.Copy, scale=CDK ** -0.5).then_inc(*ea.step("k"))
                    a.activation(vR, hg(16 + 4 * h, 4, g), ACT.Copy).then_inc(*ea.step("v"))
                    after(ep, "vr")
                    a.activation(vTk, ps[:, 1, :], ACT.Copy).then_inc(*ea.step("vt"))
                    after(ep, "o")
                    a.activation(YB, bk(3), ACT.Copy).then_inc(*ea.step("y"))
                    after(ed, "yc")
                    a.activation(YQ, YC, ACT.Square).then_inc(*ea.step("ysq"))
                    after(ep, "var")
                    a.activation(RI, ps[:, 7, 0:P], ACT.Sqrt, bias=GN_EPS).then_inc(*ea.step("sd"))

        def pe_ret(pe):
            pe.wait_ge(s_rz, 1)
            with pe.Fori(0, NG) as g:
                for h in range(CH):
                    def after(steps, name):
                        pe.wait_ge(*steps.at(name, 4 * g + h))
                    after(ea, "k")
                    for k in range(2):
                        mm = pe.transpose(ps[:, 0, k * P:(k + 1) * P], kR[:, k, :], C("ident"))
                    mm.then_inc(*ep.step("kr"))
                    after(ea, "v")
                    for e in range(4):
                        mm = pe.transpose(bk(1)[:, e, :], vR[:, e, :], C("ident"))
                    mm.then_inc(*ep.step("vr"))
                    for k in range(2):
                        mm = pe.matmul(ps[:, 2, 0:P], kR[:, k, :], hid[:, 2 * h + k, ds(L * g, L)],
                                       start=(k == 0), stop=(k == 1))
                    mm.then_inc(*ep.step("sc"))
                    after(ea, "vt")
                    after(ed, "qd")
                    for e in range(4):
                        pe.matmul(bk(3)[:, e, :], vTk[:, e * P:(e + 1) * P], PR, start=True, stop=False)
                        for k in range(2):
                            mm = pe.matmul(bk(3)[:, e, :], rS[:, h, k, e * P:(e + 1) * P], QD[:, k, :],
                                           start=False, stop=(k == 1))
                    mm.then_inc(*ep.step("o"))
                    for k in range(2):
                        mm = pe.matmul(ps[:, 4 + k, :], kTk[:, k * P:(k + 1) * P], vTk, start=True, stop=True)
                    mm.then_inc(*ep.step("st"))
                    after(ea, "y")
                    for e in range(4):
                        mm = pe.matmul(ps[:, 6, 0:P], C("mean512"), YB[:, e, :], start=(e == 0), stop=(e == 3))
                    mm.then_inc(*ep.step("mean"))
                    after(ea, "ysq")
                    for e in range(4):
                        mm = pe.matmul(ps[:, 7, 0:P], C("mean512"), YQ[:, e, :], start=(e == 0), stop=(e == 3))
                    mm.then_inc(*ep.step("var"))

        r5 = Space([hbuf[0][:, :], free[:, used0:], pjw[:, :], free[:, 0:3 * T]])
        ring = [r5.take(2, CDV) for _ in range(4)]
        krow, km = r5.take(4, 2 * P), [r5.take(2 * P) for _ in range(2)]
        ys1, yc1, yq1 = [r5.take(16, NS) for _ in range(3)]
        ri1 = r5.take(4, NS)
        vrow = tmp_rows = None
        r5v = Space([r5.free[2][0][:, r5.free[2][2]:], r5.free[3][0][:, r5.free[3][2]:]])
        vrow = [r5v.take(CDV) for _ in range(4)]
        s_rin = [sem(f"ret_state_loaded{i}") for i in range(4)]
        s_rout = sem("ret_state_stored")
        e1 = {k: sem(f"ret1_{k}") for k in ("pe", "dve", "act")}
        ep1 = Steps(e1["pe"], ["krows", "v0", "v1"])
        epj = Steps(e1["pe"], ["outer", "o"], 3)
        ep2 = Steps(e1["pe"], ["mean", "var"], 3 + 64)
        edj = Steps(e1["dve"], ["km", "s"])
        ed2 = Steps(e1["dve"], ["yc", "ri", "yn", "out"], 64)
        ea1 = Steps(e1["act"], ["krows", "v0", "v1", "y", "ysq", "sd"])
        s_prs = sem("prompt_ret_stored")

        def dve_ret1(dve):
            v = nc.vector

            def after(steps, name, it=0):
                dve.wait_ge(*steps.at(name, it))
            after(ea1, "krows")
            for h in range(CH):
                with dve.Fori(0, 2) as i:
                    for s in range(4):
                        it = 8 * h + 4 * i + s
                        b = 4 * i + s
                        dve.wait_ge(epj.sem, (16 * h + 2 * s + 1) + 8 * i)
                        v.tensor_scalar(km[s % 2][0:NS], krow[0:NS, h, :], con[0:NS, ds(CON["ident"][0] + b, 1)], None,
                                        ALU.mult).then_inc(*edj.step("km"))
                        after(epj, "outer", it)
                        dve.wait_ge(s_rin[s], (16 * 2 * h + 16) + 16 * i)
                        v.scalar_tensor_tensor(ring[s], ring[s], CDEC_ONE[h], ps[:, 2 * (s % 2):2 * (s % 2) + 2, :],
                                               ALU.mult, ALU.add).then_inc(*edj.step("s"))
            after(ep2, "mean")
            four = lambda x: x.rearrange("p (h e) s -> p h e s", h=4)
            b4 = lambda x: x.unsqueeze(2).to_broadcast([P, 4, 4, NS])
            mean = ps[:, 5, 0:32].rearrange("p (h s) -> p h s", h=4)
            v.tensor_tensor(four(yc1), four(ys1), b4(mean), ALU.subtract).then_inc(*ed2.step("yc"))
            after(ea1, "sd")
            v.reciprocal(ri1, ri1).then_inc(*ed2.step("ri"))
            after(ed2, "ri")
            v.tensor_tensor(four(yc1), four(yc1), b4(ri1), ALU.mult).then_inc(*ed2.step("yn"))
            after(ed2, "yn")
            v.tensor_tensor(hid[:, 16:32, TP:], yc1, bc(V("rgn", 0, 16), NS), ALU.mult).then_inc(*ed2.step("out"))
            after(ed2, "out")

        def act_ret1(act):
            a = nc.scalar

            def after(steps, name, it=0):
                act.wait_ge(*steps.at(name, it))
            act.wait_ge(*ed.at("out", 15))
            act.wait_ge(s_prs, 16)
            after(ep1, "krows")
            a.activation(krow[0:NS].rearrange("p h n -> p (h n)").rearrange("p (b n) -> p b n", b=2), ps[0:NS, 0:2, :],
                         ACT.Copy, scale=CDK ** -0.5).then_inc(*ea1.step("krows"))
            for k in range(2):
                after(ep1, f"v{k}")
                a.activation(vrow[2 * k][0:NS], ps[0:NS, 2, :], ACT.Copy)
                a.activation(vrow[2 * k + 1][0:NS], ps[0:NS, 3, :], ACT.Copy).then_inc(*ea1.step(f"v{k}"))
            after(epj, "o", 31)
            a.activation(ys1, ps[:, 4, 0:P].rearrange("p (k s) -> p k s", s=NS), ACT.Copy).then_inc(*ea1.step("y"))
            after(ed2, "yc")
            a.activation(yq1, yc1, ACT.Square).then_inc(*ea1.step("ysq"))
            after(ep2, "var")
            a.activation(ri1, ps[:, 6, 0:32].rearrange("p (h s) -> p h s", h=4), ACT.Sqrt,
                         bias=GN_EPS).then_inc(*ea1.step("sd"))

        def pe_ret1(pe):
            def after(steps, name, it=0):
                pe.wait_ge(*steps.at(name, it))
            after(ed, "out", 15)
            for k in range(8):
                mm = pe.transpose(ps[0:NS, k // 4, (k % 4) * P:(k % 4 + 1) * P], hid[:, 8 + k, TP:], C("ident"))
            mm.then_inc(*ep1.step("krows"))
            for k in range(2):
                if k:
                    after(ea1, "v0")
                for e in range(8):
                    mm = pe.transpose(ps[0:NS, 2 + e // 4, (e % 4) * P:(e % 4 + 1) * P], hid[:, 16 + 8 * k + e, TP:],
                                      C("ident"))
                mm.then_inc(*ep1.step(f"v{k}"))
            after(ea1, "v1")

            def o_product(h, i, s):
                after(edj, "s", 8 * h + 4 * i + s)
                for e in range(4):
                    for k in range(2):
                        mm = pe.matmul(ps[:, 4, ds(4 * NS * h + NS * e + 4 * i + s, 1)],
                                       ring[s][:, k, e * P:(e + 1) * P],
                                       hid[:, 2 * h + k, ds(TP + 4 * i + s, 1)],
                                       start=(k == 0), stop=(k == 1), skip_group_check=True)
                mm.then_inc(*epj.step("o"))
            for h in range(CH):
                with pe.Fori(0, 2) as i:
                    for s in range(4):
                        it = 8 * h + 4 * i + s
                        after(edj, "km", it)
                        for k in range(2):
                            mm = pe.matmul(ps[:, 2 * (s % 2) + k, :], km[s % 2][0:NS, k * P:(k + 1) * P],
                                           vrow[h][0:NS], start=True, stop=True)
                        mm.then_inc(*epj.step("outer"))
                        o_product(h, i, s)
            after(ea1, "y")
            for h in range(4):
                for e in range(4):
                    mm = pe.matmul(ps[:, 5, NS * h:NS * h + NS], C("mean512"), ys1[:, 4 * h + e, :],
                                   start=(e == 0), stop=(e == 3))
            mm.then_inc(*ep2.step("mean"))
            after(ea1, "ysq")
            for h in range(4):
                for e in range(4):
                    mm = pe.matmul(ps[:, 6, NS * h:NS * h + NS], C("mean512"), yq1[:, 4 * h + e, :],
                                   start=(e == 0), stop=(e == 3))
            mm.then_inc(*ep2.step("var"))

        def dve_up(dve, lyr):
            _, t0, _, _, _ = GEMMS[f"up{lyr}"]
            with dve.Fori(0, KF // 2) as i:
                for s in range(2):
                    dve.wait_ge(s_tile, (t0 + s + 1) + 2 * i)
                    dve.wait_ge(s_hid, (KF * lyr + s + 1) + 2 * i)
                    nc.vector.scalar_tensor_tensor(two(tmp[s]), bank(s), 0.0, two(rb), ALU.max,
                                                   ALU.mult).then_inc(s_bank, 1)

        def act_up(act, lyr):
            _, t0, _, _, _ = GEMMS[f"up{lyr}"]
            with act.Fori(0, KF // 2) as i:
                for s in range(2):
                    act.wait_ge(s_bank, (t0 + s + 3) + 2 * i)
                    nc.scalar.activation(hid[:, ds(2 * i + s, 1), :].squeeze(1), tmp[s],
                                         ACT.Square).then_inc(s_hid, 1)

        def pe_proj(pe, lyr):
            pe.wait_ge(s_pj_w, 16 * (lyr + 1))
            pe.wait_ge(s_pt, 16 * (lyr + 1))
            pe.wait_ge(s_rt, 4 * lyr + 4)
            for mt in range(KD):
                if mt >= 2:
                    pe.wait_ge(s_pjc, 8 * lyr + mt - 1)
                for kt in range(KP):
                    for hf in range(2):
                        at = (mt * KP + kt) * P
                        mm = pe.matmul(ps[:, 4 + 2 * (mt % 2) + hf, 0:HALF], pjw[:, at:at + P],
                                       pt[:, kt, hf * HALF:(hf + 1) * HALF], start=(kt == 0), stop=(kt == KP - 1))
                mm.then_inc(s_pj, 1)

        def act_ple(act, lyr, hn, more):
            a = nc.scalar
            for mt in range(KD):
                act.wait_ge(s_pj, 8 * lyr + mt + 1)
                p4 = 4 + 2 * (mt % 2)
                a.activation(two(hid[:, mt, :]), ps[:, p4:p4 + 2, 0:HALF], ACT.Copy).then_inc(s_pjc, 1)
            for mt in range(KD + 1):
                if mt < KD:
                    act.wait_ge(s_tile, tile_at(f"gate{lyr}", mt))
                    if mt >= 2:
                        act.wait_ge(s_hn, 8 * lyr + mt - 1)
                    a.activation(two(sqr[mt % 2]), bank(mt % 2), ACT.Exp, scale=-1.0).then_inc(s_bank, 1)
                if mt and more:
                    kt = mt - 1
                    act.wait_ge(s_hn, 8 * lyr + mt)
                    a.activation(xg[:, kt, :], hn[:, kt, :], ACT.Copy, scale=V("norm_g", 32 + kt))
                    a.activation(hid[:, 24 + kt, :], hn[:, kt, :], ACT.Square).then_inc(s_xg, 1)

        def dve_ple(dve, lyr, h, hn):
            v = nc.vector
            _, t0, _, _, _ = GEMMS[f"gate{lyr}"]
            for mt in range(KD):
                e = sqr[mt % 2]
                n = 24 * lyr + 3 * mt
                dve.wait_ge(s_bank, t0 + mt + 3)
                v.tensor_scalar(e, e, 1.0, None, ALU.add).then_inc(s_pl, 1)
                dve.wait_ge(s_pl, n + 1)
                v.reciprocal(e, e).then_inc(s_pl, 1)
                dve.wait_ge(s_pl, n + 2)
                dve.wait_ge(s_pjc, 8 * lyr + mt + 1)
                v.tensor_tensor(e, e, hid[:, mt, :], ALU.mult).then_inc(s_pl, 1)
                dve.wait_ge(s_pl, n + 3)
                v.tensor_tensor(hn[:, mt, :], h[:, mt, :], e, ALU.add).then_inc(s_hn, 1)

        def dve_gate_g(dve):
            v = nc.vector
            t0 = GEMMS["g"][1]
            with dve.Fori(0, 8) as i:
                for s in range(2):
                    dve.wait_ge(s_tile, (t0 + s + 1) + 2 * i)
                    v.tensor_tensor(two(tmp[s]), bank(s), two(rb), ALU.mult).then_inc(s_bank, 1)
                    dve.wait_ge(s_silu, (s + 1) + 2 * i)
                    y = hid[:, ds(2 * i + 16 + s, 1), :].squeeze(1)
                    v.tensor_tensor(y, y, tmp[s], ALU.mult).then_inc(s_yg, 1)

        def act_gate_g(act):
            t0 = GEMMS["g"][1]
            with act.Fori(0, 8) as i:
                for s in range(2):
                    act.wait_ge(s_bank, (t0 + s + 3) + 2 * i)
                    nc.scalar.activation(tmp[s], tmp[s], ACT.Silu).then_inc(s_silu, 1)
        s_silu, s_yg = sem("gate_silu"), sem("gated")
        s_x2, s_st1 = sem("x_reloaded"), sem("rwkv_sample_state_stored")
        s_ro = [sem(f"ret_state_stored{i}") for i in range(4)]

        block = ctx.enter_context(nc.Block())
        cols = lambda hf, off=0: slice(off + hf * HALF, off + (hf + 1) * HALF)

        @block.sync
        def _(sp):
            sp.dma_start(vec[:, :], dram["vec"]).then_inc(s_vec, 16)
            sp.dma_start(hbuf[0][:, :], dram["x"]).then_inc(s_x, 16)
            sp.dma_start(con[:, :], dram["con"]).then_inc(s_con, 16)

            def slabs(name, first=0, last=None, prev=None):
                slab0, tile0, n, ntiles, per = GEMMS[name]
                last = n // 2 if last is None else last
                if first == 0:
                    for s in range(2):
                        if prev:
                            _, pt0, pn, ptiles, pper = GEMMS[prev]
                            sp.wait_ge(s_tile, pt0 + min(ptiles, (pn - 1 + s) * pper))
                        sp.dma_start(slot[s][:, :], dram["w"][slab0 + s]).then_inc(s_w[s], 16)
                if last > max(first, 1):
                    with sp.Fori(max(first, 1), last) as i:
                        for s in range(2):
                            sp.wait_ge(s_tile, (tile0 + (s + 1) * per - 2 * per) + 2 * per * i)
                            sp.dma_start(slot[s][:, :], dram["w"][slab0 + 2 * i + s]).then_inc(s_w[s], 16)

            slabs("in0")
            slabs("out0", prev="in0")
            sp.wait_ge(s_raw, NA + 8)
            store(sp, dram["sho"], sho.rearrange("p a b -> p (a b)"))
            store(sp, dram["cvo"], cvo.rearrange("p a b -> p (a b)"))
            store(sp, dram["conv_o"], V("conv", 0, 192))
            sp.wait_ge(*row_d.at("tm"))
            store(sp, dram["mo"], mo[0:4])
            with sp.Fori(0, 2) as h:
                sp.wait_ge(*rd.at("out", 4 * h + 3))
                sp.dma_start(dram["rs_o"][h], s_buf[0].rearrange("p a b -> p (a b)")).then_inc(s_rs, 16)
            sp.dma_start(sst.rearrange("p j s n -> p (j s n)"), dram["sst"]).then_inc(s_sst, 16)
            sp.wait_ge(*sdj.at("s", 3))
            sp.dma_start(dram["sst_o"], sst.rearrange("p j s n -> p (j s n)")).then_inc(s_st1, 16)
            sp.wait_ge(*sd2.at("out"))
            sp.dma_start(cst.rearrange("p h s n -> p (h s n)"), dram["cst"]).then_inc(s_cst, 16)
            sp.wait_ge(*md.at("out", NG - 1))
            store(sp, dram["cn_o"], cn.rearrange("p h n -> p (h n)"))
            sp.wait_ge(*nd.at("n"))
            store(sp, dram["n_o"], n_new.rearrange("p h n -> p (h n)"))
            sp.wait_ge(*ndj.at("c", 3))
            store(sp, dram["cst_o"], cst.rearrange("p h s n -> p (h s n)"))
            sp.wait_ge(*nd2.at("out"))
            assert outs[0] == MIXER_STORES
            sp.wait_ge(s_out, MIXER_STORES)
            sp.wait_ge(s_rs, 33)
            sp.dma_start(hbuf[0][:, :], dram["x"]).then_inc(s_x2, 16)
            sp.dma_start(pjw[:, :], dram["pjw"][0]).then_inc(s_pj_w, 16)
            sp.dma_start(pt.rearrange("p k t -> p (k t)"), dram["pt"][0]).then_inc(s_pt, 16)
            slabs("up0", prev="out0")
            slabs("down0", prev="up0")
            slabs("gate0", prev="down0")
            slabs("qkv", prev="gate0")
            slabs("g", 0, 1, prev="qkv")
            sp.wait_ge(*ed.at("out", 4 * NG - 1))
            sp.dma_start(dram["rS_o"], rS.rearrange("p h k n -> p (h k n)")).then_inc(s_prs, 16)
            sp.wait_ge(s_prs, 16)

            def ret_load(it, s):
                sp.dma_start(ring[s].rearrange("p k n -> p (k n)"), dram["rst"][it]).then_inc(s_rin[s], 16)

            def ret_store(it, s):
                sp.wait_ge(*edj.at("s", it))
                sp.dma_start(dram["rst_o"][it], ring[s].rearrange("p k n -> p (k n)")).then_inc(s_ro[s], 16)
            for s in range(4):
                ret_load(s, s)
            ret_store(0, 0)
            ret_store(1, 1)
            with sp.Fori(0, 7) as i:
                for s in range(4):
                    ret_store(4 * i + (2 + s), (2 + s) % 4)
                    sp.wait_ge(*epj.at("o", 4 * i + s))
                    sp.wait_ge(s_ro[s], 16 * i + 16)
                    ret_load(4 * i + (4 + s), s)
            ret_store(30, 2)
            ret_store(31, 3)
            slabs("g", 1)
            slabs("out1", prev="g")
            sp.wait_ge(*ea1.at("sd"))
            sp.wait_ge(*ed2.at("out"))
            sp.dma_start(pjw[:, :], dram["pjw"][1]).then_inc(s_pj_w, 16)
            sp.wait_ge(s_pj, 8)
            sp.dma_start(pt.rearrange("p k t -> p (k t)"), dram["pt"][1]).then_inc(s_pt, 16)
            slabs("up1", prev="out1")
            slabs("down1", prev="up1")
            slabs("gate1", prev="down1")
            for mt in range(KD):
                sp.wait_ge(s_hn, 8 + mt + 1)
                store(sp, dram["y"][:, mt * T:(mt + 1) * T], hb[0][:, mt, :])
            sp.wait_ge(s_out, outs[0])
            sp.wait_ge(s_rs, 33)
            sp.wait_ge(s_st1, 16)
            sp.wait_ge(s_prs, 16)
            for s in range(4):
                sp.wait_ge(s_ro[s], 128)

        @block.tensor
        def _(pe):
            stream = lambda t: (lambda kt, hf: t[:, kt, cols(hf)])
            pe.wait_ge(s_con, 16)
            pe.wait_ge(s_vec, 16)
            pe_prenorm(pe, 0)
            gemm(pe, "in0", KD, stream(xg))
            pe_in0(pe)
            pe_rwkv(pe)
            pe_rwkv1(pe)
            pe_mlstm(pe)
            pe_mlstm1(pe)
            pe.wait_ge(*nd2.at("out"))
            gemm(pe, "out0", KD, lambda kt, hf: ua[:, kt, cols(hf, 1)] if kt < 4 else ub[:, kt - 4, cols(hf)])
            pe_postnorm(pe, 0)
            pe_prenorm(pe, 1)
            gemm(pe, "up0", KD, stream(xg))
            gemm(pe, "down0", KF, stream(hid), lambda kt: (s_hid, kt + 3))
            pe_postnorm(pe, 1)
            pe_proj(pe, 0)
            gemm(pe, "gate0", KD, stream(hb[0]), lambda kt: (s_h, 8 + kt + 1))
            pe_prenorm(pe, 2)
            gemm(pe, "qkv", KD, stream(xg))
            pe_ret(pe)
            pe_ret1(pe)
            gemm(pe, "g", KD, stream(xg))
            gemm(pe, "out1", 16, lambda kt, hf: hid[:, 16 + kt, cols(hf)], lambda kt: (s_yg, kt + 1))
            pe_postnorm(pe, 2)
            pe_prenorm(pe, 3)
            gemm(pe, "up1", KD, stream(xg))
            gemm(pe, "down1", KF, stream(hid), lambda kt: (s_hid, KF + kt + 3))
            pe_postnorm(pe, 3)
            pe_proj(pe, 1)
            gemm(pe, "gate1", KD, stream(hb[1]), lambda kt: (s_h, 24 + kt + 1))

        @block.scalar
        def _(act):
            act.wait_ge(s_vec, 16)
            act_prenorm(act, 0, hb[0], 0, lambda kt: (s_x, 16))
            act_rms(act, 0)
            act_in0(act)
            act_rwkv(act)
            act_rwkv1(act)
            act.wait_ge(s_st1, 16)
            act_mlstm(act)
            act_mlstm1(act)
            act.wait_ge(s_out, MIXER_STORES)
            act_outproj(act, "out0", 0, hb[1])
            act_rms(act, 1)
            act_prenorm(act, 1, hb[0], 2, lambda kt: (s_h, kt + 1))
            act_rms(act, 2)
            act_up(act, 0)
            act_outproj(act, "down0", 1, hb[1])
            act_rms(act, 3)
            act_ple(act, 0, hb[1], True)
            act_rms(act, 4)
            act_ret(act)
            act_ret1(act)
            act_gate_g(act)
            act_outproj(act, "out1", 2, hb[0])
            act_rms(act, 5)
            act_prenorm(act, 3, hb[1], 6, lambda kt: (s_h, 16 + kt + 1))
            act_rms(act, 6)
            act_up(act, 1)
            act_outproj(act, "down1", 3, hb[0])
            act_rms(act, 7)
            act_ple(act, 1, hb[0], False)

        @block.vector
        def _(dve):
            nc.vector.memset(tmp[0][:, 0:1], 0.0).then_inc(s_bank, 2)
            nc.vector.memset(tmp[1][:, 0:1], 0.0).then_inc(s_hid, 2)
            for n, s in enumerate([rd.sem, md.sem, ed.sem, s_rs, s_shf, s_cvd, s_rope]):
                nc.vector.memset(tmp[0][:, n + 1:n + 2], 0.0).then_inc(s, 1)
            dve_rinv(dve, 0)
            dve_in0(dve)
            dve_rwkv(dve)
            dve_rwkv1(dve)
            dve_mlstm(dve)
            dve_mlstm1(dve)
            dve_rinv(dve, 1)
            dve.wait_ge(s_x2, 16)
            dve_residual(dve, 0, hb[1], hb[0], 1)
            dve_rinv(dve, 2)
            dve_up(dve, 0)
            dve_rinv(dve, 3)
            dve_residual(dve, 1, hb[1], hb[0], 3)
            dve_ple(dve, 0, hb[0], hb[1])
            dve_rinv(dve, 4)
            dve_qkv(dve)
            dve_ret(dve)
            dve_ret1(dve)
            dve_gate_g(dve)
            dve_rinv(dve, 5)
            dve_residual(dve, 2, hb[0], hb[1], 5)
            dve_rinv(dve, 6)
            dve_up(dve, 1)
            dve_rinv(dve, 7)
            dve_residual(dve, 3, hb[0], hb[1], 7)
            dve_ple(dve, 1, hb[1], hb[0])

        @block.gpsimd
        def _(pool):
            pool_in0(pool)
            pool_rwkv(pool)
            for n in range(4):
                pool_sum(pool, n)


INS = {"vec": (P, NVEC), "con": (P, NCON), "x": (P, KD * T), "w": (NSLAB, P, SLAB), "pjw": (2, P, KP * KD * P),
       "pt": (2, P, KP * T), "sst": (P, 4 * NS * 64), "cst": (P, 4 * NS * P), "rst": (32, P, 2 * CDV)}
OUTS = {"y": (P, KD * T), "sho": (P, NA * (NS + 1)), "cvo": (P, 88), "conv_o": (P, 192), "mo": (4, NS + 1),
        "rs_o": (2, P, 2 * P), "sst_o": (P, 4 * NS * 64), "cn_o": (P, BH * 2 * P), "n_o": (P, BH * NS),
        "cst_o": (P, 4 * NS * P), "rS_o": (P, 4 * 2 * CDV), "rst_o": (32, P, 2 * CDV)}


def lay_out(i):
    def fm(v):
        v = np.asarray(v)
        return v.reshape(-1, P).T

    def slabs(w):
        k, n = w.shape
        b = w.reshape(k // P, P, n // P, P).transpose(2, 0, 1, 3).reshape(-1, P, P)
        pad = -len(b) % 32
        b = np.concatenate([b, np.zeros((pad, P, P), b.dtype)]) if pad else b
        return b.reshape(-1, 32, P, P).transpose(0, 2, 1, 3).reshape(-1, P, SLAB)

    f = np.float32
    vec = np.zeros((P, NVEC), f)

    def put(name, a, rows=P):
        at, n = VEC[name]
        vec[:rows, at:at + n] = np.asarray(a).reshape(rows, n)

    put("norm_g", np.concatenate([fm(i["norm_g"][l, k]) for l in range(2) for k in range(4)], 1))
    put("mu", fm(i["rw_mu"][0]))
    for name, key in [("w0", "rw_w0"), ("a0", "rw_a0"), ("kk", "rw_kk"), ("ka", "rw_ka"), ("rk", "rw_rk"),
                      ("rln", "rw_ln"), ("mgn", "ml_gn"), ("cb", "ml_conv_b"), ("rgn", "ret_gn")]:
        put(name, fm(i[key][0]))
    put("cw", np.concatenate([fm(i["ml_conv_w"][0, j]) for j in range(4)], 1))
    put("ib", i["ml_i_bias"][0], 4)
    put("fb", i["ml_f_bias"][0], 4)
    put("m", i["state_mlstm_m"][0].T, 4)
    put("shift", i["state_rwkv_shift"][0].reshape(NS, NA, P).transpose(2, 1, 0))
    put("conv", i["state_mlstm_conv"][0].reshape(NS, 3, 8, P).transpose(3, 2, 1, 0))
    put("n", i["state_mlstm_n"][0].transpose(2, 1, 0))
    w_in = i["mix0_w_in"][0]
    na, nb = NA * P, (NA + NB) * P
    wif = np.zeros((KD, P, 36), f)
    wif[:, :, 0:4] = w_in[:, nb:nb + 4].reshape(KD, P, 4)
    wif[:, :, 32:36] = w_in[:, nb + 4:nb + 8].reshape(KD, P, 4)
    put("wif", wif.transpose(1, 0, 2))
    put("w2a2", np.concatenate([i["rw_w2"][0], i["rw_a2"][0]], 0))
    put("g2", i["rw_g2"][0])
    big = [w_in[:, :nb], i["mix0_w_out"][0], i["ffn_up"][0], i["ffn_down"][0], i["ple_gate"][0],
           i["ret_w_in"][0], i["ret_w_out"][0], i["ffn_up"][1], i["ffn_down"][1], i["ple_gate"][1]]

    def tokens(a, b):
        t = np.concatenate([a[0], b[:, 0]], 0).T
        return t.reshape(-1, P, T).transpose(1, 0, 2).reshape(P, -1)

    return {
        "vec": vec, "con": shape_constants(), "x": tokens(i["x_prompt"], i["x_sample"]),
        "w": np.concatenate([slabs(w) for w in big]),
        "pjw": np.stack([slabs(i["ple_proj"][l])[0][:, :KP * KD * P] for l in range(2)]),
        "pt": np.stack([tokens(i["p_prompt"][l], i["p_sample"][l]) for l in range(2)]),
        "sst": i["state_rwkv_S"][0].reshape(NS, 4, 2, 64, 64).transpose(2, 4, 1, 0, 3).reshape(P, -1),
        "cst": i["state_mlstm_C"][0].transpose(2, 1, 0, 3).reshape(P, -1),
        "rst": i["state_ret_S"][0].reshape(NS, 4, 2, P, CDV).transpose(1, 0, 3, 2, 4).reshape(32, P, -1),
    }


def unpack(o):
    y = o["y"].reshape(P, KD, T).transpose(2, 1, 0).reshape(T, D)
    sho = o["sho"].reshape(P, NA, NS + 1).transpose(2, 1, 0).reshape(NS + 1, NA * P)
    cvo = o["cvo"].reshape(P, 8, 11).transpose(2, 1, 0).reshape(11, 8 * P)
    conv = o["conv_o"].reshape(P, 8, 3, NS).transpose(3, 2, 1, 0).reshape(NS, 3, 8 * P)
    rs = o["rs_o"].reshape(2, 2, 64, 2, 2, 64)
    rs = np.stack([rs[:, q, :, :, q, :] for q in range(2)], 3).transpose(0, 2, 3, 4, 1)
    sst = o["sst_o"].reshape(2, 64, 4, NS, 64).transpose(3, 2, 0, 4, 1).reshape(NS, 8, 64, 64)
    cn = o["cn_o"].reshape(P, 4, 2 * P).transpose(1, 0, 2)
    rS = o["rS_o"].reshape(P, 4, 2, CDV).transpose(1, 2, 0, 3).reshape(4, CDK, CDV)
    rst = o["rst_o"].reshape(4, NS, P, 2, CDV).transpose(1, 0, 3, 2, 4).reshape(NS, 4, CDK, CDV)
    c = np.ascontiguousarray
    return (c(y[None, :TP]), c(y[TP:, None]),
            c(sho[None, 0:1]), c(rs.reshape(1, 1, 8, 64, 64)), c(cvo[None, None, 0:3]), c(cn[None, None, :, :, 0:P]),
            c(cn[None, None, :, :, P]), c(o["mo"][:, 0][None, None]), c(rS[None, None]),
            c(sho[None, 1:]), c(sst[None]), c(np.concatenate([conv[:, 1:], cvo[3:, None]], 1)[None]),
            c(o["cst_o"].reshape(P, 4, NS, P).transpose(2, 1, 0, 3)[None]),
            c(o["n_o"].reshape(P, 4, NS).transpose(2, 1, 0)[None]), c(o["mo"][:, 1:].T[None]), c(rst[None]))


def kernel(**inputs):
    import concourse.bacc as bacc
    from concourse.bass_utils import run_bass_kernel_spmd

    nc = bacc.Bacc("TRN2", target_bir_lowering=False, num_devices=1)
    arrays = {k: np.ascontiguousarray(a) for k, a in lay_out({k: np.asarray(a) for k, a in inputs.items()}).items()}
    dram = {k: nc.dram_tensor(f"in_{k}", s, F32, kind="ExternalInput").ap() for k, s in INS.items()}
    dram.update({k: nc.dram_tensor(f"out_{k}", s, F32, kind="ExternalOutput").ap() for k, s in OUTS.items()})
    program(nc, **dram)
    r = run_bass_kernel_spmd(nc, [{f"in_{k}": a for k, a in arrays.items()}], core_ids=[0])
    return unpack({k: np.asarray(r.results[0][f"out_{k}"]) for k in OUTS})
```

```python
from contextlib import ExitStack

import numpy as np

import concourse.bass as bass
from concourse import mybir

F32 = mybir.dt.float32
ALU = mybir.AluOpType
ACT = mybir.ActivationFunctionType

P = 128
D = 1024
KD = D // P
TP = 512
NS = 8
T = TP + NS
HALF = T // 2
FF = 4 * D
KF = FF // P
PLE = 256
KP = PLE // P
L = 128
NG = TP // L
SUB = 64
AH, AHD = 8, 64
BH, BHD = 4, 128
CH, CDK, CDV = 4, 256, 512
NA = 14
NB = 16
RMS_EPS = 1e-6
GN_EPS = 1e-5
A_LN_EPS = 64e-5
C0 = float(np.exp(-0.5))
SLAB = 32 * P
NEG = -1e30


def columns(parts):
    at, out = 0, {}
    for name, n in parts:
        out[name] = (at, n)
        at += n
    return out, at


VEC, NVEC = columns([
    ("norm_g", 64), ("mu", NA), ("w0", 4), ("a0", 4), ("kk", 4), ("ka", 4), ("rk", 4), ("rln", 4),
    ("cw", 32), ("cb", 8), ("mgn", 4), ("rgn", 16), ("ib", 1), ("fb", 1), ("m", NS),
    ("shift", NA * NS), ("conv", 8 * 3 * NS), ("n", BH * NS), ("wif", KD * 36), ("w2a2", 512), ("g2", 512)])
CON, NCON = columns([
    ("ident", P), ("ones", P), ("mean_d", P), ("ones64", P), ("mean64", P), ("mean128", P), ("mean512", P),
    ("gram", 2 * P), ("bd16", P), ("n1t", P), ("n2", P), ("reset", P), ("neg", P), ("sel", 4 * P),
    ("cos", T), ("sin", T), ("rmask", CH * P), ("qdec", CH * P), ("kdec", CH), ("cdec", CH)])


def shape_constants():
    f = np.float32
    c = np.zeros((P, NCON), f)

    def put(name, a):
        at, n = CON[name]
        c[:a.shape[0], at:at + n] = a.reshape(a.shape[0], n)

    i = np.arange(P)
    row, col = i[:, None], i[None, :]
    put("ident", np.eye(P, dtype=f))
    put("ones", np.ones((P, P), f))
    put("mean_d", np.full((P, P), 1.0 / D, f))
    same64 = row // 64 == col // 64
    put("ones64", same64.astype(f))
    put("mean64", same64.astype(f) / f(64))
    put("mean128", np.full((P, P), 1.0 / 128, f))
    put("mean512", np.full((P, P), 1.0 / 512, f))
    put("gram", np.concatenate([same64 & (row < col), same64 & (row <= col)], 1).astype(f))
    put("bd16", (row // 16 == col // 16).astype(f))
    put("n1t", ((col // 16 % 2 == 1) & (row // 16 == col // 16 - 1)).astype(f))
    put("n2", ((row // 32 % 2 == 1) & (col // 32 == row // 32 - 1)).astype(f))
    put("reset", np.broadcast_to((col % SUB != 0).astype(f), (P, P)))
    put("neg", np.where(row <= col, 0.0, NEG).astype(f))
    sel = np.zeros((4, 4, P), f)
    for h in range(4):
        sel[h, h] = 1.0
    put("sel", sel.reshape(4, -1))
    half = CDK // 2
    pos = np.concatenate([np.arange(TP), np.full(NS, 4096)]).astype(f)
    inv = (f(10000.0) ** (-np.arange(half, dtype=f) / f(half))).astype(f)
    ang = (pos[None, :] * inv[:, None]).astype(f)
    put("cos", np.cos(ang))
    put("sin", np.sin(ang))
    lg = np.log1p(-np.exp2(-5.0 - np.arange(CH)))
    put("rmask", np.stack([np.where(row <= col, np.exp(np.maximum(col - row, 0) * g), 0.0) for g in lg], 1))
    put("qdec", np.broadcast_to(np.stack([np.exp((i + 1) * g) for g in lg])[None], (P, CH, P)))
    put("kdec", np.stack([np.exp((L - 1 - i) * g) for g in lg], 1))
    put("cdec", np.broadcast_to(np.exp(lg)[None], (P, CH)))
    return c


CDEC_CHUNK = [float(np.exp(L * np.log1p(-np.exp2(-5.0 - h)))) for h in range(CH)]
CDEC_ONE = [float(np.exp(np.log1p(-np.exp2(-5.0 - h)))) for h in range(CH)]


def in_turn(*parts):
    for _ in zip(*parts):
        pass


class Steps:

    def __init__(self, sem, names, base=0):
        self.sem, self.names, self.base, self.at_now = sem, names, base, 0

    def at(self, name, it=0):
        return self.sem, it * len(self.names) + (self.base + self.names.index(name) + 1)

    def step(self, name):
        want = self.names[self.at_now % len(self.names)]
        assert name == want, (name, want)
        self.at_now += 1
        return self.sem, 1


class Space:

    def __init__(self, stretches):
        self.free = [[ap, ap.shape[1], 0] for ap in stretches]

    def take(self, *dims):
        n = int(np.prod(dims))
        for s in self.free:
            if s[2] + n <= s[1]:
                ap = s[0][:, s[2]:s[2] + n]
                s[2] += n
                if len(dims) == 1:
                    return ap
                names = "abcd"[:len(dims)]
                return ap.rearrange(f"p ({' '.join(names)}) -> p {' '.join(names)}",
                                    **{k: d for k, d in zip(names[1:], dims[1:])})
        raise AssertionError(f"no room for {dims}: {[(s[1], s[2]) for s in self.free]}")


GEMMS, _s, _t = {}, 0, 0
for _name, _slabs, _tiles, _per in [
        ("in0", 8, NA + NB, 4), ("out0", 2, 8, 4), ("up0", 8, KF, 4), ("down0", 8, 8, 1), ("gate0", 2, 8, 4),
        ("qkv", 8, 32, 4), ("g", 4, 16, 4), ("out1", 4, 8, 2), ("up1", 8, KF, 4), ("down1", 8, 8, 1),
        ("gate1", 2, 8, 4)]:
    GEMMS[_name] = (_s, _t, _slabs, _tiles, _per)
    _s, _t = _s + _slabs, _t + _tiles
NSLAB = _s

RW_DVE = ["kkr", "cum0", "cum1", "prev", "floor", "rinv", "kk", "ka0", "ka1", "kp", "at", "rt", "kka", "bt", "kt",
          "bh", "kh", "bon", "ad0", "ad1", "me0", "me1", "d0", "n2", "t1", "d2t", "t2", "d4t", "t4", "t8", "z",
          "t16", "zz", "tt", "qp", "gh0", "gh1", "s0a", "s0b", "mid", "s1a", "s1b", "end", "yc", "vinv", "yn",
          "yg0", "yg1", "out"]
RW_ACT = ["v", "sq", "p", "q", "pm", "norm", "ar", "br", "vr", "mv", "d2", "d4", "d8t", "t8t", "t16t", "w",
          "y", "ysq", "ysd"]
RW_POOL = ["rk", "rkw", "d0t", "n1t"]
RW_PE = ["norm", "bonus", "rows", "gram_b", "gram_k", "a", "mv", "d2", "d2t", "t2", "d4", "d4t", "t4", "d8t",
         "t8", "t8t", "z", "t16", "t16t", "zz", "tt", "w", "qp", "gh", "s0", "s1", "y", "mean", "var"]


def program(nc, stop=None, **dram):
    with ExitStack() as ctx:
        def sb(name, n):
            return ctx.enter_context(nc.sbuf_tensor(name, [P, n], F32))

        def sem(name):
            return ctx.enter_context(nc.semaphore(name))

        con, vec = sb("con", NCON), sb("vec", NVEC)
        hbuf = [sb("h_a", KD * T), sb("h_b", KD * T)]
        xg_t = sb("xg", KD * T)
        big = sb("big", KF * T)
        slot = [sb("slot0", SLAB), sb("slot1", SLAB)]
        pjw = sb("pjw", KP * KD * P)
        rb_t = sb("rb", T)
        free = sb("free", 6400)
        ps = ctx.enter_context(nc.psum_tensor("ps", [P, 8, 512], F32))

        def tiles(t, n=KD, w=T):
            return t[:, 0:n * w].rearrange("p (k t) -> p k t", t=w)

        hb = [tiles(t) for t in hbuf]
        xg, hid = tiles(xg_t), tiles(big, KF)
        ua = big[:, 0:NA * (T + 1)].rearrange("p (k t) -> p k t", t=T + 1)
        ub = big[:, NA * (T + 1):NA * (T + 1) + NB * T].rearrange("p (k t) -> p k t", t=T)
        rb = rb_t[:, :]
        tail = Space([free[:, :]])
        sqr = [tail.take(T), tail.take(T)]
        ss = tail.take(T)
        rt = tail.take(T)
        tmp = [tail.take(T), tail.take(T)]
        pt = tail.take(KP, T)

        def C(name, i=0, n=None):
            a, w = CON[name]
            n = w if n is None else n
            return con[:, a + i:a + i + n]

        def V(name, i=0, n=1):
            a, _ = VEC[name]
            return vec[:, a + i:a + i + n]

        def two(ap):
            return ap.rearrange("p (a n) -> p a n", a=2)

        def bank(par):
            return ps[:, 2 * par:2 * par + 2, 0:HALF]

        s_vec, s_con, s_x = sem("vec_loaded"), sem("con_loaded"), sem("x_loaded")
        s_w = [sem("slab_loaded0"), sem("slab_loaded1")]
        s_tile = sem("tile_done")
        s_bank = sem("bank_free")
        s_xg = sem("xg_ready")
        s_st = sem("stats_done")
        s_rt = sem("rms_ready")
        s_rb = sem("rinv_ready")
        s_sq = sem("square_ready")
        s_ss = sem("square_summed")
        s_h = sem("h_ready")
        s_res = sem("residual_step")
        s_relu = sem("relu_ready")
        s_hid = sem("hidden_ready")
        s_pj_w, s_pt = sem("proj_weights_loaded"), sem("p_loaded")
        s_pj = sem("proj_done")
        s_pjc = sem("proj_copied")
        s_e = sem("gate_exp")
        s_pl = sem("gate_step")
        s_hn = sem("next_h_ready")
        s_out = sem("stored")
        outs = [0]
        MIXER_STORES = 16 * 7

        def store(eng, dst, src):
            outs[0] += 16
            eng.dma_start(dst, src).then_inc(s_out, 16)
            return outs[0]

        def part(name, names_by_engine):
            return {k: Steps(sem(f"{name}_{k}"), v, int(k == "dve")) for k, v in names_by_engine.items()}

        def gemm(pe, name, nk, rhs, before=None):
            slab0, tile0, slabs, ntiles, per = GEMMS[name]

            def slab(i, s, count, waits):
                pe.wait_ge(s_w[s], 16 * (slab0 // 2 + 1) + 16 * i)
                for mt in range(count):
                    pe.wait_ge(s_bank, (tile0 + s * per + mt + 1) + 2 * per * i)
                    par = (s * per + mt) % 2
                    for kt in range(nk):
                        if waits and s == 0 and mt == 0:
                            pe.wait_ge(*waits(kt))
                        for hf in range(2):
                            at = (mt * nk + kt) * P
                            mm = pe.matmul(ps[:, 2 * par + hf, 0:HALF], slot[s][:, at:at + P], rhs(kt, hf),
                                           start=(kt == 0), stop=(kt == nk - 1))
                    mm.then_inc(s_tile, 1)

            whole = ntiles // (2 * per)
            with pe.Fori(0, whole) as i:
                for s in range(2):
                    slab(i, s, per, before)
            left = ntiles - whole * 2 * per
            if left:
                slab(whole, 0, per, None)
                slab(whole, 1, left - per, None)

        def tile_at(name, k, i=0, step=0):
            return (GEMMS[name][1] + k + 1) + step * i

        def pe_prenorm(pe, n):
            for kt in range(KD):
                pe.wait_ge(s_xg, 8 * n + kt + 1)
                for hf in range(2):
                    mm = pe.matmul(ps[:, 4 + hf, 0:HALF], C("mean_d"),
                                   hid[:, 24 + kt, hf * HALF:(hf + 1) * HALF], start=(kt == 0), stop=(kt == KD - 1))
            mm.then_inc(s_st, 1)

        def pe_postnorm(pe, n):
            pe.wait_ge(s_ss, 8 * n + 8)
            for hf in range(2):
                mm = pe.matmul(ps[:, 4 + hf, 0:HALF], C("mean_d"), ss[:, hf * HALF:(hf + 1) * HALF],
                               start=True, stop=True)
            mm.then_inc(s_st, 1)

        def act_rms(act, r):
            act.wait_ge(s_st, r + 1)
            if r:
                act.wait_ge(s_rb, r)
            nc.scalar.activation(two(rt), ps[:, 4:6, 0:HALF], ACT.Sqrt, bias=RMS_EPS).then_inc(s_rt, 1)

        def dve_rinv(dve, r):
            dve.wait_ge(s_rt, r + 1)
            nc.vector.reciprocal(rb, rt).then_inc(s_rb, 1)
            dve.wait_ge(s_rb, r + 1)

        def act_prenorm(act, n, h, gain, ready):
            for kt in range(KD):
                act.wait_ge(*ready(kt))
                nc.scalar.activation(xg[:, kt, :], h[:, kt, :], ACT.Copy, scale=V("norm_g", gain * 8 + kt))
                nc.scalar.activation(hid[:, 24 + kt, :], h[:, kt, :], ACT.Square).then_inc(s_xg, 1)


        def act_outproj(act, name, n, out):
            for mt in range(KD):
                act.wait_ge(s_tile, tile_at(name, mt))
                if 8 * n + mt >= 2:
                    act.wait_ge(s_ss, 8 * n + mt - 1)
                nc.scalar.activation(two(sqr[mt % 2]), bank(mt % 2), ACT.Square).then_inc(s_sq, 1)
                nc.scalar.activation(two(out[:, mt, :]), bank(mt % 2), ACT.Copy).then_inc(s_bank, 1)

        def pool_sum(pool, n):
            for mt in range(KD):
                pool.wait_ge(s_sq, 8 * n + mt + 1)
                if mt == 0:
                    nc.gpsimd.tensor_copy(ss, sqr[0]).then_inc(s_ss, 1)
                else:
                    pool.wait_ge(s_ss, 8 * n + mt)
                    nc.gpsimd.tensor_tensor(ss, ss, sqr[mt % 2], ALU.add).then_inc(s_ss, 1)

        def dve_residual(dve, n, out, h, gain):
            for kt in range(KD):
                nc.vector.scalar_tensor_tensor(tmp[0], out[:, kt, :], V("norm_g", gain * 8 + kt), rb,
                                               ALU.mult, ALU.mult).then_inc(s_res, 1)
                dve.wait_ge(s_res, 8 * n + kt + 1)
                nc.vector.tensor_tensor(h[:, kt, :], h[:, kt, :], tmp[0], ALU.add).then_inc(s_h, 1)
                dve.wait_ge(s_h, 8 * n + kt + 1)

        ds = bass.ds
        half_b, xg_q = 4 * T, 4 * T
        sig = tiles(hbuf[1], 4)
        aa = xg[:, 0:4, :]
        gg = xg[:, 4:8, :]
        used0 = tail.free[0][2]
        pieces = [hbuf[0][:, :], free[:, used0:], hbuf[1][:, half_b:], pjw[:, :],
                  big[:, NA * (T + 1) + NB * T:], free[:, 0:3 * T], free[:, 6 * T:6 * T + KP * T]]


        r0 = Space(pieces)
        sho = r0.take(NA, NS + 1)
        cvo = r0.take(8, 11)
        ct = r0.take(NG * BH)
        sr = r0.take(24)
        mo = r0.take(NS + 1)
        s_end = [r0.take(2, P) for _ in range(2)]
        crow, nmrow, nmtrow = tmp[0], tmp[1], rt

        rwkv_space = Space([*[p[:, u:] for p, u in [(r[0], r[2]) for r in r0.free]], slot[0][:, :], slot[1][:, :]])

        class RwkvBuffers:

            def __init__(self, r, s_first):
                pair = lambda ap: ap.rearrange("p (j t) -> p j t", j=2)
                halves = lambda ap: (ap[:, 0:2], ap[:, 2:4])
                self.RH = r.take(2, 4, 64)
                rhf = self.RH.rearrange("p a h n -> p (a h n)")
                self.kkr, self.ksq = pair(rhf[:, 0:256]), pair(rhf[:, 256:512])
                self.d0, self.d0t, self.t2 = [r.take(4, P) for _ in range(3)]
                self.n1t, self.n2, self.t1, self.d2, self.d2t = [r.take(4, P) for _ in range(5)]
                self.kkn, self.cum = halves(self.n1t)
                self.kp, self.knr = halves(self.n2)
                self.qq, self.pm = halves(self.t1)
                self.bt, self.kt_ = halves(self.d2)
                self.bh, self.kh = halves(self.d2t)
                self.pp, self.tb, self.vS = [r.take(2, P) for _ in range(3)]
                self.AR = r.take(2, 2, P)
                self.bht, self.kht, self.vt = [r.take(4, 64) for _ in range(3)]
                self.AD = r.take(4, 2 * P)
                self.ME = r.take(4, 2 * P)
                self.GH = r.take(2, 4, P)
                ghf = self.GH.rearrange("p c a n -> p (c a n)")
                self.d4, self.d4t = [ghf[:, i * 512:(i + 1) * 512].rearrange("p (h n) -> p h n", h=4)
                                     for i in range(2)]
                self.t4 = self.tt = self.t1
                self.t8, self.t8t, self.d8t, self.zb, self.zz = self.t2, self.d2, self.d0t, self.d2t, self.d0
                self.t16, self.t16t = self.d4, self.d4t
                self.Wb = self.t2.rearrange("p h n -> p (h n)")
                self.qp, self.yb_, self.rkb, self.yc = self.knr, self.kkn, self.kkn, self.cum
                self.ysq, self.yr, self.sh_ = self.qq, self.pm, self.tb
                self.s_buf = [s_first, r.take(2, P)]
        halves_of_heads = [RwkvBuffers(rwkv_space, s_end[h]) for h in range(2)]

        def bk(b, n=4):
            return ps[:, b, 0:n * P].rearrange("p (h t) -> p h t", t=P)

        def bc(ap, n):
            return ap.unsqueeze(2).to_broadcast([ap.shape[0], ap.shape[1], n])

        def mid(ap, k):
            return ap.unsqueeze(1).to_broadcast([ap.shape[0], k, ap.shape[1]])

        rw = [part(f"rwkv_half{h}", dict(pe=RW_PE, dve=RW_DVE, act=RW_ACT, pool=RW_POOL)) for h in range(2)]
        s_zero, s_rs = sem("state_zeroed"), sem("rwkv_state_stored")

        def rw_bank(h, n, k=4):
            return ps[:, 4 * h + n, 0:k * P].rearrange("p (h t) -> p h t", t=P)

        def uah(arr, h, g):
            return ua[:, 2 * h + arr:2 * h + arr + 2, ds(L * g + 1, L)]

        def th(x, h, g):
            return x[:, 2 * h:2 * h + 2, ds(L * g, L)]

        def dve_rwkv(dve):
            v = nc.vector

            def half(h, g):
                rd, ra, rp, rl, b = rw[h]["dve"], rw[h]["act"], rw[h]["pe"], rw[h]["pool"], halves_of_heads[h]
                bk = lambda n, k=4: rw_bank(h, n, k)

                def after(steps, name, back=0):
                    dve.wait_ge(*steps.at(name, g - back))
                v.tensor_tensor(b.kkr, uah(4, h, g), bc(V("kk", 2 * h, 2), L),
                                ALU.mult).then_inc(*rd.step("kkr"))
                for j in range(2):
                    v.tensor_tensor_scan(b.cum[:, j, :], C("reset"), sig[:, 2 * h + j, ds(L * g, L)], 0.0,
                                         ALU.mult, ALU.add).then_inc(*rd.step(f"cum{j}"))
                after(rd, "cum1")
                v.tensor_tensor(b.tb, b.cum, th(sig, h, g), ALU.subtract).then_inc(*rd.step("prev"))
                yield
                after(rp, "norm")
                v.tensor_scalar(b.knr, bk(0, 2), 1e-24, None, ALU.max).then_inc(*rd.step("floor"))
                yield
                after(ra, "norm")
                v.reciprocal(b.knr, b.knr).then_inc(*rd.step("rinv"))
                after(rd, "rinv")
                v.tensor_tensor(b.kkn, b.kkr, b.knr, ALU.mult).then_inc(*rd.step("kk"))
                yield
                after(ra, "pm")
                for j in range(2):
                    v.tensor_scalar(b.tb[:, j, :], aa[:, 2 * h + j, ds(L * g, L)], -1.0,
                                    V("ka", 2 * h + j), ALU.add,
                                    ALU.mult).then_inc(*rd.step(f"ka{j}"))
                after(rd, "ka1")
                v.scalar_tensor_tensor(b.kp, b.tb, 1.0, uah(4, h, g), ALU.add, ALU.mult).then_inc(*rd.step("kp"))
                v.scalar_tensor_tensor(b.AR[:, :, 0, :], b.kkn, -1.0, b.pm, ALU.mult, ALU.mult).then_inc(*rd.step("at"))
                v.tensor_tensor(b.AR[:, :, 1, :], uah(0, h, g), b.pp, ALU.mult).then_inc(*rd.step("rt"))
                after(rd, "kp")
                v.tensor_tensor(b.tb, b.kkn, th(aa, h, g), ALU.mult).then_inc(*rd.step("kka"))
                after(rd, "kka")
                v.tensor_tensor(b.bt, b.tb, b.qq, ALU.mult).then_inc(*rd.step("bt"))
                v.tensor_tensor(b.kt_, b.kp, b.qq, ALU.mult).then_inc(*rd.step("kt"))
                after(rd, "kt")
                last = b.pp.rearrange("p j (c n) -> p (j c) n", n=SUB)[:, :, SUB - 1:SUB].to_broadcast([P, 4, SUB])
                by_chunk = lambda ap: ap.rearrange("p j (c n) -> p (j c) n", n=SUB)
                v.tensor_tensor(by_chunk(b.bh), by_chunk(b.bt), last, ALU.mult).then_inc(*rd.step("bh"))
                v.tensor_tensor(by_chunk(b.kh), by_chunk(b.kt_), last, ALU.mult).then_inc(*rd.step("kh"))
                yield
                after(rp, "bonus")
                after(rp, "rows")
                v.tensor_tensor(b.vS, ps[:, 4 * h, 256:512].rearrange("p (j t) -> p j t", j=2), b.vS,
                                ALU.mult).then_inc(*rd.step("bon"))
                yield
                after(rp, "gram_b")
                for par in range(2):
                    o = b.AD.rearrange("p (j q) n -> p q j n", q=2)[:, par]
                    v.tensor_tensor(o, ps[:, 4 * h + (3, 0)[par], :].rearrange("p (j n) -> p j n", j=2),
                                    mid(C("gram"), 2), ALU.mult).then_inc(*rd.step(f"ad{par}"))
                yield
                after(rp, "gram_k")
                for par in range(2):
                    o = b.ME.rearrange("p (j q) n -> p q j n", q=2)[:, par]
                    v.tensor_tensor(o, ps[:, 4 * h + 1 + par, :].rearrange("p (j n) -> p j n", j=2),
                                    mid(C("gram"), 2), ALU.mult).then_inc(*rd.step(f"me{par}"))
                yield
                after(rp, "a")
                v.tensor_tensor(b.d0, bk(3), mid(C("bd16"), 4), ALU.mult).then_inc(*rd.step("d0"))
                v.tensor_tensor(b.n2, bk(3), mid(C("n2"), 4), ALU.mult).then_inc(*rd.step("n2"))
                after(rd, "d0")
                v.tensor_tensor(b.t1, b.d0, mid(C("ident"), 4), ALU.add).then_inc(*rd.step("t1"))
                yield
                after(rp, "d2t")
                v.tensor_copy(b.d2t, bk(2)).then_inc(*rd.step("d2t"))
                yield
                after(rp, "t2")
                after(rd, "t1")
                v.tensor_tensor(b.t2, bk(3), b.t1, ALU.add).then_inc(*rd.step("t2"))
                yield
                after(rp, "d4t")
                v.tensor_copy(b.d4t, bk(1)).then_inc(*rd.step("d4t"))
                yield
                after(rp, "t4")
                v.tensor_tensor(b.t4, bk(2), b.t2, ALU.add).then_inc(*rd.step("t4"))
                yield
                after(rp, "t8")
                after(rd, "t4")
                v.tensor_tensor(b.t8, bk(0), b.t4, ALU.add).then_inc(*rd.step("t8"))
                yield
                after(rp, "z")
                v.tensor_copy(b.zb, bk(2)).then_inc(*rd.step("z"))
                yield
                after(rp, "t16")
                v.tensor_tensor(b.t16, bk(3), b.t8, ALU.add).then_inc(*rd.step("t16"))
                yield
                after(rp, "zz")
                v.tensor_copy(b.zz, bk(1)).then_inc(*rd.step("zz"))
                yield
                after(rp, "tt")
                v.tensor_tensor(b.tt, bk(2), b.t16t, ALU.add).then_inc(*rd.step("tt"))
                yield
                after(rp, "qp")
                v.tensor_tensor(b.qp, bk(3, 2), b.AR[:, :, 1, :], ALU.add).then_inc(*rd.step("qp"))
                yield
                after(rp, "gh")
                for c in range(2):
                    v.tensor_tensor(b.GH[:, c], bk(2 * c), mid(C("ones64"), 4),
                                    ALU.mult).then_inc(*rd.step(f"gh{c}"))
                after(rd, "gh1")
                dve.wait_ge(s_zero, 2)
                for c in range(2):
                    for j in range(2):
                        v.scalar_tensor_tensor(b.sh_[:, j, :], b.s_buf[c][:, j, :],
                                               b.pp[:, j, SUB * c + SUB - 1:SUB * c + SUB], b.GH[:, c, 2 + j],
                                               ALU.mult, ALU.add).then_inc(*rd.step(f"s{c}{'ab'[j]}"))
                    after(rd, f"s{c}b")
                    yield
                    after(rp, f"s{c}")
                    v.tensor_tensor(b.s_buf[1 - c], bk(3 * (1 - c), 2), b.sh_, ALU.add).then_inc(*rd.step(["mid", "end"][c]))
                    after(rd, ["mid", "end"][c])
                yield
                after(rp, "mean")
                v.tensor_tensor(b.yc, b.yb_, bk(2, 2), ALU.subtract).then_inc(*rd.step("yc"))
                yield
                after(ra, "ysd")
                v.reciprocal(b.yr, b.yr).then_inc(*rd.step("vinv"))
                after(rd, "vinv")
                v.tensor_tensor(b.yc, b.yc, b.yr, ALU.mult).then_inc(*rd.step("yn"))
                after(rd, "yn")
                for j in range(2):
                    v.scalar_tensor_tensor(b.yc[:, j, :], b.yc[:, j, :], V("rln", 2 * h + j),
                                           b.vS[:, j, :], ALU.mult, ALU.add).then_inc(*rd.step(f"yg{j}"))
                after(rd, "yg1")
                v.tensor_tensor(uah(0, h, g), b.yc, th(gg, h, g), ALU.mult).then_inc(*rd.step("out"))
                after(rd, "out")
                yield

            for h in range(2):
                v.memset(s_end[h], 0.0).then_inc(s_zero, 1)
            with dve.Fori(0, NG) as g:
                in_turn(half(0, g), half(1, g))

        def act_rwkv(act):
            a = nc.scalar

            def half(h, g):
                rd, ra, rp, rl, b = rw[h]["dve"], rw[h]["act"], rw[h]["pe"], rw[h]["pool"], halves_of_heads[h]
                bk = lambda n, k=4: rw_bank(h, n, k)

                def after(steps, name, back=0):
                    act.wait_ge(*steps.at(name, g - back))
                yield
                after(rd, "out", 1)
                a.activation(b.vS, uah(8, h, g), ACT.Copy).then_inc(*ra.step("v"))
                yield
                after(rd, "kkr")
                a.activation(b.ksq, b.kkr, ACT.Square).then_inc(*ra.step("sq"))
                yield
                after(rd, "cum1")
                a.activation(b.pp, b.cum, ACT.Exp, scale=-C0).then_inc(*ra.step("p"))
                a.activation(b.qq, b.cum, ACT.Exp, scale=C0).then_inc(*ra.step("q"))
                yield
                after(rd, "prev")
                a.activation(b.pm, b.tb, ACT.Exp, scale=-C0).then_inc(*ra.step("pm"))
                yield
                after(rd, "floor")
                a.activation(b.knr, b.knr, ACT.Sqrt).then_inc(*ra.step("norm"))
                yield
                after(rp, "rows")
                r4 = lambda n, k: ps[:, 4 * h + n, 256 * k:256 * k + 256].rearrange("p (h n) -> p h n", h=4)
                a.activation(b.RH[:, 0], r4(1, 0), ACT.Copy).then_inc(*ra.step("ar"))
                a.activation(b.bht, r4(1, 1), ACT.Copy)
                a.activation(b.kht, r4(2, 0), ACT.Copy).then_inc(*ra.step("br"))
                a.activation(b.vt, r4(2, 1), ACT.Copy).then_inc(*ra.step("vr"))
                yield
                after(rp, "mv")
                a.activation(b.RH[:, 1], r4(0, 0), ACT.Copy).then_inc(*ra.step("mv"))
                for name, out, n in [("d2", b.d2, 1), ("d4", b.d4, 0), ("d8t", b.d8t, 3), ("t8t", b.t8t, 1),
                                     ("t16t", b.t16t, 0)]:
                    yield
                    after(rp, name)
                    a.activation(out, bk(n), ACT.Copy).then_inc(*ra.step(name))
                yield
                after(rp, "w")
                a.activation(b.Wb.rearrange("p (a h n) -> p h a n", a=2, h=4),
                             bk(3).rearrange("p h (a n) -> p h a n", a=2), ACT.Copy).then_inc(*ra.step("w"))
                yield
                after(rp, "y")
                a.activation(b.yb_, bk(1, 2), ACT.Copy).then_inc(*ra.step("y"))
                yield
                after(rd, "yc")
                a.activation(b.ysq, b.yc, ACT.Square).then_inc(*ra.step("ysq"))
                yield
                after(rp, "var")
                a.activation(b.yr, bk(3, 2), ACT.Sqrt, bias=A_LN_EPS).then_inc(*ra.step("ysd"))
                yield

            with act.Fori(0, NG) as g:
                in_turn(half(0, g), half(1, g))

        def pool_rwkv(pool):
            def half(h, g):
                rd, ra, rp, rl, b = rw[h]["dve"], rw[h]["act"], rw[h]["pe"], rw[h]["pool"], halves_of_heads[h]
                bk = lambda n, k=4: rw_bank(h, n, k)

                def after(steps, name, back=0):
                    pool.wait_ge(*steps.at(name, g - back))
                after(rd, "kka")
                nc.gpsimd.tensor_tensor(b.rkb, uah(0, h, g), b.kp, ALU.mult).then_inc(*rl.step("rk"))
                after(rl, "rk")
                nc.gpsimd.tensor_tensor(b.rkb, b.rkb, bc(V("rk", 2 * h, 2), L), ALU.mult).then_inc(*rl.step("rkw"))
                yield
                after(rd, "ad1")
                nc.gpsimd.tensor_tensor(b.d0t, b.AD[:, :, 0:P], mid(C("bd16"), 4), ALU.mult).then_inc(*rl.step("d0t"))
                nc.gpsimd.tensor_tensor(b.n1t, b.AD[:, :, 0:P], mid(C("n1t"), 4), ALU.mult).then_inc(*rl.step("n1t"))
                yield

            with pool.Fori(0, NG) as g:
                in_turn(half(0, g), half(1, g))

        def pe_rwkv(pe):
            def half(h, g):
                rd, ra, rp, rl, b = rw[h]["dve"], rw[h]["act"], rw[h]["pe"], rw[h]["pool"], halves_of_heads[h]
                bk = lambda n, k=4: rw_bank(h, n, k)

                def after(steps, name, back=0):
                    pe.wait_ge(*steps.at(name, g - back))

                def mm4(n, lhs, rhs, step):
                    for hh in range(4):
                        mm = pe.matmul(bk(n)[:, hh, :], lhs[:, hh, :], rhs[:, hh, :], start=True, stop=True)
                    mm.then_inc(*rp.step(step))

                def transposed(n, x, step):
                    for hh in range(4):
                        mm = pe.transpose(bk(n)[:, hh, :], x(hh), C("ident"))
                    mm.then_inc(*rp.step(step))
                o = 4 * h
                after(ra, "sq")
                pe.matmul(ps[:, o, 0:256], C("ones64"), b.ksq, start=True, stop=True).then_inc(*rp.step("norm"))
                yield
                after(rl, "rkw")
                after(rd, "floor")
                pe.matmul(ps[:, o, 256:512], C("ones64"), b.rkb, start=True, stop=True).then_inc(*rp.step("bonus"))
                yield
                after(rd, "kh")
                for j in range(2):
                    pe.transpose(ps[:, o + 1, j * P:(j + 1) * P], b.AR[:, j, 0, :], C("ident"))
                    pe.transpose(ps[:, o + 1, 256 + j * P:256 + (j + 1) * P], b.bh[:, j, :], C("ident"))
                    pe.transpose(ps[:, o + 2, j * P:(j + 1) * P], b.kh[:, j, :], C("ident"))
                    mm = pe.transpose(ps[:, o + 2, 256 + j * P:256 + (j + 1) * P], b.vS[:, j, :], C("ident"))
                mm.then_inc(*rp.step("rows"))
                for w, banks, step, waits in [(b.bt, (3, 0), "gram_b", (rd, "bon")), (b.kt_, (1, 2), "gram_k", (ra, "vr"))]:
                    yield
                    after(*waits)
                    for par in range(2):
                        rows = slice(64 * par, 64 * par + 64)
                        for j in range(2):
                            mm = pe.matmul(ps[:, o + banks[par], 256 * j:256 * j + 256], w[rows, j, :],
                                           b.AR[rows, j, :, :], start=True, stop=True)
                    mm.then_inc(*rp.step(step))
                yield
                after(rd, "ad1")
                transposed(3, lambda hh: b.AD[:, hh, 0:P], "a")
                yield
                after(rd, "me1")
                for hh in range(4):
                    mm = pe.matmul(ps[:, o, 64 * hh:64 * hh + 64], b.ME[:, hh, 0:P], b.vt[:, hh, :],
                                   start=True, stop=True)
                mm.then_inc(*rp.step("mv"))
                yield
                after(rl, "d0t")
                after(rd, "d0")
                mm4(1, b.d0t, b.d0, "d2")
                mm4(2, b.d0, b.d0t, "d2t")
                yield
                after(rd, "d2t")
                after(rd, "t1")
                mm4(3, b.d2t, b.t1, "t2")
                yield
                after(ra, "d2")
                mm4(0, b.d2t, b.d2, "d4")
                mm4(1, b.d2, b.d2t, "d4t")
                yield
                after(rd, "d4t")
                after(rd, "t2")
                mm4(2, b.d4t, b.t2, "t4")
                yield
                after(ra, "d4")
                mm4(3, b.d4, b.d4t, "d8t")
                yield
                after(ra, "d8t")
                after(rd, "t4")
                mm4(0, b.d8t, b.t4, "t8")
                yield
                after(rd, "t8")
                transposed(1, lambda hh: b.t8[:, hh, :], "t8t")
                yield
                after(rl, "n1t")
                mm4(2, b.n1t, b.t8, "z")
                yield
                after(rd, "z")
                after(ra, "t8t")
                mm4(3, b.t8t, b.zb, "t16")
                yield
                after(rd, "t16")
                transposed(0, lambda hh: b.t16[:, hh, :], "t16t")
                yield
                after(ra, "t16t")
                mm4(1, b.n2, b.t16t, "zz")
                yield
                after(rd, "zz")
                mm4(2, b.t16, b.zz, "tt")
                yield
                after(rd, "tt")
                after(ra, "mv")
                for hh in range(4):
                    mm = pe.matmul(bk(3)[:, hh, :].rearrange("p (a n) -> p a n", a=2), b.tt[:, hh, :],
                                   b.RH[:, :, hh, :], start=True, stop=True)
                mm.then_inc(*rp.step("w"))
                yield
                after(ra, "w")
                w1 = lambda hh: b.Wb[:, 64 * hh:64 * hh + 64]
                u0 = lambda hh: b.Wb[:, 256 + 64 * hh:256 + 64 * hh + 64]
                for hh in range(4):
                    j, par = hh // 2, hh % 2
                    mm = pe.matmul(ps[64 * par:64 * par + 64, o + 3, j * P:(j + 1) * P], w1(hh), b.AD[:, hh, P:2 * P],
                                   start=True, stop=True)
                mm.then_inc(*rp.step("qp"))
                for c in range(2):
                    rows = slice(64 * c, 64 * c + 64)
                    for j in range(2):
                        two_heads = slice(P * j, P * j + P)
                        bhj = b.bht.rearrange("p h n -> p (h n)")[rows, two_heads]
                        khj = b.kht.rearrange("p h n -> p (h n)")[rows, two_heads]
                        vtj = b.vt.rearrange("p h n -> p (h n)")[rows, two_heads]
                        pe.matmul(bk(2 * c)[:, j, :], b.Wb[rows, two_heads], bhj, start=True, stop=True)
                        pe.matmul(bk(2 * c)[:, 2 + j, :], bhj, b.Wb[rows, 256 + P * j:256 + P * j + P],
                                  start=True, stop=False)
                        mm = pe.matmul(bk(2 * c)[:, 2 + j, :], khj, vtj, start=False, stop=True)
                mm.then_inc(*rp.step("gh"))
                for hh in range(4):
                    j, par = hh // 2, hh % 2
                    y = ps[64 * par:64 * par + 64, o + 1, j * P:(j + 1) * P]
                    pe.matmul(y, u0(hh), b.AD[:, hh, P:2 * P], start=(j == 0), stop=False, skip_group_check=True)
                    pe.matmul(y, b.vt[:, hh, :], b.ME[:, hh, P:2 * P], start=False, stop=False, skip_group_check=True)
                yield
                after(rd, "qp")
                for c in range(2):
                    after(rd, ["gh1", "mid"][c])
                    for j in range(2):
                        mm = pe.matmul(bk(3 * (1 - c))[:, j, :], b.GH[:, c, j, :], b.s_buf[c][:, j, :],
                                       start=True, stop=True)
                    mm.then_inc(*rp.step(f"s{c}"))
                    for j in range(2):
                        mm = pe.matmul(ps[:, o + 1, j * P + SUB * c:j * P + SUB * c + SUB], b.s_buf[c][:, j, :],
                                       b.qp[:, j, SUB * c:SUB * c + SUB], start=False, stop=(c == 1),
                                       skip_group_check=True)
                    if c == 0:
                        yield
                mm.then_inc(*rp.step("y"))
                yield
                after(ra, "y")
                pe.matmul(bk(2, 2), C("mean64"), b.yb_, start=True, stop=True).then_inc(*rp.step("mean"))
                yield
                after(ra, "ysq")
                pe.matmul(bk(3, 2), C("mean64"), b.ysq, start=True, stop=True).then_inc(*rp.step("var"))
                yield

            with pe.Fori(0, NG) as g:
                in_turn(half(0, g), half(1, g))

        r1 = Space([pieces[0][:, 1024:], *pieces[1:]])
        sst = r1.take(4, NS, 64)
        um, vm = r1.take(2, NS, 64), r1.take(2, NS, 64)
        rows3 = r1.take(3, 4, P)
        xk, xq, xn, xkk, xw, xa, xkp, xb, xan, xbo, xy, xyc, xr = [r1.take(4, NS) for _ in range(13)]
        RS_DVE = ["kkr", "floor", "rinv", "kk", "a1", "ka", "kp", "an", "b", "rk", "rkw", "bon"]
        RS_DVEJ = ["um", "vm", "sw", "s"]
        RS_DVE2 = ["yc", "rinv2", "yn", "yl", "yg", "out"]
        rs_sem = {k: sem(f"rwkv1_{k}") for k in ("pe", "dve", "act")}
        sd = Steps(rs_sem["dve"], RS_DVE)
        sdj = Steps(rs_sem["dve"], RS_DVEJ, len(RS_DVE))
        sd2 = Steps(rs_sem["dve"], RS_DVE2, len(RS_DVE) + 4 * len(RS_DVEJ))
        sa = Steps(rs_sem["act"], ["sq", "norm", "w", "rows", "y", "ysq", "ysd"])
        sp_ = Steps(rs_sem["pe"], ["norm", "bonus", "rows"])
        spj = Steps(rs_sem["pe"], ["sa", "outer"], 3)
        sp2 = Steps(rs_sem["pe"], ["y", "mean", "var"], 3 + 8)
        s_sst, s_cst = sem("rwkv_state_loaded"), sem("mlstm_state_loaded")
        uas = lambda arr: ua[:, arr:arr + 4, TP + 1:]
        smp = lambda x: x[:, :, TP:]
        eight = C("ident")[0:NS, 0:NS]

        def dve_rwkv1(dve):
            v = nc.vector

            def after(steps, name, it=0):
                dve.wait_ge(*steps.at(name, it))
            v.tensor_tensor(xk, uas(4), bc(V("kk", 0, 4), NS), ALU.mult).then_inc(*sd.step("kkr"))
            after(sp_, "norm")
            v.tensor_scalar(xn, ps[:, 0, 0:32].rearrange("p (j t) -> p j t", j=4), 1e-24, None,
                            ALU.max).then_inc(*sd.step("floor"))
            after(sa, "norm")
            v.reciprocal(xn, xn).then_inc(*sd.step("rinv"))
            after(sd, "rinv")
            v.tensor_tensor(xkk, xk, xn, ALU.mult).then_inc(*sd.step("kk"))
            v.tensor_scalar(xa, smp(aa), -1.0, None, ALU.add).then_inc(*sd.step("a1"))
            after(sd, "a1")
            v.tensor_tensor(xa, xa, bc(V("ka", 0, 4), NS), ALU.mult).then_inc(*sd.step("ka"))
            after(sd, "ka")
            v.scalar_tensor_tensor(xkp, xa, 1.0, uas(4), ALU.add, ALU.mult).then_inc(*sd.step("kp"))
            v.tensor_scalar(xan, xkk, -1.0, None, ALU.mult).then_inc(*sd.step("an"))
            v.tensor_tensor(xb, xkk, smp(aa), ALU.mult).then_inc(*sd.step("b"))
            after(sd, "kp")
            v.tensor_tensor(xbo, uas(0), xkp, ALU.mult).then_inc(*sd.step("rk"))
            after(sd, "rk")
            v.tensor_tensor(xbo, xbo, bc(V("rk", 0, 4), NS), ALU.mult).then_inc(*sd.step("rkw"))
            after(sp_, "bonus")
            v.tensor_tensor(xbo, ps[:, 0, 32:64].rearrange("p (j t) -> p j t", j=4), uas(8),
                            ALU.mult).then_inc(*sd.step("bon"))
            dve.wait_ge(s_sst, 16)
            after(sa, "rows")
            for j in range(4):
                after(spj, "sa", j)
                b = 2 * (j % 2)
                v.tensor_tensor(um[0:NS], ps[0:NS, b:b + 2, :].rearrange("p q (s n) -> p q s n", s=NS),
                                eight.unsqueeze(1).unsqueeze(3).to_broadcast([NS, 2, NS, 64]),
                                ALU.mult).then_inc(*sdj.step("um"))
                vr = rows3[0:NS, 2, j, :].rearrange("p (q n) -> p q n", q=2)
                v.tensor_tensor(vm[0:NS], vr.unsqueeze(2).to_broadcast([NS, 2, NS, 64]),
                                eight.unsqueeze(1).unsqueeze(3).to_broadcast([NS, 2, NS, 64]),
                                ALU.mult).then_inc(*sdj.step("vm"))
                v.tensor_tensor(sst[:, j], sst[:, j], bc(xw[:, j, :], 64), ALU.mult).then_inc(*sdj.step("sw"))
                after(sdj, "sw", j)
                after(spj, "outer", j)
                v.tensor_tensor(sst[:, j], sst[:, j], ps[:, 4 + j % 2, :].rearrange("p (s n) -> p s n", s=NS),
                                ALU.add).then_inc(*sdj.step("s"))
            after(sp2, "mean")
            v.tensor_tensor(xyc, xy, ps[:, 0, 0:32].rearrange("p (j t) -> p j t", j=4),
                            ALU.subtract).then_inc(*sd2.step("yc"))
            after(sa, "ysd")
            v.reciprocal(xr, xr).then_inc(*sd2.step("rinv2"))
            after(sd2, "rinv2")
            v.tensor_tensor(xyc, xyc, xr, ALU.mult).then_inc(*sd2.step("yn"))
            after(sd2, "yn")
            v.tensor_tensor(xyc, xyc, bc(V("rln", 0, 4), NS), ALU.mult).then_inc(*sd2.step("yl"))
            after(sd2, "yl")
            v.tensor_tensor(xyc, xyc, xbo, ALU.add).then_inc(*sd2.step("yg"))
            after(sd2, "yg")
            v.tensor_tensor(uas(0), xyc, smp(gg), ALU.mult).then_inc(*sd2.step("out"))
            after(sd2, "out")

        def act_rwkv1(act):
            a = nc.scalar

            def after(steps, name, it=0):
                act.wait_ge(*steps.at(name, it))
            after(sd, "kkr")
            a.activation(xq, xk, ACT.Square).then_inc(*sa.step("sq"))
            after(sd, "floor")
            a.activation(xn, xn, ACT.Sqrt).then_inc(*sa.step("norm"))
            a.activation(xw, smp(sig), ACT.Exp, scale=-C0).then_inc(*sa.step("w"))
            after(sp_, "rows")
            a.activation(rows3[0:NS].rearrange("p k j n -> p k (j n)"), ps[0:NS, 4:7, :],
                         ACT.Copy).then_inc(*sa.step("rows"))
            after(sp2, "y")
            a.activation(xy[0:64], ps[0:64, 6, 0:32].rearrange("p (j t) -> p j t", j=4), ACT.Copy)
            a.activation(xy[64:P], ps[64:P, 7, 0:32].rearrange("p (j t) -> p j t", j=4),
                         ACT.Copy).then_inc(*sa.step("y"))
            after(sd2, "yc")
            a.activation(xq, xyc, ACT.Square).then_inc(*sa.step("ysq"))
            after(sp2, "var")
            a.activation(xr, ps[:, 1, 0:32].rearrange("p (j t) -> p j t", j=4), ACT.Sqrt,
                         bias=A_LN_EPS).then_inc(*sa.step("ysd"))

        def pe_rwkv1(pe):
            def after(steps, name, it=0):
                pe.wait_ge(*steps.at(name, it))
            flat = lambda x: x.rearrange("p j t -> p (j t)")
            after(sa, "sq")
            pe.matmul(ps[:, 0, 0:32], C("ones64"), flat(xq), start=True, stop=True).then_inc(*sp_.step("norm"))
            after(sd, "rkw")
            pe.matmul(ps[:, 0, 32:64], C("ones64"), flat(xbo), start=True, stop=True).then_inc(*sp_.step("bonus"))
            for k, src in enumerate([xb, xkp, uas(8)]):
                for j in range(4):
                    mm = pe.transpose(ps[0:NS, 4 + k, j * P:(j + 1) * P], src[:, j, :], C("ident"))
            mm.then_inc(*sp_.step("rows"))
            after(sd, "bon")
            pe.wait_ge(s_sst, 16)
            for j in range(4):
                if j >= 2:
                    after(sdj, "um", j - 2)
                for par in range(2):
                    r = slice(64 * par, 64 * par + 64)
                    mm = pe.matmul(ps[0:NS, 2 * (j % 2) + par, :], xan[r, j, :],
                                   sst[r, j].rearrange("p s n -> p (s n)"), start=True, stop=True)
                mm.then_inc(*spj.step("sa"))
                after(sdj, "vm", j)
                if j >= 2:
                    after(sdj, "s", j - 2)
                after(sa, "rows")
                for par in range(2):
                    o = ps[64 * par:64 * par + 64, 4 + j % 2, :]
                    c = slice(64 * par, 64 * par + 64)
                    pe.matmul(o, rows3[0:NS, 0, j, c], um[0:NS, par].rearrange("p s n -> p (s n)"),
                              start=True, stop=False)
                    mm = pe.matmul(o, rows3[0:NS, 1, j, c], vm[0:NS, par].rearrange("p s n -> p (s n)"),
                                   start=False, stop=True)
                mm.then_inc(*spj.step("outer"))
            after(sdj, "s", 3)
            for j in range(4):
                for b in range(NS):
                    for par in range(2):
                        r = slice(64 * par, 64 * par + 64)
                        mm = pe.matmul(ps[r, 6 + par, NS * j + b:NS * j + b + 1], sst[r, j, b, :],
                                       ua[r, j, TP + 1 + b:TP + 2 + b], start=True, stop=True)
            mm.then_inc(*sp2.step("y"))
            after(sa, "y")
            pe.matmul(ps[:, 0, 0:32], C("mean64"), flat(xy), start=True, stop=True).then_inc(*sp2.step("mean"))
            after(sa, "ysq")
            pe.matmul(ps[:, 1, 0:32], C("mean64"), flat(xq), start=True, stop=True).then_inc(*sp2.step("var"))

        r2 = Space([pieces[0][:, 1024:], *pieces[1:]])
        kS, vS2, PT, IW, QI, EN, HD, HB, E, KH = [r2.take(4, P) for _ in range(10)]
        cn = r2.take(4, 2 * P)
        vo = r2.take(4, 2 * P)
        mprev, wia, wi, wca, wc = [r2.take(4) for _ in range(5)]
        ml = part("mlstm", dict(
            pe=["nm", "nb", "rows", "sc", "num", "den", "st", "mean", "var"],
            dve=["wia", "wca", "e0", "e1", "e2", "e3", "iwa", "mprev", "kh", "pt", "qi", "c0", "c1", "c2", "c3",
                 "hd", "hr", "hb", "ho", "yc", "rinv", "yn", "out"],
            act=["k", "v", "wi", "wc", "e", "iw", "en", "vo", "abs", "ysq", "ysd"]))
        mp, md, ma = ml["pe"], ml["dve"], ml["act"]
        s_mz = sem("mlstm_zeroed")
        ubg = lambda arr, g: ub[:, arr:arr + 4, ds(L * g, L)]

        def dve_mlstm(dve):
            v = nc.vector
            dve.wait_ge(s_st1, 16)
            v.memset(cn, 0.0).then_inc(s_mz, 1)
            v.memset(mprev, 0.0).then_inc(s_mz, 1)
            v.memset(vo[:, :, P:2 * P], 1.0).then_inc(s_mz, 1)
            dve.wait_ge(s_mz, 3)
            with dve.Fori(0, NG) as g:
                def after(steps, name):
                    dve.wait_ge(*steps.at(name, g))
                after(mp, "nm")
                nml = bk(0)[:, :, P - 1]
                v.tensor_tensor(wia, ct[:, ds(4 * g, 4)], nml, ALU.add).then_inc(*md.step("wia"))
                v.tensor_tensor(wca, mprev, nml, ALU.add).then_inc(*md.step("wca"))
                for h in range(4):
                    v.scalar_tensor_tensor(E[:, h, :], bk(0)[:, h, :], ct[:, ds(4 * g + h, 1)], C("neg"),
                                           ALU.add, ALU.min).then_inc(*md.step(f"e{h}"))
                v.tensor_tensor(IW, bk(0), bc(mprev, P), ALU.add).then_inc(*md.step("iwa"))
                after(md, "iwa")
                v.tensor_scalar(mprev, nml, -1.0, None, ALU.mult).then_inc(*md.step("mprev"))
                after(mp, "rows")
                after(ma, "wc")
                v.tensor_tensor(KH, bk(2), bc(wi, P), ALU.mult).then_inc(*md.step("kh"))
                after(mp, "sc")
                after(ma, "iw")
                v.tensor_tensor(PT, bk(4), E, ALU.mult).then_inc(*md.step("pt"))
                v.tensor_tensor(QI, ubg(0, g), IW, ALU.mult).then_inc(*md.step("qi"))
                after(mp, "st")
                for h in range(4):
                    v.scalar_tensor_tensor(cn[:, h, :], cn[:, h, :], wc[:, h:h + 1],
                                           ps[:, 2 + h // 2, 256 * (h % 2):256 * (h % 2) + 256],
                                           ALU.mult, ALU.add).then_inc(*md.step(f"c{h}"))
                after(ma, "abs")
                v.tensor_tensor(HD, HD, EN, ALU.max).then_inc(*md.step("hd"))
                after(md, "hd")
                v.reciprocal(HD, HD).then_inc(*md.step("hr"))
                after(md, "hr")
                v.tensor_tensor(HB, bk(5), HD, ALU.mult).then_inc(*md.step("hb"))
                after(md, "hb")
                v.tensor_tensor(HB, HB, ubg(12, g), ALU.mult).then_inc(*md.step("ho"))
                after(mp, "mean")
                v.tensor_tensor(HB, HB, bk(4), ALU.subtract).then_inc(*md.step("yc"))
                after(ma, "ysd")
                v.reciprocal(HD, HD).then_inc(*md.step("rinv"))
                after(md, "rinv")
                v.tensor_tensor(HB, HB, HD, ALU.mult).then_inc(*md.step("yn"))
                after(md, "yn")
                v.tensor_tensor(ubg(0, g), HB, bc(V("mgn", 0, 4), P), ALU.mult).then_inc(*md.step("out"))
                after(md, "out")

        def act_mlstm(act):
            a = nc.scalar
            with act.Fori(0, NG) as g:
                def after(steps, name, back=0):
                    act.wait_ge(*steps.at(name, g - back))
                after(md, "out", 1)
                a.activation(kS, ubg(4, g), ACT.Copy, scale=BHD ** -0.5).then_inc(*ma.step("k"))
                a.activation(vS2, ubg(8, g), ACT.Copy).then_inc(*ma.step("v"))
                after(md, "wca")
                a.activation(wi, wia, ACT.Exp).then_inc(*ma.step("wi"))
                a.activation(wc, wca, ACT.Exp).then_inc(*ma.step("wc"))
                after(md, "e3")
                a.activation(E, E, ACT.Exp).then_inc(*ma.step("e"))
                after(md, "iwa")
                a.activation(IW, IW, ACT.Exp).then_inc(*ma.step("iw"))
                after(mp, "nb")
                a.activation(EN, bk(1), ACT.Exp).then_inc(*ma.step("en"))
                after(mp, "rows")
                a.activation(vo[:, :, 0:P], bk(3), ACT.Copy).then_inc(*ma.step("vo"))
                after(mp, "den")
                a.activation(HD, bk(6), ACT.Abs).then_inc(*ma.step("abs"))
                after(md, "yc")
                a.activation(E, HB, ACT.Square).then_inc(*ma.step("ysq"))
                after(mp, "var")
                a.activation(HD, bk(7), ACT.Sqrt, bias=GN_EPS).then_inc(*ma.step("ysd"))

        def pe_mlstm(pe):
            sel = lambda h: C("sel", h * P, P)[0:4]
            pe.wait_ge(*sd2.at("out"))
            with pe.Fori(0, NG) as g:
                def after(steps, name, back=0):
                    pe.wait_ge(*steps.at(name, g - back))
                after(md, "out", 1)
                for h in range(4):
                    mm = pe.matmul(bk(0)[:, h, :], sel(h), nmrow[0:4, ds(L * g, L)], start=True, stop=True)
                mm.then_inc(*mp.step("nm"))
                for h in range(4):
                    mm = pe.matmul(bk(1)[:, h, :], sel(h), nmtrow[0:4, ds(L * g, L)], start=True, stop=True)
                mm.then_inc(*mp.step("nb"))
                after(ma, "v")
                for h in range(4):
                    pe.transpose(bk(2)[:, h, :], kS[:, h, :], C("ident"))
                    mm = pe.transpose(bk(3)[:, h, :], vS2[:, h, :], C("ident"))
                mm.then_inc(*mp.step("rows"))
                for h in range(4):
                    mm = pe.matmul(bk(4)[:, h, :], kS[:, h, :], ub[:, h, ds(L * g, L)], start=True, stop=True)
                mm.then_inc(*mp.step("sc"))
                after(md, "qi")
                after(ma, "vo")
                pe.wait_ge(s_mz, 3)
                for h in range(4):
                    pe.matmul(bk(5)[:, h, :], vo[:, h, 0:P], PT[:, h, :], start=True, stop=False)
                    mm = pe.matmul(bk(5)[:, h, :], cn[:, h, 0:P], QI[:, h, :], start=False, stop=True)
                mm.then_inc(*mp.step("num"))
                for h in range(4):
                    pe.matmul(bk(6)[:, h, :], C("ones"), PT[:, h, :], start=True, stop=False)
                    mm = pe.matmul(bk(6)[:, h, :], cn[:, h, P:2 * P], QI[:, h, :], start=False, stop=True)
                mm.then_inc(*mp.step("den"))
                for h in range(4):
                    mm = pe.matmul(ps[:, 2 + h // 2, 256 * (h % 2):256 * (h % 2) + 256], KH[:, h, :], vo[:, h, :],
                                   start=True, stop=True)
                mm.then_inc(*mp.step("st"))
                after(md, "ho")
                pe.matmul(bk(4), C("mean128"), HB, start=True, stop=True).then_inc(*mp.step("mean"))
                after(ma, "ysq")
                pe.matmul(bk(7), C("mean128"), E, start=True, stop=True).then_inc(*mp.step("var"))

        r3 = Space([pieces[0][:, 1024:], *pieces[1:]])
        vm3 = r3.take(NS, P)
        rows2 = r3.take(2, 4, P)
        n_new, khs, qn, hs, dn, ys = [r3.take(4, NS) for _ in range(6)]
        sb3 = r3.take(4, 24)
        cst = xg[:, :, :].rearrange("p k t -> p (k t)")[:, 0:4 * NS * P].rearrange("p (h s n) -> p h s n", h=4, s=NS)
        m1_sem = {k: sem(f"mlstm1_{k}") for k in ("pe", "dve", "act")}
        nd = Steps(m1_sem["dve"], ["kh", "nw", "n", "qn"])
        ndj = Steps(m1_sem["dve"], ["vm", "cw", "c"], 4)
        nd2 = Steps(m1_sem["dve"], ["dn", "dr", "h", "ho", "yc", "rinv", "yn", "out"], 4 + 12)
        na = Steps(m1_sem["act"], ["exp", "bc", "rows", "abs", "ysq", "ysd"])
        np_ = Steps(m1_sem["pe"], ["bc", "rows", "qn"])
        npj = Steps(m1_sem["pe"], ["outer"], 3)
        np2 = Steps(m1_sem["pe"], ["num", "mean", "var"], 3 + 4)
        ubs = lambda arr: ub[:, arr:arr + 4, TP:]
        p32 = lambda b: ps[:, b, 0:32].rearrange("p (h s) -> p h s", h=4)

        def dve_mlstm1(dve):
            v = nc.vector

            def after(steps, name, it=0):
                dve.wait_ge(*steps.at(name, it))
            after(na, "bc")
            iw, wi1, en1 = [sb3[:, :, 8 * k:8 * k + 8] for k in range(3)]
            v.scalar_tensor_tensor(khs, ubs(4), BHD ** -0.5, wi1, ALU.mult, ALU.mult).then_inc(*nd.step("kh"))
            v.tensor_tensor(n_new, V("n", 0, 32).rearrange("p (h s) -> p h s", h=4), iw,
                            ALU.mult).then_inc(*nd.step("nw"))
            after(nd, "nw")
            v.tensor_tensor(n_new, n_new, khs, ALU.add).then_inc(*nd.step("n"))
            after(nd, "n")
            v.tensor_tensor(qn, n_new, ubs(0), ALU.mult).then_inc(*nd.step("qn"))
            after(na, "rows")
            dve.wait_ge(s_cst, 16)
            for h in range(4):
                if h:
                    after(npj, "outer", h - 1)
                v.tensor_tensor(vm3[0:NS], mid(rows2[0:NS, 1, h, :], NS), bc(eight, P),
                                ALU.mult).then_inc(*ndj.step("vm"))
                v.tensor_tensor(cst[:, h], cst[:, h], bc(iw[:, h, :], P), ALU.mult).then_inc(*ndj.step("cw"))
                after(ndj, "cw", h)
                after(npj, "outer", h)
                b = 2 * (h % 2)
                v.tensor_tensor(cst[:, h], cst[:, h],
                                ps[:, b:b + 2, :].rearrange("p q (s n) -> p (q s) n", n=P),
                                ALU.add).then_inc(*ndj.step("c"))
            after(na, "abs")
            v.tensor_tensor(dn, dn, en1, ALU.max).then_inc(*nd2.step("dn"))
            after(nd2, "dn")
            v.reciprocal(dn, dn).then_inc(*nd2.step("dr"))
            after(nd2, "dr")
            after(np2, "num")
            v.tensor_tensor(hs, p32(7), dn, ALU.mult).then_inc(*nd2.step("h"))
            after(nd2, "h")
            v.tensor_tensor(hs, hs, ubs(12), ALU.mult).then_inc(*nd2.step("ho"))
            after(np2, "mean")
            v.tensor_tensor(hs, hs, p32(4), ALU.subtract).then_inc(*nd2.step("yc"))
            after(na, "ysd")
            v.reciprocal(dn, dn).then_inc(*nd2.step("rinv"))
            after(nd2, "rinv")
            v.tensor_tensor(hs, hs, dn, ALU.mult).then_inc(*nd2.step("yn"))
            after(nd2, "yn")
            v.tensor_tensor(ubs(0), hs, bc(V("mgn", 0, 4), NS), ALU.mult).then_inc(*nd2.step("out"))

        def act_mlstm1(act):
            a = nc.scalar

            def after(steps, name, it=0):
                act.wait_ge(*steps.at(name, it))
            act.wait_ge(*row_d.at("en"))
            a.activation(sr[0:4], sr[0:4], ACT.Exp).then_inc(*na.step("exp"))
            after(np_, "bc")
            a.activation(sb3, ps[:, 0, 0:96].rearrange("p (h n) -> p h n", h=4), ACT.Copy).then_inc(*na.step("bc"))
            after(np_, "rows")
            a.activation(rows2[0:NS].rearrange("p k h n -> p k (h n)"), ps[0:NS, 4:6, :],
                         ACT.Copy).then_inc(*na.step("rows"))
            after(np_, "qn")
            a.activation(dn, p32(6), ACT.Abs).then_inc(*na.step("abs"))
            after(nd2, "yc")
            a.activation(ys, hs, ACT.Square).then_inc(*na.step("ysq"))
            after(np2, "var")
            a.activation(dn, p32(5), ACT.Sqrt, bias=GN_EPS).then_inc(*na.step("ysd"))

        def pe_mlstm1(pe):
            def after(steps, name, it=0):
                pe.wait_ge(*steps.at(name, it))
            flat = lambda x: x.rearrange("p j t -> p (j t)")
            after(md, "out", NG - 1)
            after(na, "exp")
            for h in range(4):
                mm = pe.matmul(ps[:, 0, 24 * h:24 * h + 24], C("sel", h * P, P)[0:4], sr[0:4, :],
                               start=True, stop=True)
            mm.then_inc(*np_.step("bc"))
            after(nd, "kh")
            for h in range(4):
                pe.transpose(ps[0:NS, 4, h * P:(h + 1) * P], khs[:, h, :], C("ident"))
                mm = pe.transpose(ps[0:NS, 5, h * P:(h + 1) * P], ubs(8)[:, h, :], C("ident"))
            mm.then_inc(*np_.step("rows"))
            after(nd, "qn")
            pe.matmul(ps[:, 6, 0:32], C("ones"), flat(qn), start=True, stop=True).then_inc(*np_.step("qn"))
            after(na, "rows")
            for h in range(4):
                after(ndj, "vm", h)
                if h >= 2:
                    after(ndj, "c", h - 2)
                for q in range(2):
                    mm = pe.matmul(ps[:, 2 * (h % 2) + q, :], rows2[0:NS, 0, h, :],
                                   vm3[0:NS, 4 * q:4 * q + 4, :], start=True, stop=True)
                mm.then_inc(*npj.step("outer"))
            after(ndj, "c", 3)
            for h in range(4):
                for b in range(NS):
                    mm = pe.matmul(ps[:, 7, NS * h + b:NS * h + b + 1], cst[:, h, b, :],
                                   ub[:, h, TP + b:TP + b + 1], start=True, stop=True)
            mm.then_inc(*np2.step("num"))
            after(nd2, "ho")
            pe.matmul(ps[:, 4, 0:32], C("mean128"), flat(hs), start=True, stop=True).then_inc(*np2.step("mean"))
            after(na, "ysq")
            pe.matmul(ps[:, 5, 0:32], C("mean128"), flat(ys), start=True, stop=True).then_inc(*np2.step("var"))

        s_ev, s_sub, s_shf = sem("in_evacuated"), sem("shift_difference"), sem("shift_mixed")
        s_raw = sem("raw_saved")
        s_tn, s_lp, s_lc = sem("lora_inputs"), sem("lora_products"), sem("lora_outputs")
        s_cv, s_cvd = sem("convolution_step"), sem("silu_done")
        s_zc = sem("zero_column")
        acc = [sqr[0], sqr[1]]
        RD = ["i", "ib", "f", "fb", "abs", "lf", "zero", "b", "c", "m", "nm", "nmt", "mo", "t", "tm", "iw", "wi",
              "en", "ct"]
        row_d, row_a, row_p = (Steps(sem(f"rows_{k}"), n) for k, n in
                               [("dve", RD), ("act", ["gate", "exp", "ln"]), ("pe", ["if", "ct"])])

        def dve_in0(dve):
            v = nc.vector
            v.memset(ua[:, :, 0:1], 0.0).then_inc(s_zc, 1)
            dve.wait_ge(s_zc, 1)
            dve.wait_ge(s_vec, 16)
            with dve.Fori(0, NA // 2) as i:
                for s in range(2):
                    t = 2 * i + s
                    dve.wait_ge(s_tile, t + 1)
                    v.tensor_tensor(two(ua[:, ds(t, 1), 1:].squeeze(1)), bank(s), two(rb), ALU.mult).then_inc(s_bank, 1)
                    dve.wait_ge(s_bank, t + 3)
                    dve.wait_ge(s_shf, t + 1)
                    v.tensor_tensor(tmp[0][:, 0:TP], ua[:, ds(t, 1), 0:TP].squeeze(1),
                                    ua[:, ds(t, 1), 1:TP + 1].squeeze(1), ALU.subtract)
                    v.tensor_tensor(tmp[0][:, TP:], vec[:, ds(VEC["shift"][0] + NS * t, NS)],
                                    ua[:, ds(t, 1), TP + 1:].squeeze(1), ALU.subtract).then_inc(s_sub, 1)
                    dve.wait_ge(s_sub, t + 1)
                    dve.wait_ge(s_raw, t + 1)
                    v.scalar_tensor_tensor(ua[:, ds(t, 1), 1:].squeeze(1), tmp[0], vec[:, ds(VEC["mu"][0] + t, 1)],
                                           ua[:, ds(t, 1), 1:].squeeze(1), ALU.mult, ALU.add).then_inc(s_shf, 1)
            with dve.Fori(0, 4) as i:
                for s in range(2):
                    t = 2 * i + s
                    u = lambda a, b: ub[:, ds(t, 1), a:b].squeeze(1)
                    dve.wait_ge(s_tile, t + NA + 1)
                    v.tensor_tensor(two(u(0, T)), bank(s), two(rb), ALU.mult).then_inc(s_bank, 1)
                    dve.wait_ge(s_bank, t + NA + 3)
                    dve.wait_ge(s_cvd, t + 1)
                    w = lambda j: vec[:, ds(VEC["cw"][0] + 8 * j + t, 1)]
                    o = acc[s]
                    v.tensor_scalar(o, u(0, T), w(3), vec[:, ds(VEC["cb"][0] + t, 1)], ALU.mult,
                                    ALU.add).then_inc(s_cv, 1)
                    for k in range(1, 4):
                        dve.wait_ge(s_cv, 4 * t + k)
                        v.scalar_tensor_tensor(o[:, TP:], vec[:, ds(VEC["conv"][0] + 24 * t + 8 * (3 - k), 8)],
                                               w(3 - k), o[:, TP:], ALU.mult, ALU.add)
                        v.scalar_tensor_tensor(o[:, k:TP], u(0, TP - k), w(3 - k), o[:, k:TP],
                                               ALU.mult, ALU.add).then_inc(s_cv, 1)
            with dve.Fori(0, 4) as i:
                for s in range(2):
                    t = 2 * i + s
                    dve.wait_ge(s_tile, t + NA + 8 + 1)
                    v.tensor_tensor(two(ub[:, ds(t + 8, 1), :].squeeze(1)), bank(s), two(rb),
                                    ALU.mult).then_inc(s_bank, 1)
            def after(steps, name):
                dve.wait_ge(*steps.at(name))
            ir, fr, er, zr = hbuf[0][0:4, 1024:1024 + T], hbuf[0][0:4, 2048:2048 + T], hbuf[0][0:4, 3072:3072 + T], \
                hbuf[0][0:4, 3600:3600 + TP]
            cr, nr, tr = crow[0:4], nmrow[0:4], nmtrow[0:4]
            after(row_p, "if")
            v.tensor_tensor(two(ir), ps[0:4, 6:8, 0:HALF], two(rb[0:4]), ALU.mult).then_inc(*row_d.step("i"))
            after(row_d, "i")
            v.tensor_scalar(ir, ir, V("ib")[0:4], None, ALU.add).then_inc(*row_d.step("ib"))
            v.tensor_tensor(two(fr), ps[32:36, 6:8, 0:HALF], two(rb[32:36]), ALU.mult).then_inc(*row_d.step("f"))
            after(row_d, "f")
            v.tensor_scalar(fr, fr, V("fb")[0:4], None, ALU.add).then_inc(*row_d.step("fb"))
            after(row_d, "fb")
            v.scalar_tensor_tensor(er, fr, -1.0, fr, ALU.mult, ALU.max).then_inc(*row_d.step("abs"))
            after(row_a, "ln")
            v.scalar_tensor_tensor(fr, fr, 0.0, er, ALU.min, ALU.subtract).then_inc(*row_d.step("lf"))
            v.memset(zr, 0.0).then_inc(*row_d.step("zero"))
            after(row_d, "zero")
            v.tensor_tensor_scan(er[:, 0:TP], fr[:, 0:TP], zr, 0.0, ALU.add, ALU.add).then_inc(*row_d.step("b"))
            after(row_d, "b")
            v.tensor_tensor(cr[:, 0:TP], ir[:, 0:TP], er[:, 0:TP], ALU.subtract).then_inc(*row_d.step("c"))
            after(row_d, "c")
            v.tensor_tensor_scan(tr[:, 0:TP], cr[:, 0:TP], cr[:, 0:TP], 0.0, ALU.max,
                                 ALU.max).then_inc(*row_d.step("m"))
            after(row_d, "m")
            v.tensor_scalar(nr[:, 0:TP], tr[:, 0:TP], -1.0, None, ALU.mult).then_inc(*row_d.step("nm"))
            v.scalar_tensor_tensor(tr[:, 0:TP], er[:, 0:TP], -1.0, tr[:, 0:TP], ALU.mult,
                                   ALU.subtract).then_inc(*row_d.step("nmt"))
            after(row_d, "nmt")
            v.tensor_scalar(mo[0:4, 0:1], tr[:, TP - 1:TP], -1.0, None, ALU.mult).then_inc(*row_d.step("mo"))
            t_, m_ = zr[:, 0:NS], mo[0:4, 1:]
            v.tensor_tensor(t_, fr[:, TP:], V("m", 0, NS)[0:4], ALU.add).then_inc(*row_d.step("t"))
            after(row_d, "t")
            v.tensor_tensor(m_, t_, ir[:, TP:], ALU.max).then_inc(*row_d.step("tm"))
            after(row_d, "tm")
            v.tensor_tensor(sr[0:4, 0:8], t_, m_, ALU.subtract).then_inc(*row_d.step("iw"))
            v.tensor_tensor(sr[0:4, 8:16], ir[:, TP:], m_, ALU.subtract).then_inc(*row_d.step("wi"))
            v.tensor_scalar(sr[0:4, 16:24], m_, -1.0, None, ALU.mult).then_inc(*row_d.step("en"))
            after(row_d, "en")
            after(row_p, "ct")
            v.tensor_copy(ct, ps[:, 4, 0:16]).then_inc(*row_d.step("ct"))
            after(row_d, "ct")

        def pool_in0(pool):
            with pool.Fori(0, NA // 2) as i:
                for s in range(2):
                    t = 2 * i + s
                    pool.wait_ge(s_bank, t + 3)
                    nc.gpsimd.tensor_copy(sho[:, ds(t, 1), :].squeeze(1),
                                          ua[:, ds(t, 1), TP:].squeeze(1)).then_inc(s_raw, 1)
            with pool.Fori(0, 4) as i:
                for s in range(2):
                    t = 2 * i + s
                    pool.wait_ge(s_bank, t + NA + 3)
                    nc.gpsimd.tensor_copy(cvo[:, ds(t, 1), :].squeeze(1),
                                          ub[:, ds(t, 1), TP - 3:].squeeze(1)).then_inc(s_raw, 1)

        def act_in0(act):
            a = nc.scalar
            act.wait_ge(s_shf, NA + 1)
            a.activation(ua[0:64, 12, 1:], ua[0:64, 12, 1:], ACT.Tanh).then_inc(s_tn, 1)
            a.activation(ua[:, 13, 1:], ua[:, 13, 1:], ACT.Sigmoid).then_inc(s_tn, 1)
            with act.Fori(0, 4) as i:
                for s in range(2):
                    t = 2 * i + s
                    act.wait_ge(s_cv, 4 * t + 4)
                    act.wait_ge(s_raw, t + 15)
                    a.activation(ub[:, ds(t, 1), :].squeeze(1), acc[s], ACT.Silu).then_inc(s_cvd, 1)
            er = hbuf[0][0:4, 3072:3072 + T]
            act.wait_ge(s_bank, NA + NB + 2)
            a.activation(ub[:, 12:16, :], ub[:, 12:16, :], ACT.Sigmoid).then_inc(*row_a.step("gate"))
            for k in range(12):
                act.wait_ge(s_lp, k + 1)
                src = ps[:, 4 + 2 * (k % 2):6 + 2 * (k % 2), 0:HALF]
                j = k % 4
                if k < 4:
                    a.activation(two(sig[:, j, :]), src, ACT.Sigmoid, bias=V("w0", j)).then_inc(s_lc, 1)
                elif k < 8:
                    a.activation(two(aa[:, j, :]), src, ACT.Sigmoid, bias=V("a0", j)).then_inc(s_lc, 1)
                else:
                    a.activation(two(gg[:, j, :]), src, ACT.Copy).then_inc(s_lc, 1)
            act.wait_ge(*row_d.at("abs"))
            a.activation(er, er, ACT.Exp, scale=-1.0).then_inc(*row_a.step("exp"))
            act.wait_ge(*row_a.at("exp"))
            a.activation(er, er, ACT.Ln, bias=1.0).then_inc(*row_a.step("ln"))

        def pe_in0(pe):
            for kt in range(KD):
                for hf in range(2):
                    mm = pe.matmul(ps[0:36, 6 + hf, 0:HALF], V("wif", 36 * kt, 36), xg[:, kt, hf * HALF:(hf + 1) * HALF],
                                   start=(kt == 0), stop=(kt == KD - 1))
            mm.then_inc(*row_p.step("if"))
            pe.wait_ge(s_tn, 2)
            for k in range(12):
                j = k % 4
                if k == 0:
                    pe.wait_ge(s_rt, 1)
                if k == 1:
                    pe.wait_ge(*row_d.at("f"))
                if k >= 2:
                    pe.wait_ge(s_lc, k - 1)
                w = (V("w2a2", j * P, P)[0:64] if k < 4 else V("w2a2", j * P, P)[64:P] if k < 8 else V("g2", j * P, P))
                for hf in range(2):
                    cols = slice(1 + hf * HALF, 1 + hf * HALF + HALF)
                    x = ua[0:64, 12, cols] if k < 4 else ua[64:P, 12, cols] if k < 8 else ua[:, 13, cols]
                    mm = pe.matmul(ps[:, 4 + 2 * (k % 2) + hf, 0:HALF], w, x, start=True, stop=True)
                mm.then_inc(s_lp, 1)
            pe.wait_ge(s_lc, 11)
            pe.wait_ge(*row_d.at("c"))
            for g in range(NG):
                mm = pe.transpose(ps[:, 4, 4 * g:4 * g + 4], crow[0:4, g * P:(g + 1) * P], C("ident")[0:4, 0:4])
            mm.then_inc(*row_p.step("ct"))
            pe.wait_ge(s_lc, 12)

        h1 = hb[1]
        r4_ = Space([hbuf[0][:, :], pjw[:, :], free[:, :], slot[1][:, :]])
        rS = r4_.take(4, 2, CDV)
        vrow = [r4_.take(CDV) for _ in range(4)]
        krow, km = r4_.take(4, 2 * P), [r4_.take(2 * P) for _ in range(2)]
        kR, QD = r4_.take(2, P), r4_.take(2, P)
        vR, YC, YQ, YB = [r4_.take(4, P) for _ in range(4)]
        kTk, vTk = r4_.take(2 * P), r4_.take(CDV)
        PR, RI = r4_.take(P), r4_.take(P)
        ys1, yc1, yq1 = [r4_.take(16, NS) for _ in range(3)]
        ri1 = r4_.take(4, NS)
        ring = [r4_.take(2, CDV) for _ in range(4)]
        s_rin = [sem(f"ret_state_loaded{i}") for i in range(4)]
        s_prs = sem("prompt_ret_stored")
        s_up, s_read = sem("sample_ret_updated"), sem("sample_ret_read")
        rp_x, s_rope, s_pair = [tmp[0], tmp[1], sqr[0], sqr[1]], sem("rope_step"), sem("rope_pair")
        def by_head(names, last):
            heads = [f"{n[1:]}{h - 1}" if n[0] == "-" else f"{n}{h}"
                     for h in range(CH) for n in names if h or n[0] != "-"]
            return heads + [f"{n}{CH - 1}" for n in last]
        re = part("ret", dict(
            pe=by_head(["sc", "vr", "outer0", "-mean", "o", "-var", "st", "outer1"], ["mean", "var"]),
            dve=by_head(["km0", "km1", "kt", "pt", "qd", "-yc", "-ri", "-yn", "-out", "s"],
                        ["yc", "ri", "yn", "out"]),
            act=by_head(["k", "v", "vt", "-ysq", "y", "-sd"], ["ysq", "sd"])))
        ep, ed, ea = re["pe"], re["dve"], re["act"]
        s_rz = sem("ret_zeroed")
        e1 = {k: sem(f"ret1_{k}") for k in ("pe", "dve", "act")}
        ep1 = Steps(e1["pe"], ["krows", "vrows"])
        ep2 = Steps(e1["pe"], ["mean", "var"], 2)
        ed2 = Steps(e1["dve"], ["yc", "ri", "yn", "out"])
        ea1 = Steps(e1["act"], ["krows", "vrows", "y", "ysq", "sd"])

        def dve_qkv(dve):
            v = nc.vector
            with dve.Fori(0, 8) as i:
                x1, x2, p1, p2 = rp_x
                t = GEMMS["qkv"][1]
                dve.wait_ge(s_tile, (t + 1) + 2 * i)
                dve.wait_ge(s_rope, 8 * i + 1)
                v.tensor_tensor(two(x1), bank(0), two(rb), ALU.mult).then_inc(s_bank, 1)
                dve.wait_ge(s_tile, (t + 2) + 2 * i)
                v.tensor_tensor(two(x2), bank(1), two(rb), ALU.mult).then_inc(s_bank, 1)
                dve.wait_ge(s_bank, (t + 4) + 2 * i)
                y = lambda k: hid[:, ds(2 * i + k, 1), :].squeeze(1)
                v.tensor_tensor(p1, x1, C("cos"), ALU.mult).then_inc(s_rope, 1)
                v.tensor_tensor(p2, x2, C("sin"), ALU.mult).then_inc(s_rope, 1)
                dve.wait_ge(s_rope, 8 * i + 3)
                v.tensor_tensor(y(0), p1, p2, ALU.subtract).then_inc(s_rope, 1)
                dve.wait_ge(s_rope, 8 * i + 4)
                v.tensor_tensor(p1, x1, C("sin"), ALU.mult).then_inc(s_rope, 1)
                v.tensor_tensor(p2, x2, C("cos"), ALU.mult).then_inc(s_rope, 1)
                dve.wait_ge(s_rope, 8 * i + 6)
                v.tensor_tensor(y(1), p1, p2, ALU.add).then_inc(s_rope, 1)
                dve.wait_ge(s_rope, 8 * i + 7)
                v.memset(PR[:, 0:1], 0.0).then_inc(s_rope, 2)
            with dve.Fori(0, 8) as i:
                for s in range(2):
                    dve.wait_ge(s_tile, (GEMMS["qkv"][1] + 17 + s) + 2 * i)
                    v.tensor_tensor(two(hid[:, ds(2 * i + 16 + s, 1), :].squeeze(1)), bank(s), two(rb),
                                    ALU.mult).then_inc(s_bank, 1)
            v.memset(rS, 0.0).then_inc(s_rz, 1)
            dve.wait_ge(s_rz, 1)

        def hg(tile, n, g):
            return hid[:, tile:tile + n, ds(L * g, L)]

        def dve_ret(dve):
            v = nc.vector
            with dve.Fori(0, NG) as g:
                def after(steps, name):
                    dve.wait_ge(*steps.at(name, g))

                def sample(h, n):
                    x = 2 * (h % 2) + n
                    after(ep, f"outer{n}{h}")
                    dve.wait_ge(s_rin[x], (16 * (h // 2) + 16) + 32 * g)
                    v.scalar_tensor_tensor(ring[x], ring[x], CDEC_ONE[h], ps[:, 6:8, :], ALU.mult,
                                           ALU.add).then_inc(s_up, 1)

                def center(h):
                    after(ep, f"mean{h}")
                    v.tensor_tensor(YC, YB, mid(ps[:, 4, 0:P], 4), ALU.subtract).then_inc(*ed.step(f"yc{h}"))

                def scale(h):
                    after(ea, f"sd{h}")
                    v.reciprocal(RI, RI).then_inc(*ed.step(f"ri{h}"))
                    after(ed, f"ri{h}")
                    v.tensor_tensor(YC, YC, mid(RI, 4), ALU.mult).then_inc(*ed.step(f"yn{h}"))
                    after(ed, f"yn{h}")
                    v.tensor_tensor(hg(16 + 4 * h, 4, g), YC, bc(V("rgn", 4 * h, 4), P),
                                    ALU.mult).then_inc(*ed.step(f"out{h}"))

                for h in range(CH):
                    if h == 0:
                        dve.wait_ge(*ea1.at("krows"))
                    for n in range(2):
                        v.tensor_scalar(km[n][0:NS], krow[0:NS, h, :], con[0:NS, ds(CON["ident"][0] + n + 2 * g, 1)],
                                        None, ALU.mult).then_inc(*ed.step(f"km{n}{h}"))
                    after(ep, f"sc{h}")
                    v.tensor_scalar(kTk, ps[:, 0, 0:256], C("kdec", h, 1), None, ALU.mult).then_inc(*ed.step(f"kt{h}"))
                    v.tensor_tensor(PR, ps[:, 0, 256:384], C("rmask", h * P, P), ALU.mult).then_inc(*ed.step(f"pt{h}"))
                    v.tensor_tensor(QD, hg(2 * h, 2, g), mid(C("qdec", h * P, P), 2),
                                    ALU.mult).then_inc(*ed.step(f"qd{h}"))
                    if h:
                        center(h - 1)
                    sample(h, 0)
                    if h:
                        scale(h - 1)
                    after(ep, f"st{h}")
                    v.scalar_tensor_tensor(rS[:, h], rS[:, h], CDEC_CHUNK[h], ps[:, 4:6, :], ALU.mult,
                                           ALU.add).then_inc(*ed.step(f"s{h}"))
                    sample(h, 1)
                center(CH - 1)
                scale(CH - 1)

        def act_ret(act):
            a = nc.scalar
            act.wait_ge(s_bank, GEMMS["qkv"][1] + 34)
            act.wait_ge(s_rope, 65)
            act.wait_ge(*ep1.at("krows"))
            a.activation(krow[0:NS].rearrange("p h n -> p (h n)").rearrange("p (b n) -> p b n", b=2), ps[0:NS, 0:2, :],
                         ACT.Copy, scale=CDK ** -0.5).then_inc(*ea1.step("krows"))
            act.wait_ge(*ep1.at("vrows"))
            for k in range(3):
                a.activation(vrow[k][0:NS], ps[0:NS, 2 + k, :], ACT.Copy)
            a.activation(vrow[3][0:NS], ps[0:NS, 5, :], ACT.Copy).then_inc(*ea1.step("vrows"))
            with act.Fori(0, NG) as g:
                def after(steps, name):
                    act.wait_ge(*steps.at(name, g))

                def square(h):
                    after(ed, f"yc{h}")
                    a.activation(YQ, YC, ACT.Square).then_inc(*ea.step(f"ysq{h}"))

                def deviation(h):
                    after(ep, f"var{h}")
                    a.activation(RI, ps[:, 1, 0:P], ACT.Sqrt, bias=GN_EPS).then_inc(*ea.step(f"sd{h}"))

                for h in range(CH):
                    a.activation(kR, hg(8 + 2 * h, 2, g), ACT.Copy, scale=CDK ** -0.5).then_inc(*ea.step(f"k{h}"))
                    a.activation(vR, hg(16 + 4 * h, 4, g), ACT.Copy).then_inc(*ea.step(f"v{h}"))
                    after(ep, f"vr{h}")
                    a.activation(vTk, ps[:, 1, :], ACT.Copy).then_inc(*ea.step(f"vt{h}"))
                    if h:
                        square(h - 1)
                    after(ep, f"o{h}")
                    a.activation(YB, bk(3), ACT.Copy).then_inc(*ea.step(f"y{h}"))
                    if h:
                        deviation(h - 1)
                square(CH - 1)
                deviation(CH - 1)

        def pe_ret(pe):
            pe.wait_ge(s_bank, GEMMS["qkv"][1] + 34)
            pe.wait_ge(s_rope, 65)
            for k in range(8):
                mm = pe.transpose(ps[0:NS, k // 4, (k % 4) * P:(k % 4 + 1) * P], hid[:, 8 + k, TP:], C("ident"))
            mm.then_inc(*ep1.step("krows"))
            for e in range(16):
                mm = pe.transpose(ps[0:NS, 2 + e // 4, (e % 4) * P:(e % 4 + 1) * P], hid[:, 16 + e, TP:], C("ident"))
            mm.then_inc(*ep1.step("vrows"))
            pe.wait_ge(s_rz, 1)
            pe.wait_ge(*ea1.at("vrows"))
            with pe.Fori(0, NG) as g:
                def after(steps, name):
                    pe.wait_ge(*steps.at(name, g))

                def outer(h, n):
                    for k in range(2):
                        mm = pe.matmul(ps[:, 6 + k, :], km[n][0:NS, k * P:(k + 1) * P], vrow[h][0:NS],
                                       start=True, stop=True)
                    mm.then_inc(*ep.step(f"outer{n}{h}"))

                def o_product(h, n):
                    pe.wait_ge(s_up, (2 * h + n + 1) + 8 * g)
                    for e in range(4):
                        for k in range(2):
                            mm = pe.matmul(ps[:, 2, ds((4 * NS * h + NS * e + n) + 2 * g, 1)],
                                           ring[2 * (h % 2) + n][:, k, e * P:(e + 1) * P],
                                           hid[:, 2 * h + k, ds((TP + n) + 2 * g, 1)],
                                           start=(k == 0), stop=(k == 1), skip_group_check=True)
                    mm.then_inc(s_read, 1)

                def mean(h):
                    after(ea, f"y{h}")
                    for e in range(4):
                        mm = pe.matmul(ps[:, 4, 0:P], C("mean512"), YB[:, e, :], start=(e == 0), stop=(e == 3))
                    mm.then_inc(*ep.step(f"mean{h}"))

                def var(h):
                    after(ea, f"ysq{h}")
                    for e in range(4):
                        mm = pe.matmul(ps[:, 1, 0:P], C("mean512"), YQ[:, e, :], start=(e == 0), stop=(e == 3))
                    mm.then_inc(*ep.step(f"var{h}"))

                for h in range(CH):
                    after(ea, f"k{h}")
                    for k in range(2):
                        pe.transpose(ps[:, 0, k * P:(k + 1) * P], kR[:, k, :], C("ident"))
                    for k in range(2):
                        mm = pe.matmul(ps[:, 0, 256:384], kR[:, k, :], hid[:, 2 * h + k, ds(L * g, L)],
                                       start=(k == 0), stop=(k == 1))
                    mm.then_inc(*ep.step(f"sc{h}"))
                    after(ea, f"v{h}")
                    for e in range(4):
                        mm = pe.transpose(bk(1)[:, e, :], vR[:, e, :], C("ident"))
                    mm.then_inc(*ep.step(f"vr{h}"))
                    after(ed, f"km1{h}")
                    outer(h, 0)
                    if h:
                        mean(h - 1)
                        o_product(h - 1, 1)
                    after(ea, f"vt{h}")
                    after(ed, f"qd{h}")
                    for e in range(4):
                        pe.matmul(bk(3)[:, e, :], vTk[:, e * P:(e + 1) * P], PR, start=True, stop=False)
                        for k in range(2):
                            mm = pe.matmul(bk(3)[:, e, :], rS[:, h, k, e * P:(e + 1) * P], QD[:, k, :],
                                           start=False, stop=(k == 1))
                    mm.then_inc(*ep.step(f"o{h}"))
                    if h:
                        var(h - 1)
                    o_product(h, 0)
                    for k in range(2):
                        mm = pe.matmul(ps[:, 4 + k, :], kTk[:, k * P:(k + 1) * P], vTk, start=True, stop=True)
                    mm.then_inc(*ep.step(f"st{h}"))
                    outer(h, 1)
                o_product(CH - 1, 1)
                mean(CH - 1)
                var(CH - 1)

        def dve_ret1(dve):
            v = nc.vector

            def after(steps, name):
                dve.wait_ge(*steps.at(name))
            after(ep2, "mean")
            four = lambda x: x.rearrange("p (h e) s -> p h e s", h=4)
            b4 = lambda x: x.unsqueeze(2).to_broadcast([P, 4, 4, NS])
            mean = ps[:, 4, 0:32].rearrange("p (h s) -> p h s", h=4)
            v.tensor_tensor(four(yc1), four(ys1), b4(mean), ALU.subtract).then_inc(*ed2.step("yc"))
            after(ea1, "sd")
            v.reciprocal(ri1, ri1).then_inc(*ed2.step("ri"))
            after(ed2, "ri")
            v.tensor_tensor(four(yc1), four(yc1), b4(ri1), ALU.mult).then_inc(*ed2.step("yn"))
            after(ed2, "yn")
            v.tensor_tensor(hid[:, 16:32, TP:], yc1, bc(V("rgn", 0, 16), NS), ALU.mult).then_inc(*ed2.step("out"))
            after(ed2, "out")

        def act_ret1(act):
            a = nc.scalar
            act.wait_ge(*ep.at("var3", NG - 1))
            a.activation(ys1, ps[:, 2, 0:P].rearrange("p (k s) -> p k s", s=NS), ACT.Copy).then_inc(*ea1.step("y"))
            act.wait_ge(*ed2.at("yc"))
            a.activation(yq1, yc1, ACT.Square).then_inc(*ea1.step("ysq"))
            act.wait_ge(*ep2.at("var"))
            a.activation(ri1, ps[:, 5, 0:32].rearrange("p (h s) -> p h s", h=4), ACT.Sqrt,
                         bias=GN_EPS).then_inc(*ea1.step("sd"))

        def pe_ret1(pe):
            pe.wait_ge(*ea1.at("y"))
            for h in range(4):
                for e in range(4):
                    mm = pe.matmul(ps[:, 4, NS * h:NS * h + NS], C("mean512"), ys1[:, 4 * h + e, :],
                                   start=(e == 0), stop=(e == 3))
            mm.then_inc(*ep2.step("mean"))
            pe.wait_ge(*ea1.at("ysq"))
            for h in range(4):
                for e in range(4):
                    mm = pe.matmul(ps[:, 5, NS * h:NS * h + NS], C("mean512"), yq1[:, 4 * h + e, :],
                                   start=(e == 0), stop=(e == 3))
            mm.then_inc(*ep2.step("var"))

        def dve_up(dve, lyr):
            _, t0, _, _, _ = GEMMS[f"up{lyr}"]
            with dve.Fori(0, KF // 2) as i:
                for s in range(2):
                    dve.wait_ge(s_tile, (t0 + s + 1) + 2 * i)
                    dve.wait_ge(s_hid, (KF * lyr + s + 1) + 2 * i)
                    nc.vector.scalar_tensor_tensor(two(tmp[s]), bank(s), 0.0, two(rb), ALU.max,
                                                   ALU.mult).then_inc(s_bank, 1)

        def act_up(act, lyr):
            _, t0, _, _, _ = GEMMS[f"up{lyr}"]
            with act.Fori(0, KF // 2) as i:
                for s in range(2):
                    act.wait_ge(s_bank, (t0 + s + 3) + 2 * i)
                    nc.scalar.activation(hid[:, ds(2 * i + s, 1), :].squeeze(1), tmp[s],
                                         ACT.Square).then_inc(s_hid, 1)

        def pe_proj(pe, lyr):
            pe.wait_ge(s_pj_w, 16 * (lyr + 1))
            pe.wait_ge(s_pt, 16 * (lyr + 1))
            pe.wait_ge(s_rt, 4 * lyr + 4)
            for mt in range(KD):
                if mt >= 2:
                    pe.wait_ge(s_pjc, 8 * lyr + mt - 1)
                for kt in range(KP):
                    for hf in range(2):
                        at = (mt * KP + kt) * P
                        mm = pe.matmul(ps[:, 4 + 2 * (mt % 2) + hf, 0:HALF], pjw[:, at:at + P],
                                       pt[:, kt, hf * HALF:(hf + 1) * HALF], start=(kt == 0), stop=(kt == KP - 1))
                mm.then_inc(s_pj, 1)

        def act_ple(act, lyr, hn, more):
            a = nc.scalar
            for mt in range(KD):
                act.wait_ge(s_pj, 8 * lyr + mt + 1)
                p4 = 4 + 2 * (mt % 2)
                a.activation(two(hid[:, mt, :]), ps[:, p4:p4 + 2, 0:HALF], ACT.Copy).then_inc(s_pjc, 1)
            for mt in range(KD + 1):
                if mt < KD:
                    act.wait_ge(s_tile, tile_at(f"gate{lyr}", mt))
                    if mt >= 2:
                        act.wait_ge(s_hn, 8 * lyr + mt - 1)
                    a.activation(two(sqr[mt % 2]), bank(mt % 2), ACT.Exp, scale=-1.0).then_inc(s_bank, 1)
                if mt and more:
                    kt = mt - 1
                    act.wait_ge(s_hn, 8 * lyr + mt)
                    a.activation(xg[:, kt, :], hn[:, kt, :], ACT.Copy, scale=V("norm_g", 32 + kt))
                    a.activation(hid[:, 24 + kt, :], hn[:, kt, :], ACT.Square).then_inc(s_xg, 1)

        def dve_ple(dve, lyr, h, hn):
            v = nc.vector
            _, t0, _, _, _ = GEMMS[f"gate{lyr}"]
            for mt in range(KD):
                e = sqr[mt % 2]
                n = 24 * lyr + 3 * mt
                dve.wait_ge(s_bank, t0 + mt + 3)
                v.tensor_scalar(e, e, 1.0, None, ALU.add).then_inc(s_pl, 1)
                dve.wait_ge(s_pl, n + 1)
                v.reciprocal(e, e).then_inc(s_pl, 1)
                dve.wait_ge(s_pl, n + 2)
                dve.wait_ge(s_pjc, 8 * lyr + mt + 1)
                v.tensor_tensor(e, e, hid[:, mt, :], ALU.mult).then_inc(s_pl, 1)
                dve.wait_ge(s_pl, n + 3)
                v.tensor_tensor(hn[:, mt, :], h[:, mt, :], e, ALU.add).then_inc(s_hn, 1)

        def dve_gate_g(dve):
            v = nc.vector
            t0 = GEMMS["g"][1]
            with dve.Fori(0, 8) as i:
                for s in range(2):
                    dve.wait_ge(s_tile, (t0 + s + 1) + 2 * i)
                    v.tensor_tensor(two(tmp[s]), bank(s), two(rb), ALU.mult).then_inc(s_bank, 1)
                    dve.wait_ge(s_silu, (s + 1) + 2 * i)
                    y = hid[:, ds(2 * i + 16 + s, 1), :].squeeze(1)
                    v.tensor_tensor(y, y, tmp[s], ALU.mult).then_inc(s_yg, 1)

        def act_gate_g(act):
            t0 = GEMMS["g"][1]
            with act.Fori(0, 8) as i:
                for s in range(2):
                    act.wait_ge(s_bank, (t0 + s + 3) + 2 * i)
                    nc.scalar.activation(tmp[s], tmp[s], ACT.Silu).then_inc(s_silu, 1)
        s_silu, s_yg = sem("gate_silu"), sem("gated")
        s_x2, s_st1 = sem("x_reloaded"), sem("rwkv_sample_state_stored")
        s_ro = [sem(f"ret_state_stored{i}") for i in range(4)]

        block = ctx.enter_context(nc.Block())
        cols = lambda hf, off=0: slice(off + hf * HALF, off + (hf + 1) * HALF)

        @block.sync
        def _(sp):
            sp.dma_start(vec[:, :], dram["vec"]).then_inc(s_vec, 16)
            sp.dma_start(hbuf[0][:, :], dram["x"]).then_inc(s_x, 16)
            sp.dma_start(con[:, :], dram["con"]).then_inc(s_con, 16)

            def slabs(name, first=0, last=None, prev=None):
                slab0, tile0, n, ntiles, per = GEMMS[name]
                last = n // 2 if last is None else last
                if first == 0:
                    for s in range(2):
                        if prev:
                            _, pt0, pn, ptiles, pper = GEMMS[prev]
                            sp.wait_ge(s_tile, pt0 + min(ptiles, (pn - 1 + s) * pper))
                        sp.dma_start(slot[s][:, :], dram["w"][slab0 + s]).then_inc(s_w[s], 16)
                if last > max(first, 1):
                    with sp.Fori(max(first, 1), last) as i:
                        for s in range(2):
                            sp.wait_ge(s_tile, (tile0 + (s + 1) * per - 2 * per) + 2 * per * i)
                            sp.dma_start(slot[s][:, :], dram["w"][slab0 + 2 * i + s]).then_inc(s_w[s], 16)

            slabs("in0")
            sp.wait_ge(s_raw, NA + 8)
            store(sp, dram["sho"], sho.rearrange("p a b -> p (a b)"))
            store(sp, dram["cvo"], cvo.rearrange("p a b -> p (a b)"))
            store(sp, dram["conv_o"], V("conv", 0, 192))
            sp.wait_ge(*row_d.at("tm"))
            store(sp, dram["mo"], mo[0:4])
            for h in range(2):
                sp.wait_ge(*rw[h]["dve"].at("out", NG - 1))
                sp.dma_start(dram["rs_o"][h], s_end[h].rearrange("p a b -> p (a b)")).then_inc(s_rs, 16)
            slabs("out0", prev="in0")
            sp.dma_start(sst.rearrange("p j s n -> p (j s n)"), dram["sst"]).then_inc(s_sst, 16)
            sp.wait_ge(*sdj.at("s", 3))
            sp.dma_start(dram["sst_o"], sst.rearrange("p j s n -> p (j s n)")).then_inc(s_st1, 16)
            sp.wait_ge(*sd2.at("out"))
            sp.dma_start(cst.rearrange("p h s n -> p (h s n)"), dram["cst"]).then_inc(s_cst, 16)
            sp.wait_ge(*md.at("out", NG - 1))
            store(sp, dram["cn_o"], cn.rearrange("p h n -> p (h n)"))
            sp.wait_ge(*nd.at("n"))
            store(sp, dram["n_o"], n_new.rearrange("p h n -> p (h n)"))
            sp.wait_ge(*ndj.at("c", 3))
            store(sp, dram["cst_o"], cst.rearrange("p h s n -> p (h s n)"))
            sp.wait_ge(*nd2.at("out"))
            assert outs[0] == MIXER_STORES
            sp.wait_ge(s_out, MIXER_STORES)
            sp.wait_ge(s_rs, 32)
            sp.dma_start(hbuf[0][:, :], dram["x"]).then_inc(s_x2, 16)
            sp.dma_start(pjw[:, :], dram["pjw"][0]).then_inc(s_pj_w, 16)
            sp.dma_start(pt.rearrange("p k t -> p (k t)"), dram["pt"][0]).then_inc(s_pt, 16)
            slabs("up0", prev="out0")
            slabs("down0", prev="up0")
            slabs("gate0", prev="down0")
            slabs("qkv", prev="gate0")
            g0, qt = GEMMS["g"][0], GEMMS["qkv"][1] + GEMMS["qkv"][3]
            sp.wait_ge(s_tile, qt - 4)
            sp.dma_start(slot[0][:, :], dram["w"][g0]).then_inc(s_w[0], 16)
            sp.wait_ge(s_tile, qt)

            def ret_load(it, s):
                sp.dma_start(ring[s].rearrange("p k n -> p (k n)"), dram["rst"][it]).then_inc(s_rin[s], 16)

            def ret_store(it, s):
                sp.wait_ge(s_up, it + 1)
                sp.dma_start(dram["rst_o"][it], ring[s].rearrange("p k n -> p (k n)")).then_inc(s_ro[s], 16)
            for s in range(4):
                ret_load(s, s)
            ret_store(0, 0)
            ret_store(1, 1)
            with sp.Fori(0, 7) as i:
                for s in range(4):
                    ret_store(4 * i + (2 + s), (2 + s) % 4)
                    sp.wait_ge(s_read, 4 * i + (s + 1))
                    sp.wait_ge(s_ro[s], 16 * i + 16)
                    ret_load(4 * i + (4 + s), s)
            ret_store(30, 2)
            ret_store(31, 3)
            for s in range(4):
                sp.wait_ge(s_ro[s], 128)
            sp.wait_ge(s_read, 32)
            sp.dma_start(slot[1][:, :], dram["w"][g0 + 1]).then_inc(s_w[1], 16)
            sp.wait_ge(*ed.at("out3", NG - 1))
            sp.dma_start(dram["rS_o"], rS.rearrange("p h k n -> p (h k n)")).then_inc(s_prs, 16)
            slabs("g", 1)
            slabs("out1", prev="g")
            sp.wait_ge(*ea1.at("sd"))
            sp.wait_ge(*ed2.at("out"))
            sp.dma_start(pjw[:, :], dram["pjw"][1]).then_inc(s_pj_w, 16)
            sp.wait_ge(s_pj, 8)
            sp.dma_start(pt.rearrange("p k t -> p (k t)"), dram["pt"][1]).then_inc(s_pt, 16)
            slabs("up1", prev="out1")
            slabs("down1", prev="up1")
            slabs("gate1", prev="down1")
            for mt in range(KD):
                sp.wait_ge(s_hn, 8 + mt + 1)
                store(sp, dram["y"][:, mt * T:(mt + 1) * T], hb[0][:, mt, :])
            sp.wait_ge(s_out, outs[0])
            sp.wait_ge(s_rs, 32)
            sp.wait_ge(s_st1, 16)
            sp.wait_ge(s_prs, 16)
            for s in range(4):
                sp.wait_ge(s_ro[s], 128)

        @block.tensor
        def _(pe):
            stream = lambda t: (lambda kt, hf: t[:, kt, cols(hf)])
            pe.wait_ge(s_con, 16)
            pe.wait_ge(s_vec, 16)
            pe_prenorm(pe, 0)
            gemm(pe, "in0", KD, stream(xg))
            pe_in0(pe)
            pe_rwkv(pe)
            pe_rwkv1(pe)
            pe_mlstm(pe)
            pe_mlstm1(pe)
            pe.wait_ge(*nd2.at("out"))
            gemm(pe, "out0", KD, lambda kt, hf: ua[:, kt, cols(hf, 1)] if kt < 4 else ub[:, kt - 4, cols(hf)])
            pe_postnorm(pe, 0)
            pe_prenorm(pe, 1)
            gemm(pe, "up0", KD, stream(xg))
            gemm(pe, "down0", KF, stream(hid), lambda kt: (s_hid, kt + 3))
            pe_postnorm(pe, 1)
            pe_proj(pe, 0)
            gemm(pe, "gate0", KD, stream(hb[0]), lambda kt: (s_h, 8 + kt + 1))
            pe_prenorm(pe, 2)
            gemm(pe, "qkv", KD, stream(xg))
            pe_ret(pe)
            pe_ret1(pe)
            gemm(pe, "g", KD, stream(xg))
            gemm(pe, "out1", 16, lambda kt, hf: hid[:, 16 + kt, cols(hf)], lambda kt: (s_yg, kt + 1))
            pe_postnorm(pe, 2)
            pe_prenorm(pe, 3)
            gemm(pe, "up1", KD, stream(xg))
            gemm(pe, "down1", KF, stream(hid), lambda kt: (s_hid, KF + kt + 3))
            pe_postnorm(pe, 3)
            pe_proj(pe, 1)
            gemm(pe, "gate1", KD, stream(hb[1]), lambda kt: (s_h, 24 + kt + 1))

        @block.scalar
        def _(act):
            act.wait_ge(s_vec, 16)
            act_prenorm(act, 0, hb[0], 0, lambda kt: (s_x, 16))
            act_rms(act, 0)
            act_in0(act)
            act_rwkv(act)
            act_rwkv1(act)
            act.wait_ge(s_st1, 16)
            act_mlstm(act)
            act_mlstm1(act)
            act.wait_ge(s_out, MIXER_STORES)
            act_outproj(act, "out0", 0, hb[1])
            act_rms(act, 1)
            act_prenorm(act, 1, hb[0], 2, lambda kt: (s_h, kt + 1))
            act_rms(act, 2)
            act_up(act, 0)
            act_outproj(act, "down0", 1, hb[1])
            act_rms(act, 3)
            act_ple(act, 0, hb[1], True)
            act_rms(act, 4)
            act_ret(act)
            act_ret1(act)
            act_gate_g(act)
            act.wait_ge(s_prs, 16)
            act_outproj(act, "out1", 2, hb[0])
            act_rms(act, 5)
            act_prenorm(act, 3, hb[1], 6, lambda kt: (s_h, 16 + kt + 1))
            act_rms(act, 6)
            act_up(act, 1)
            act_outproj(act, "down1", 3, hb[0])
            act_rms(act, 7)
            act_ple(act, 1, hb[0], False)

        @block.vector
        def _(dve):
            nc.vector.memset(tmp[0][:, 0:1], 0.0).then_inc(s_bank, 2)
            nc.vector.memset(tmp[1][:, 0:1], 0.0).then_inc(s_hid, 2)
            for n, s in enumerate([rw[0]["dve"].sem, rw[1]["dve"].sem, md.sem, ed.sem, s_shf, s_cvd, s_rope]):
                nc.vector.memset(tmp[0][:, n + 1:n + 2], 0.0).then_inc(s, 1)
            dve_rinv(dve, 0)
            dve_in0(dve)
            dve_rwkv(dve)
            dve_rwkv1(dve)
            dve_mlstm(dve)
            dve_mlstm1(dve)
            dve_rinv(dve, 1)
            dve.wait_ge(s_x2, 16)
            dve_residual(dve, 0, hb[1], hb[0], 1)
            dve_rinv(dve, 2)
            dve_up(dve, 0)
            dve_rinv(dve, 3)
            dve_residual(dve, 1, hb[1], hb[0], 3)
            dve_ple(dve, 0, hb[0], hb[1])
            dve_rinv(dve, 4)
            dve_qkv(dve)
            dve_ret(dve)
            dve_ret1(dve)
            dve_gate_g(dve)
            dve_rinv(dve, 5)
            dve_residual(dve, 2, hb[0], hb[1], 5)
            dve_rinv(dve, 6)
            dve_up(dve, 1)
            dve_rinv(dve, 7)
            dve_residual(dve, 3, hb[0], hb[1], 7)
            dve_ple(dve, 1, hb[1], hb[0])

        @block.gpsimd
        def _(pool):
            pool_in0(pool)
            pool_rwkv(pool)
            for n in range(4):
                pool_sum(pool, n)


INS = {"vec": (P, NVEC), "con": (P, NCON), "x": (P, KD * T), "w": (NSLAB, P, SLAB), "pjw": (2, P, KP * KD * P),
       "pt": (2, P, KP * T), "sst": (P, 4 * NS * 64), "cst": (P, 4 * NS * P), "rst": (32, P, 2 * CDV)}
OUTS = {"y": (P, KD * T), "sho": (P, NA * (NS + 1)), "cvo": (P, 88), "conv_o": (P, 192), "mo": (4, NS + 1),
        "rs_o": (2, P, 2 * P), "sst_o": (P, 4 * NS * 64), "cn_o": (P, BH * 2 * P), "n_o": (P, BH * NS),
        "cst_o": (P, 4 * NS * P), "rS_o": (P, 4 * 2 * CDV), "rst_o": (32, P, 2 * CDV)}


def lay_out(i):
    def fm(v):
        v = np.asarray(v)
        return v.reshape(-1, P).T

    def slabs(w):
        k, n = w.shape
        b = w.reshape(k // P, P, n // P, P).transpose(2, 0, 1, 3).reshape(-1, P, P)
        pad = -len(b) % 32
        b = np.concatenate([b, np.zeros((pad, P, P), b.dtype)]) if pad else b
        return b.reshape(-1, 32, P, P).transpose(0, 2, 1, 3).reshape(-1, P, SLAB)

    f = np.float32
    vec = np.zeros((P, NVEC), f)

    def put(name, a, rows=P):
        at, n = VEC[name]
        vec[:rows, at:at + n] = np.asarray(a).reshape(rows, n)

    put("norm_g", np.concatenate([fm(i["norm_g"][l, k]) for l in range(2) for k in range(4)], 1))
    put("mu", fm(i["rw_mu"][0]))
    for name, key in [("w0", "rw_w0"), ("a0", "rw_a0"), ("kk", "rw_kk"), ("ka", "rw_ka"), ("rk", "rw_rk"),
                      ("rln", "rw_ln"), ("mgn", "ml_gn"), ("cb", "ml_conv_b"), ("rgn", "ret_gn")]:
        put(name, fm(i[key][0]))
    put("cw", np.concatenate([fm(i["ml_conv_w"][0, j]) for j in range(4)], 1))
    put("ib", i["ml_i_bias"][0], 4)
    put("fb", i["ml_f_bias"][0], 4)
    put("m", i["state_mlstm_m"][0].T, 4)
    put("shift", i["state_rwkv_shift"][0].reshape(NS, NA, P).transpose(2, 1, 0))
    put("conv", i["state_mlstm_conv"][0].reshape(NS, 3, 8, P).transpose(3, 2, 1, 0))
    put("n", i["state_mlstm_n"][0].transpose(2, 1, 0))
    w_in = i["mix0_w_in"][0]
    na, nb = NA * P, (NA + NB) * P
    wif = np.zeros((KD, P, 36), f)
    wif[:, :, 0:4] = w_in[:, nb:nb + 4].reshape(KD, P, 4)
    wif[:, :, 32:36] = w_in[:, nb + 4:nb + 8].reshape(KD, P, 4)
    put("wif", wif.transpose(1, 0, 2))
    put("w2a2", np.concatenate([i["rw_w2"][0], i["rw_a2"][0]], 0))
    put("g2", i["rw_g2"][0])
    big = [w_in[:, :nb], i["mix0_w_out"][0], i["ffn_up"][0], i["ffn_down"][0], i["ple_gate"][0],
           i["ret_w_in"][0], i["ret_w_out"][0], i["ffn_up"][1], i["ffn_down"][1], i["ple_gate"][1]]

    def tokens(a, b):
        t = np.concatenate([a[0], b[:, 0]], 0).T
        return t.reshape(-1, P, T).transpose(1, 0, 2).reshape(P, -1)

    return {
        "vec": vec, "con": shape_constants(), "x": tokens(i["x_prompt"], i["x_sample"]),
        "w": np.concatenate([slabs(w) for w in big]),
        "pjw": np.stack([slabs(i["ple_proj"][l])[0][:, :KP * KD * P] for l in range(2)]),
        "pt": np.stack([tokens(i["p_prompt"][l], i["p_sample"][l]) for l in range(2)]),
        "sst": i["state_rwkv_S"][0].reshape(NS, 4, 2, 64, 64).transpose(2, 4, 1, 0, 3).reshape(P, -1),
        "cst": i["state_mlstm_C"][0].transpose(2, 1, 0, 3).reshape(P, -1),
        "rst": i["state_ret_S"][0].reshape(4, 2, 4, 2, P, CDV).transpose(0, 2, 1, 4, 3, 5).reshape(32, P, -1),
    }


def unpack(o):
    y = o["y"].reshape(P, KD, T).transpose(2, 1, 0).reshape(T, D)
    sho = o["sho"].reshape(P, NA, NS + 1).transpose(2, 1, 0).reshape(NS + 1, NA * P)
    cvo = o["cvo"].reshape(P, 8, 11).transpose(2, 1, 0).reshape(11, 8 * P)
    conv = o["conv_o"].reshape(P, 8, 3, NS).transpose(3, 2, 1, 0).reshape(NS, 3, 8 * P)
    rs = o["rs_o"].reshape(2, 2, 64, 2, 2, 64)
    rs = np.stack([rs[:, q, :, :, q, :] for q in range(2)], 3).transpose(0, 2, 3, 4, 1)
    sst = o["sst_o"].reshape(2, 64, 4, NS, 64).transpose(3, 2, 0, 4, 1).reshape(NS, 8, 64, 64)
    cn = o["cn_o"].reshape(P, 4, 2 * P).transpose(1, 0, 2)
    rS = o["rS_o"].reshape(P, 4, 2, CDV).transpose(1, 2, 0, 3).reshape(4, CDK, CDV)
    rst = o["rst_o"].reshape(4, 4, 2, P, 2, CDV).transpose(0, 2, 1, 4, 3, 5).reshape(NS, 4, CDK, CDV)
    c = np.ascontiguousarray
    return (c(y[None, :TP]), c(y[TP:, None]),
            c(sho[None, 0:1]), c(rs.reshape(1, 1, 8, 64, 64)), c(cvo[None, None, 0:3]), c(cn[None, None, :, :, 0:P]),
            c(cn[None, None, :, :, P]), c(o["mo"][:, 0][None, None]), c(rS[None, None]),
            c(sho[None, 1:]), c(sst[None]), c(np.concatenate([conv[:, 1:], cvo[3:, None]], 1)[None]),
            c(o["cst_o"].reshape(P, 4, NS, P).transpose(2, 1, 0, 3)[None]),
            c(o["n_o"].reshape(P, 4, NS).transpose(2, 1, 0)[None]), c(o["mo"][:, 1:].T[None]), c(rst[None]))


def kernel(**inputs):
    import concourse.bacc as bacc
    from concourse.bass_utils import run_bass_kernel_spmd

    nc = bacc.Bacc("TRN2", target_bir_lowering=False, num_devices=1)
    arrays = {k: np.ascontiguousarray(a) for k, a in lay_out({k: np.asarray(a) for k, a in inputs.items()}).items()}
    dram = {k: nc.dram_tensor(f"in_{k}", s, F32, kind="ExternalInput").ap() for k, s in INS.items()}
    dram.update({k: nc.dram_tensor(f"out_{k}", s, F32, kind="ExternalOutput").ap() for k, s in OUTS.items()})
    program(nc, **dram)
    r = run_bass_kernel_spmd(nc, [{f"in_{k}": a for k, a in arrays.items()}], core_ids=[0])
    return unpack({k: np.asarray(r.results[0][f"out_{k}"]) for k in OUTS})
```

```python
from contextlib import ExitStack
from itertools import zip_longest

import numpy as np

import concourse.bass as bass
from concourse import mybir

F32 = mybir.dt.float32
F32R = mybir.dt.float32r
ALU = mybir.AluOpType
ACT = mybir.ActivationFunctionType

P = 128
D = 1024
KD = D // P
TP = 512
NS = 8
T = TP + NS
HALF = T // 2
FF = 4 * D
KF = FF // P
PLE = 256
KP = PLE // P
L = 128
NG = TP // L
SUB = 64
AH, AHD = 8, 64
BH, BHD = 4, 128
CH, CDK, CDV = 4, 256, 512
NA = 14
NB = 16
RMS_EPS = 1e-6
GN_EPS = 1e-5
A_LN_EPS = 64e-5
C0 = float(np.exp(-0.5))
SLAB = 32 * P
NEG = -1e30


def columns(parts):
    at, out = 0, {}
    for name, n in parts:
        out[name] = (at, n)
        at += n
    return out, at


VEC, NVEC = columns([
    ("norm_g", 64), ("mu", NA), ("w0", 4), ("a0", 4), ("kk", 4), ("ka", 4), ("rk", 4), ("rln", 4),
    ("cw", 32), ("cb", 8), ("mgn", 4), ("rgn", 16), ("ib", 1), ("fb", 1), ("m", NS),
    ("shift", NA * NS), ("conv", 8 * 3 * NS), ("n", BH * NS), ("wif", KD * 36), ("w2a2", 512), ("g2", 512)])
CON, NCON = columns([
    ("mean_d", P), ("ident", P), ("ones", P), ("ones64", P), ("mean64", P), ("mean128", P), ("mean512", P),
    ("gram", 2 * P), ("bd16", P), ("n1t", P), ("n2", P), ("reset", P), ("neg", P), ("sel", 4 * P),
    ("cos", T), ("sin", T), ("rmask", CH * P), ("qdec", CH * P), ("kdec", CH), ("cdec", CH)])


def shape_constants():
    f = np.float32
    c = np.zeros((P, NCON), f)

    def put(name, a):
        at, n = CON[name]
        c[:a.shape[0], at:at + n] = a.reshape(a.shape[0], n)

    i = np.arange(P)
    row, col = i[:, None], i[None, :]
    put("ident", np.eye(P, dtype=f))
    put("ones", np.ones((P, P), f))
    put("mean_d", np.full((P, P), 1.0 / D, f))
    same64 = row // 64 == col // 64
    put("ones64", same64.astype(f))
    put("mean64", same64.astype(f) / f(64))
    put("mean128", np.full((P, P), 1.0 / 128, f))
    put("mean512", np.full((P, P), 1.0 / 512, f))
    put("gram", np.concatenate([same64 & (row < col), same64 & (row <= col)], 1).astype(f))
    put("bd16", (row // 16 == col // 16).astype(f))
    put("n1t", ((col // 16 % 2 == 1) & (row // 16 == col // 16 - 1)).astype(f))
    put("n2", ((row // 32 % 2 == 1) & (col // 32 == row // 32 - 1)).astype(f))
    put("reset", np.broadcast_to((col % SUB != 0).astype(f), (P, P)))
    put("neg", np.where(row <= col, 0.0, NEG).astype(f))
    sel = np.zeros((4, 4, P), f)
    for h in range(4):
        sel[h, h] = 1.0
    put("sel", sel.reshape(4, -1))
    half = CDK // 2
    pos = np.concatenate([np.arange(TP), np.full(NS, 4096)]).astype(f)
    inv = (f(10000.0) ** (-np.arange(half, dtype=f) / f(half))).astype(f)
    ang = (pos[None, :] * inv[:, None]).astype(f)
    put("cos", np.cos(ang))
    put("sin", np.sin(ang))
    lg = np.log1p(-np.exp2(-5.0 - np.arange(CH)))
    put("rmask", np.stack([np.where(row <= col, np.exp(np.maximum(col - row, 0) * g), 0.0) for g in lg], 1))
    put("qdec", np.broadcast_to(np.stack([np.exp((i + 1) * g) for g in lg])[None], (P, CH, P)))
    put("kdec", np.stack([np.exp((L - 1 - i) * g) for g in lg], 1))
    put("cdec", np.broadcast_to(np.exp(lg)[None], (P, CH)))
    return c


CDEC_CHUNK = [float(np.exp(L * np.log1p(-np.exp2(-5.0 - h)))) for h in range(CH)]
CDEC_ONE = [float(np.exp(np.log1p(-np.exp2(-5.0 - h)))) for h in range(CH)]


def in_turn(*parts):
    for _ in zip_longest(*parts):
        pass


class Steps:

    def __init__(self, sem, names, base=0):
        self.sem, self.names, self.base, self.at_now = sem, names, base, 0

    def at(self, name, it=0):
        return self.sem, it * len(self.names) + (self.base + self.names.index(name) + 1)

    def step(self, name):
        want = self.names[self.at_now % len(self.names)]
        assert name == want, (name, want)
        self.at_now += 1
        return self.sem, 1


class Space:

    def __init__(self, stretches):
        self.free = [[ap, ap.shape[1], 0] for ap in stretches]

    def take(self, *dims):
        n = int(np.prod(dims))
        for s in self.free:
            if s[2] + n <= s[1]:
                ap = s[0][:, s[2]:s[2] + n]
                s[2] += n
                if len(dims) == 1:
                    return ap
                names = "abcd"[:len(dims)]
                return ap.rearrange(f"p ({' '.join(names)}) -> p {' '.join(names)}",
                                    **{k: d for k, d in zip(names[1:], dims[1:])})
        raise AssertionError(f"no room for {dims}: {[(s[1], s[2]) for s in self.free]}")


CHUNK = 8 * P
HH = KF // 2
FFN0 = ["up0a", "down0a", "up0b", "down0b"]
FFN1 = ["up1a", "down1a", "up1b", "down1b"]
SPLIT = ["in0"] + FFN0 + ["qkv", "g"] + FFN1
GEMMS, RING, _s, _t, _r = {}, {}, 0, 0, 0
for _name, _slabs, _tiles, _per in [
        ("in0", 8, NA + NB, 4), ("out0", 2, 8, 4), ("up0a", 4, HH, 4), ("down0a", 4, 8, 2),
        ("up0b", 4, HH, 4), ("down0b", 4, 8, 2), ("gate0", 2, 8, 4),
        ("qkv", 8, 32, 4), ("g", 4, 16, 4), ("out1", 4, 8, 2), ("up1a", 4, HH, 4), ("down1a", 4, 8, 2),
        ("up1b", 4, HH, 4), ("down1b", 4, 8, 2), ("gate1", 2, 8, 4)]:
    GEMMS[_name] = (_s, _t, _slabs, _tiles, _per)
    RING[_name] = _r
    _s, _t, _r = _s + _slabs, _t + _tiles, _r + _slabs * (_name not in SPLIT)
NSLAB = _s
CHUNKS = {n: sum(4 * GEMMS[m][2] for m in SPLIT[:k]) for k, n in enumerate(SPLIT)}
FFN_CHUNKS = [CHUNKS["up0a"], CHUNKS["up1a"]]

RW_DVE = ["kkr", "cum0", "cum1", "prev", "floor", "rinv", "kk", "ka0", "ka1", "kp", "at", "rt", "kka", "bt", "kt",
          "bh", "kh", "bon", "ad0", "ad1", "me0", "me1", "d0", "n2", "t1", "d2t", "t2", "d4t", "t4", "t8", "z",
          "t16", "zz", "tt", "qp", "gh0", "gh1", "s0a", "s0b", "mid", "s1a", "s1b", "end", "yc", "vinv", "yn",
          "yg0", "yg1", "out"]
RW_ACT = ["v", "sq", "p", "q", "pm", "norm", "ar", "br", "vr", "mv", "d2", "d4", "d8t", "t8t", "t16t", "w",
          "y", "ysq", "ysd"]
RW_POOL = ["rk", "rkw", "d0t", "n1t"]
RW_PE = ["norm", "bonus", "rows", "gram_b", "gram_k", "a", "mv", "d2", "d2t", "t2", "d4", "d4t", "t4", "d8t",
         "t8", "t8t", "z", "t16", "t16t", "zz", "tt", "w", "qp", "gh", "s0", "s1", "y", "mean", "var"]


def program(nc, stop=None, **dram):
    with ExitStack() as ctx:
        def sb(name, n):
            return ctx.enter_context(nc.sbuf_tensor(name, [P, n], F32))

        def sem(name):
            return ctx.enter_context(nc.semaphore(name))

        con, vec = sb("con", NCON), sb("vec", NVEC)
        hbuf = [sb("h_a", KD * T), sb("h_b", KD * T)]
        rb_t = sb("rb", T)
        free = sb("free", 8 * T)
        with ExitStack() as first:
            def sb1(name, n):
                return first.enter_context(nc.sbuf_tensor(name, [P, n], F32))
            xg_t = sb1("xg", KD * T)
            pjw = sb1("pjw", KP * KD * P)
            spare = sb1("spare", KD * T - KP * KD * P)
            big = sb1("big", KF * T)
            slot = [sb1("slot0", SLAB), sb1("slot1", SLAB)]
        def sbr(name, n):
            return ctx.enter_context(nc.sbuf_tensor(name, [P, n], F32R))
        xh_t, xl_t = sbr("x_high", KD * T), sbr("x_low", KD * T)
        hh_t, hl_t = sbr("hidden_high", HH * T), sbr("hidden_low", HH * T)
        under_slot0 = sbr("under_slot0", SLAB)
        wh_t, wl_t = sbr("w_high", 2 * CHUNK), sbr("w_low", 2 * CHUNK)
        ps = ctx.enter_context(nc.psum_tensor("ps", [P, 8, 512], F32))

        def tiles(t, n=KD, w=T):
            return t[:, 0:n * w].rearrange("p (k t) -> p k t", t=w)

        hb = [tiles(t) for t in hbuf]
        xg, hid = tiles(xg_t), tiles(big, KF)
        xh, xl, hh, hl = tiles(xh_t), tiles(xl_t), tiles(hh_t, HH), tiles(hl_t, HH)
        raw = [slot[0][:, c * CHUNK:(c + 1) * CHUNK] for c in range(4)]
        wh, wl = [[t[:, c * CHUNK:(c + 1) * CHUNK] for c in range(2)] for t in (wh_t, wl_t)]
        ua = big[:, 0:NA * (T + 1)].rearrange("p (k t) -> p k t", t=T + 1)
        ub = big[:, NA * (T + 1):NA * (T + 1) + NB * T].rearrange("p (k t) -> p k t", t=T)
        rb = rb_t[:, :]
        tail = Space([free[:, :]])
        sqr = [tail.take(T), tail.take(T)]
        ss = tail.take(T)
        rt = tail.take(T)
        tmp = [tail.take(T), tail.take(T)]
        pt = tail.take(KP, T)

        def C(name, i=0, n=None):
            a, w = CON[name]
            n = w if n is None else n
            return con[:, a + i:a + i + n]

        def V(name, i=0, n=1):
            a, _ = VEC[name]
            return vec[:, a + i:a + i + n]

        def two(ap):
            return ap.rearrange("p (a n) -> p a n", a=2)

        def bank(par):
            return ps[:, 2 * par:2 * par + 2, 0:HALF]

        s_vec, s_con = sem("vec_loaded"), sem("con_loaded")
        s_first, s_x = sem("first_constants_loaded"), [sem(f"x_loaded{k}") for k in range(4)]
        s_w = [sem("slab_loaded0"), sem("slab_loaded1")]
        s_tile = sem("tile_done")
        s_bank = sem("bank_free")
        s_xg = sem("xg_ready")
        s_st = sem("stats_done")
        s_rt = sem("rms_ready")
        s_rb = sem("rinv_ready")
        s_sq = sem("square_ready")
        s_ss = sem("square_summed")
        s_h = sem("h_ready")
        s_res = sem("residual_step")
        s_hid = sem("hidden_squared")
        s_chunk = [sem(f"chunk_loaded{c}") for c in range(4)]
        s_wh, s_wl = sem("chunk_high"), sem("chunk_low")
        s_half = sem("half_tile_done")
        s_xl = sem("x_low_ready")
        s_hh, s_hl = sem("hidden_high_ready"), sem("hidden_low_ready")
        s_pj_w, s_pt = sem("proj_weights_loaded"), sem("p_loaded")
        s_pj = sem("proj_done")
        s_pjc = sem("proj_copied")
        s_e = sem("gate_exp")
        s_pl = sem("gate_step")
        s_hn = sem("next_h_ready")
        s_out = sem("stored")
        outs = [0]
        MIXER_STORES = 16 * 6

        def store(eng, dst, src):
            outs[0] += 16
            eng.dma_start(dst, src).then_inc(s_out, 16)
            return outs[0]

        def part(name, names_by_engine):
            return {k: Steps(sem(f"{name}_{k}"), v, int(k == "dve")) for k, v in names_by_engine.items()}

        def gemm(pe, name, nk, rhs, before=None):
            slab0, tile0, slabs, ntiles, per = GEMMS[name]

            def slab(i, s, count, waits):
                pe.wait_ge(s_w[s], 16 * (RING[name] // 2 + 1) + 16 * i)
                for mt in range(count):
                    pe.wait_ge(s_bank, (tile0 + s * per + mt + 1) + 2 * per * i)
                    par = (s * per + mt) % 2
                    for kt in range(nk):
                        if waits and s == 0 and mt == 0:
                            pe.wait_ge(*waits(kt))
                        for hf in range(2):
                            at = (mt * nk + kt) * P
                            mm = pe.matmul(ps[:, 2 * par + hf, 0:HALF], slot[s][:, at:at + P], rhs(kt, hf),
                                           start=(kt == 0), stop=(kt == nk - 1))
                    mm.then_inc(s_tile, 1)

            whole = ntiles // (2 * per)
            with pe.Fori(0, whole) as i:
                for s in range(2):
                    slab(i, s, per, before)

        def tile_at(name, k, i=0, step=0):
            return (GEMMS[name][1] + k + 1) + step * i

        def pe_prenorm(pe, n):
            for kt in range(KD):
                pe.wait_ge(s_xg, 8 * n + kt + 1)
                for hf in range(2):
                    mm = pe.matmul(ps[:, 4 + hf, 0:HALF], C("mean_d"),
                                   hid[:, 24 + kt, hf * HALF:(hf + 1) * HALF], start=(kt == 0), stop=(kt == KD - 1))
            mm.then_inc(s_st, 1)

        def pe_postnorm(pe, n):
            pe.wait_ge(s_ss, 8 * n + 8)
            for hf in range(2):
                mm = pe.matmul(ps[:, 4 + hf, 0:HALF], C("mean_d"), ss[:, hf * HALF:(hf + 1) * HALF],
                               start=True, stop=True)
            mm.then_inc(s_st, 1)

        def act_rms(act, r):
            act.wait_ge(s_st, r + 1)
            if r:
                act.wait_ge(s_rb, r)
            nc.scalar.activation(two(rt), ps[:, 4:6, 0:HALF], ACT.Sqrt, bias=RMS_EPS).then_inc(s_rt, 1)

        def dve_rinv(dve, r):
            dve.wait_ge(s_rt, r + 1)
            nc.vector.reciprocal(rb, rt).then_inc(s_rb, 1)
            dve.wait_ge(s_rb, r + 1)

        def act_prenorm(act, n, h, gain, ready, xg):
            for kt in range(KD):
                act.wait_ge(*ready(kt))
                nc.scalar.activation(xg[:, kt, :], h[:, kt, :], ACT.Copy, scale=V("norm_g", gain * 8 + kt))
                nc.scalar.activation(hid[:, 24 + kt, :], h[:, kt, :], ACT.Square).then_inc(s_xg, 1)


        def act_outproj(act, name, n, out):
            for mt in range(KD):
                act.wait_ge(s_tile, tile_at(name, mt))
                if 8 * n + mt >= 2:
                    act.wait_ge(s_ss, 8 * n + mt - 1)
                nc.scalar.activation(two(sqr[mt % 2]), bank(mt % 2), ACT.Square).then_inc(s_sq, 1)
                nc.scalar.activation(two(out[:, mt, :]), bank(mt % 2), ACT.Copy).then_inc(s_bank, 1)

        def pool_sum(pool, n):
            for mt in range(KD):
                pool.wait_ge(s_sq, 8 * n + mt + 1)
                if mt == 0:
                    nc.gpsimd.tensor_copy(ss, sqr[0]).then_inc(s_ss, 1)
                else:
                    pool.wait_ge(s_ss, 8 * n + mt)
                    nc.gpsimd.tensor_tensor(ss, ss, sqr[mt % 2], ALU.add).then_inc(s_ss, 1)

        def dve_residual(dve, n, out, h, gain, split=None):
            def low(kt):
                lyr, g = split
                dve.wait_ge(s_xg, 8 * (2 * lyr + 1) + kt + 1)
                nc.vector.scalar_tensor_tensor(xl[:, kt, :], h[:, kt, :], V("norm_g", g * 8 + kt),
                                               xh[:, kt, :].bitcast(F32), ALU.mult, ALU.subtract).then_inc(s_xl, 1)
            for kt in range(KD):
                if split and kt >= 2:
                    low(kt - 2)
                nc.vector.scalar_tensor_tensor(tmp[0], out[:, kt, :], V("norm_g", gain * 8 + kt), rb,
                                               ALU.mult, ALU.mult).then_inc(s_res, 1)
                dve.wait_ge(s_res, 8 * n + kt + 1)
                nc.vector.tensor_tensor(h[:, kt, :], h[:, kt, :], tmp[0], ALU.add).then_inc(s_h, 1)
                dve.wait_ge(s_h, 8 * n + kt + 1)
            if split:
                low(KD - 2)
                low(KD - 1)

        ds = bass.ds
        half_b, xg_q = 4 * T, 4 * T
        sig = tiles(hbuf[1], 4)
        aa = xg[:, 0:4, :]
        gg = xg[:, 4:8, :]
        used0 = tail.free[0][2]
        pieces = [hbuf[0][:, :], spare[:, :], hbuf[1][:, half_b:], pjw[:, :],
                  big[:, NA * (T + 1) + NB * T:], free[:, 0:3 * T], free[:, 6 * T:6 * T + KP * T]]


        r0 = Space(pieces)
        sho = r0.take(NA, NS + 1)
        cvo = r0.take(8, 11)
        ct = r0.take(NG * BH)
        sr = r0.take(24)
        mo = r0.take(NS + 1)
        s_end = [r0.take(2, P) for _ in range(2)]
        crow, nmrow, nmtrow = tmp[0], tmp[1], rt

        rwkv_space = Space([*[p[:, u:] for p, u in [(r[0], r[2]) for r in r0.free]], slot[0][:, :], slot[1][:, :]])

        class RwkvBuffers:

            def __init__(self, r, s_first):
                pair = lambda ap: ap.rearrange("p (j t) -> p j t", j=2)
                halves = lambda ap: (ap[:, 0:2], ap[:, 2:4])
                self.RH = r.take(2, 4, 64)
                rhf = self.RH.rearrange("p a h n -> p (a h n)")
                self.kkr, self.ksq = pair(rhf[:, 0:256]), pair(rhf[:, 256:512])
                self.d0, self.d0t, self.t2 = [r.take(4, P) for _ in range(3)]
                self.n1t, self.n2, self.t1, self.d2, self.d2t = [r.take(4, P) for _ in range(5)]
                self.kkn, self.cum = halves(self.n1t)
                self.kp, self.knr = halves(self.n2)
                self.qq, self.pm = halves(self.t1)
                self.bt, self.kt_ = halves(self.d2)
                self.bh, self.kh = halves(self.d2t)
                self.pp, self.tb, self.vS = [r.take(2, P) for _ in range(3)]
                self.AR = r.take(2, 2, P)
                self.bht, self.kht, self.vt = [r.take(4, 64) for _ in range(3)]
                self.AD = r.take(4, 2 * P)
                self.ME = r.take(4, 2 * P)
                self.GH = r.take(2, 4, P)
                ghf = self.GH.rearrange("p c a n -> p (c a n)")
                self.d4, self.d4t = [ghf[:, i * 512:(i + 1) * 512].rearrange("p (h n) -> p h n", h=4)
                                     for i in range(2)]
                self.t4 = self.tt = self.t1
                self.t8, self.t8t, self.d8t, self.zb, self.zz = self.t2, self.d2, self.d0t, self.d2t, self.d0
                self.t16, self.t16t = self.d4, self.d4t
                self.Wb = self.t2.rearrange("p h n -> p (h n)")
                self.qp, self.yb_, self.rkb, self.yc = self.knr, self.kkn, self.kkn, self.cum
                self.ysq, self.yr, self.sh_ = self.qq, self.pm, self.tb
                self.s_buf = [s_first, r.take(2, P)]
        halves_of_heads = [RwkvBuffers(rwkv_space, s_end[h]) for h in range(2)]

        def bk(b, n=4):
            return ps[:, b, 0:n * P].rearrange("p (h t) -> p h t", t=P)

        def bc(ap, n):
            return ap.unsqueeze(2).to_broadcast([ap.shape[0], ap.shape[1], n])

        def mid(ap, k):
            return ap.unsqueeze(1).to_broadcast([ap.shape[0], k, ap.shape[1]])

        rw = [part(f"rwkv_half{h}", dict(pe=RW_PE, dve=RW_DVE, act=RW_ACT, pool=RW_POOL)) for h in range(2)]
        s_zero, s_rs = sem("state_zeroed"), sem("rwkv_state_stored")

        def rw_bank(h, n, k=4):
            return ps[:, 4 * h + n, 0:k * P].rearrange("p (h t) -> p h t", t=P)

        def uah(arr, h, g):
            return ua[:, 2 * h + arr:2 * h + arr + 2, ds(L * g + 1, L)]

        def th(x, h, g):
            return x[:, 2 * h:2 * h + 2, ds(L * g, L)]

        def dve_rwkv(dve):
            v = nc.vector

            def half(h, g):
                rd, ra, rp, rl, b = rw[h]["dve"], rw[h]["act"], rw[h]["pe"], rw[h]["pool"], halves_of_heads[h]
                bk = lambda n, k=4: rw_bank(h, n, k)

                def after(steps, name, back=0):
                    dve.wait_ge(*steps.at(name, g - back))
                v.tensor_tensor(b.kkr, uah(4, h, g), bc(V("kk", 2 * h, 2), L),
                                ALU.mult).then_inc(*rd.step("kkr"))
                for j in range(2):
                    v.tensor_tensor_scan(b.cum[:, j, :], C("reset"), sig[:, 2 * h + j, ds(L * g, L)], 0.0,
                                         ALU.mult, ALU.add).then_inc(*rd.step(f"cum{j}"))
                after(rd, "cum1")
                v.tensor_tensor(b.tb, b.cum, th(sig, h, g), ALU.subtract).then_inc(*rd.step("prev"))
                yield
                after(rp, "norm")
                v.tensor_scalar(b.knr, bk(0, 2), 1e-24, None, ALU.max).then_inc(*rd.step("floor"))
                yield
                after(ra, "norm")
                v.reciprocal(b.knr, b.knr).then_inc(*rd.step("rinv"))
                after(rd, "rinv")
                v.tensor_tensor(b.kkn, b.kkr, b.knr, ALU.mult).then_inc(*rd.step("kk"))
                yield
                after(ra, "pm")
                for j in range(2):
                    v.tensor_scalar(b.tb[:, j, :], aa[:, 2 * h + j, ds(L * g, L)], -1.0,
                                    V("ka", 2 * h + j), ALU.add,
                                    ALU.mult).then_inc(*rd.step(f"ka{j}"))
                after(rd, "ka1")
                v.scalar_tensor_tensor(b.kp, b.tb, 1.0, uah(4, h, g), ALU.add, ALU.mult).then_inc(*rd.step("kp"))
                v.scalar_tensor_tensor(b.AR[:, :, 0, :], b.kkn, -1.0, b.pm, ALU.mult, ALU.mult).then_inc(*rd.step("at"))
                v.tensor_tensor(b.AR[:, :, 1, :], uah(0, h, g), b.pp, ALU.mult).then_inc(*rd.step("rt"))
                after(rd, "kp")
                v.tensor_tensor(b.tb, b.kkn, th(aa, h, g), ALU.mult).then_inc(*rd.step("kka"))
                after(rd, "kka")
                v.tensor_tensor(b.bt, b.tb, b.qq, ALU.mult).then_inc(*rd.step("bt"))
                v.tensor_tensor(b.kt_, b.kp, b.qq, ALU.mult).then_inc(*rd.step("kt"))
                after(rd, "kt")
                last = b.pp.rearrange("p j (c n) -> p (j c) n", n=SUB)[:, :, SUB - 1:SUB].to_broadcast([P, 4, SUB])
                by_chunk = lambda ap: ap.rearrange("p j (c n) -> p (j c) n", n=SUB)
                v.tensor_tensor(by_chunk(b.bh), by_chunk(b.bt), last, ALU.mult).then_inc(*rd.step("bh"))
                v.tensor_tensor(by_chunk(b.kh), by_chunk(b.kt_), last, ALU.mult).then_inc(*rd.step("kh"))
                yield
                after(rp, "bonus")
                after(rp, "rows")
                v.tensor_tensor(b.vS, ps[:, 4 * h, 256:512].rearrange("p (j t) -> p j t", j=2), b.vS,
                                ALU.mult).then_inc(*rd.step("bon"))
                yield
                after(rp, "gram_b")
                for par in range(2):
                    o = b.AD.rearrange("p (j q) n -> p q j n", q=2)[:, par]
                    v.tensor_tensor(o, ps[:, 4 * h + (3, 0)[par], :].rearrange("p (j n) -> p j n", j=2),
                                    mid(C("gram"), 2), ALU.mult).then_inc(*rd.step(f"ad{par}"))
                yield
                after(rp, "gram_k")
                for par in range(2):
                    o = b.ME.rearrange("p (j q) n -> p q j n", q=2)[:, par]
                    v.tensor_tensor(o, ps[:, 4 * h + 1 + par, :].rearrange("p (j n) -> p j n", j=2),
                                    mid(C("gram"), 2), ALU.mult).then_inc(*rd.step(f"me{par}"))
                yield
                after(rp, "a")
                v.tensor_tensor(b.d0, bk(3), mid(C("bd16"), 4), ALU.mult).then_inc(*rd.step("d0"))
                v.tensor_tensor(b.n2, bk(3), mid(C("n2"), 4), ALU.mult).then_inc(*rd.step("n2"))
                after(rd, "d0")
                v.tensor_tensor(b.t1, b.d0, mid(C("ident"), 4), ALU.add).then_inc(*rd.step("t1"))
                yield
                after(rp, "d2t")
                v.tensor_copy(b.d2t, bk(2)).then_inc(*rd.step("d2t"))
                yield
                after(rp, "t2")
                after(rd, "t1")
                v.tensor_tensor(b.t2, bk(3), b.t1, ALU.add).then_inc(*rd.step("t2"))
                yield
                after(rp, "d4t")
                v.tensor_copy(b.d4t, bk(1)).then_inc(*rd.step("d4t"))
                yield
                after(rp, "t4")
                v.tensor_tensor(b.t4, bk(2), b.t2, ALU.add).then_inc(*rd.step("t4"))
                yield
                after(rp, "t8")
                after(rd, "t4")
                v.tensor_tensor(b.t8, bk(0), b.t4, ALU.add).then_inc(*rd.step("t8"))
                yield
                after(rp, "z")
                v.tensor_copy(b.zb, bk(2)).then_inc(*rd.step("z"))
                yield
                after(rp, "t16")
                v.tensor_tensor(b.t16, bk(3), b.t8, ALU.add).then_inc(*rd.step("t16"))
                yield
                after(rp, "zz")
                v.tensor_copy(b.zz, bk(1)).then_inc(*rd.step("zz"))
                yield
                after(rp, "tt")
                v.tensor_tensor(b.tt, bk(2), b.t16t, ALU.add).then_inc(*rd.step("tt"))
                yield
                after(rp, "qp")
                v.tensor_tensor(b.qp, bk(3, 2), b.AR[:, :, 1, :], ALU.add).then_inc(*rd.step("qp"))
                yield
                after(rp, "gh")
                for c in range(2):
                    v.tensor_tensor(b.GH[:, c], bk(2 * c), mid(C("ones64"), 4),
                                    ALU.mult).then_inc(*rd.step(f"gh{c}"))
                after(rd, "gh1")
                dve.wait_ge(s_zero, 2)
                for c in range(2):
                    for j in range(2):
                        v.scalar_tensor_tensor(b.sh_[:, j, :], b.s_buf[c][:, j, :],
                                               b.pp[:, j, SUB * c + SUB - 1:SUB * c + SUB], b.GH[:, c, 2 + j],
                                               ALU.mult, ALU.add).then_inc(*rd.step(f"s{c}{'ab'[j]}"))
                    after(rd, f"s{c}b")
                    yield
                    after(rp, f"s{c}")
                    v.tensor_tensor(b.s_buf[1 - c], bk(3 * (1 - c), 2), b.sh_, ALU.add).then_inc(*rd.step(["mid", "end"][c]))
                    after(rd, ["mid", "end"][c])
                yield
                after(rp, "mean")
                v.tensor_tensor(b.yc, b.yb_, bk(2, 2), ALU.subtract).then_inc(*rd.step("yc"))
                yield
                after(ra, "ysd")
                v.reciprocal(b.yr, b.yr).then_inc(*rd.step("vinv"))
                after(rd, "vinv")
                v.tensor_tensor(b.yc, b.yc, b.yr, ALU.mult).then_inc(*rd.step("yn"))
                after(rd, "yn")
                for j in range(2):
                    v.scalar_tensor_tensor(b.yc[:, j, :], b.yc[:, j, :], V("rln", 2 * h + j),
                                           b.vS[:, j, :], ALU.mult, ALU.add).then_inc(*rd.step(f"yg{j}"))
                after(rd, "yg1")
                v.tensor_tensor(uah(0, h, g), b.yc, th(gg, h, g), ALU.mult).then_inc(*rd.step("out"))
                after(rd, "out")
                yield

            for h in range(2):
                v.memset(s_end[h], 0.0).then_inc(s_zero, 1)
            with dve.Fori(0, NG) as g:
                in_turn(half(0, g), half(1, g))

        def act_rwkv(act):
            a = nc.scalar

            def half(h, g):
                rd, ra, rp, rl, b = rw[h]["dve"], rw[h]["act"], rw[h]["pe"], rw[h]["pool"], halves_of_heads[h]
                bk = lambda n, k=4: rw_bank(h, n, k)

                def after(steps, name, back=0):
                    act.wait_ge(*steps.at(name, g - back))
                yield
                after(rd, "out", 1)
                a.activation(b.vS, uah(8, h, g), ACT.Copy).then_inc(*ra.step("v"))
                yield
                after(rd, "kkr")
                a.activation(b.ksq, b.kkr, ACT.Square).then_inc(*ra.step("sq"))
                yield
                after(rd, "cum1")
                a.activation(b.pp, b.cum, ACT.Exp, scale=-C0).then_inc(*ra.step("p"))
                a.activation(b.qq, b.cum, ACT.Exp, scale=C0).then_inc(*ra.step("q"))
                yield
                after(rd, "prev")
                a.activation(b.pm, b.tb, ACT.Exp, scale=-C0).then_inc(*ra.step("pm"))
                yield
                after(rd, "floor")
                a.activation(b.knr, b.knr, ACT.Sqrt).then_inc(*ra.step("norm"))
                yield
                after(rp, "rows")
                r4 = lambda n, k: ps[:, 4 * h + n, 256 * k:256 * k + 256].rearrange("p (h n) -> p h n", h=4)
                a.activation(b.RH[:, 0], r4(1, 0), ACT.Copy).then_inc(*ra.step("ar"))
                a.activation(b.bht, r4(1, 1), ACT.Copy)
                a.activation(b.kht, r4(2, 0), ACT.Copy).then_inc(*ra.step("br"))
                a.activation(b.vt, r4(2, 1), ACT.Copy).then_inc(*ra.step("vr"))
                yield
                after(rp, "mv")
                a.activation(b.RH[:, 1], r4(0, 0), ACT.Copy).then_inc(*ra.step("mv"))
                for name, out, n in [("d2", b.d2, 1), ("d4", b.d4, 0), ("d8t", b.d8t, 3), ("t8t", b.t8t, 1),
                                     ("t16t", b.t16t, 0)]:
                    yield
                    after(rp, name)
                    a.activation(out, bk(n), ACT.Copy).then_inc(*ra.step(name))
                yield
                after(rp, "w")
                a.activation(b.Wb.rearrange("p (a h n) -> p h a n", a=2, h=4),
                             bk(3).rearrange("p h (a n) -> p h a n", a=2), ACT.Copy).then_inc(*ra.step("w"))
                yield
                after(rp, "y")
                a.activation(b.yb_, bk(1, 2), ACT.Copy).then_inc(*ra.step("y"))
                yield
                after(rd, "yc")
                a.activation(b.ysq, b.yc, ACT.Square).then_inc(*ra.step("ysq"))
                yield
                after(rp, "var")
                a.activation(b.yr, bk(3, 2), ACT.Sqrt, bias=A_LN_EPS).then_inc(*ra.step("ysd"))
                yield

            with act.Fori(0, NG) as g:
                in_turn(half(0, g), half(1, g))

        def pool_rwkv(pool):
            def half(h, g):
                rd, ra, rp, rl, b = rw[h]["dve"], rw[h]["act"], rw[h]["pe"], rw[h]["pool"], halves_of_heads[h]
                bk = lambda n, k=4: rw_bank(h, n, k)

                def after(steps, name, back=0):
                    pool.wait_ge(*steps.at(name, g - back))
                after(rd, "kka")
                nc.gpsimd.tensor_tensor(b.rkb, uah(0, h, g), b.kp, ALU.mult).then_inc(*rl.step("rk"))
                after(rl, "rk")
                nc.gpsimd.tensor_tensor(b.rkb, b.rkb, bc(V("rk", 2 * h, 2), L), ALU.mult).then_inc(*rl.step("rkw"))
                yield
                after(rd, "ad1")
                nc.gpsimd.tensor_tensor(b.d0t, b.AD[:, :, 0:P], mid(C("bd16"), 4), ALU.mult).then_inc(*rl.step("d0t"))
                nc.gpsimd.tensor_tensor(b.n1t, b.AD[:, :, 0:P], mid(C("n1t"), 4), ALU.mult).then_inc(*rl.step("n1t"))
                yield

            with pool.Fori(0, NG) as g:
                in_turn(half(0, g), half(1, g))

        def pe_rwkv(pe):
            def half(h, g):
                rd, ra, rp, rl, b = rw[h]["dve"], rw[h]["act"], rw[h]["pe"], rw[h]["pool"], halves_of_heads[h]
                bk = lambda n, k=4: rw_bank(h, n, k)

                def after(steps, name, back=0):
                    pe.wait_ge(*steps.at(name, g - back))

                def mm4(n, lhs, rhs, step):
                    for hh in range(4):
                        mm = pe.matmul(bk(n)[:, hh, :], lhs[:, hh, :], rhs[:, hh, :], start=True, stop=True)
                    mm.then_inc(*rp.step(step))

                def transposed(n, x, step):
                    for hh in range(4):
                        mm = pe.transpose(bk(n)[:, hh, :], x(hh), C("ident"))
                    mm.then_inc(*rp.step(step))
                o = 4 * h
                after(ra, "sq")
                pe.matmul(ps[:, o, 0:256], C("ones64"), b.ksq, start=True, stop=True).then_inc(*rp.step("norm"))
                yield
                after(rl, "rkw")
                after(rd, "floor")
                pe.matmul(ps[:, o, 256:512], C("ones64"), b.rkb, start=True, stop=True).then_inc(*rp.step("bonus"))
                yield
                after(rd, "kh")
                for j in range(2):
                    pe.transpose(ps[:, o + 1, j * P:(j + 1) * P], b.AR[:, j, 0, :], C("ident"))
                    pe.transpose(ps[:, o + 1, 256 + j * P:256 + (j + 1) * P], b.bh[:, j, :], C("ident"))
                    pe.transpose(ps[:, o + 2, j * P:(j + 1) * P], b.kh[:, j, :], C("ident"))
                    mm = pe.transpose(ps[:, o + 2, 256 + j * P:256 + (j + 1) * P], b.vS[:, j, :], C("ident"))
                mm.then_inc(*rp.step("rows"))
                for w, banks, step, waits in [(b.bt, (3, 0), "gram_b", (rd, "bon")), (b.kt_, (1, 2), "gram_k", (ra, "vr"))]:
                    yield
                    after(*waits)
                    for par in range(2):
                        rows = slice(64 * par, 64 * par + 64)
                        for j in range(2):
                            mm = pe.matmul(ps[:, o + banks[par], 256 * j:256 * j + 256], w[rows, j, :],
                                           b.AR[rows, j, :, :], start=True, stop=True)
                    mm.then_inc(*rp.step(step))
                yield
                after(rd, "ad1")
                transposed(3, lambda hh: b.AD[:, hh, 0:P], "a")
                yield
                after(rd, "me1")
                for hh in range(4):
                    mm = pe.matmul(ps[:, o, 64 * hh:64 * hh + 64], b.ME[:, hh, 0:P], b.vt[:, hh, :],
                                   start=True, stop=True)
                mm.then_inc(*rp.step("mv"))
                yield
                after(rl, "d0t")
                after(rd, "d0")
                mm4(1, b.d0t, b.d0, "d2")
                mm4(2, b.d0, b.d0t, "d2t")
                yield
                after(rd, "d2t")
                after(rd, "t1")
                mm4(3, b.d2t, b.t1, "t2")
                yield
                after(ra, "d2")
                mm4(0, b.d2t, b.d2, "d4")
                mm4(1, b.d2, b.d2t, "d4t")
                yield
                after(rd, "d4t")
                after(rd, "t2")
                mm4(2, b.d4t, b.t2, "t4")
                yield
                after(ra, "d4")
                mm4(3, b.d4, b.d4t, "d8t")
                yield
                after(ra, "d8t")
                after(rd, "t4")
                mm4(0, b.d8t, b.t4, "t8")
                yield
                after(rd, "t8")
                transposed(1, lambda hh: b.t8[:, hh, :], "t8t")
                yield
                after(rl, "n1t")
                mm4(2, b.n1t, b.t8, "z")
                yield
                after(rd, "z")
                after(ra, "t8t")
                mm4(3, b.t8t, b.zb, "t16")
                yield
                after(rd, "t16")
                transposed(0, lambda hh: b.t16[:, hh, :], "t16t")
                yield
                after(ra, "t16t")
                mm4(1, b.n2, b.t16t, "zz")
                yield
                after(rd, "zz")
                mm4(2, b.t16, b.zz, "tt")
                yield
                after(rd, "tt")
                after(ra, "mv")
                for hh in range(4):
                    mm = pe.matmul(bk(3)[:, hh, :].rearrange("p (a n) -> p a n", a=2), b.tt[:, hh, :],
                                   b.RH[:, :, hh, :], start=True, stop=True)
                mm.then_inc(*rp.step("w"))
                yield
                after(ra, "w")
                w1 = lambda hh: b.Wb[:, 64 * hh:64 * hh + 64]
                u0 = lambda hh: b.Wb[:, 256 + 64 * hh:256 + 64 * hh + 64]
                for hh in range(4):
                    j, par = hh // 2, hh % 2
                    mm = pe.matmul(ps[64 * par:64 * par + 64, o + 3, j * P:(j + 1) * P], w1(hh), b.AD[:, hh, P:2 * P],
                                   start=True, stop=True)
                mm.then_inc(*rp.step("qp"))
                for c in range(2):
                    rows = slice(64 * c, 64 * c + 64)
                    for j in range(2):
                        two_heads = slice(P * j, P * j + P)
                        bhj = b.bht.rearrange("p h n -> p (h n)")[rows, two_heads]
                        khj = b.kht.rearrange("p h n -> p (h n)")[rows, two_heads]
                        vtj = b.vt.rearrange("p h n -> p (h n)")[rows, two_heads]
                        pe.matmul(bk(2 * c)[:, j, :], b.Wb[rows, two_heads], bhj, start=True, stop=True)
                        pe.matmul(bk(2 * c)[:, 2 + j, :], bhj, b.Wb[rows, 256 + P * j:256 + P * j + P],
                                  start=True, stop=False)
                        mm = pe.matmul(bk(2 * c)[:, 2 + j, :], khj, vtj, start=False, stop=True)
                mm.then_inc(*rp.step("gh"))
                for hh in range(4):
                    j, par = hh // 2, hh % 2
                    y = ps[64 * par:64 * par + 64, o + 1, j * P:(j + 1) * P]
                    pe.matmul(y, u0(hh), b.AD[:, hh, P:2 * P], start=(j == 0), stop=False, skip_group_check=True)
                    pe.matmul(y, b.vt[:, hh, :], b.ME[:, hh, P:2 * P], start=False, stop=False, skip_group_check=True)
                yield
                after(rd, "qp")
                for c in range(2):
                    after(rd, ["gh1", "mid"][c])
                    for j in range(2):
                        mm = pe.matmul(bk(3 * (1 - c))[:, j, :], b.GH[:, c, j, :], b.s_buf[c][:, j, :],
                                       start=True, stop=True)
                    mm.then_inc(*rp.step(f"s{c}"))
                    for j in range(2):
                        mm = pe.matmul(ps[:, o + 1, j * P + SUB * c:j * P + SUB * c + SUB], b.s_buf[c][:, j, :],
                                       b.qp[:, j, SUB * c:SUB * c + SUB], start=False, stop=(c == 1),
                                       skip_group_check=True)
                    if c == 0:
                        yield
                mm.then_inc(*rp.step("y"))
                yield
                after(ra, "y")
                pe.matmul(bk(2, 2), C("mean64"), b.yb_, start=True, stop=True).then_inc(*rp.step("mean"))
                yield
                after(ra, "ysq")
                pe.matmul(bk(3, 2), C("mean64"), b.ysq, start=True, stop=True).then_inc(*rp.step("var"))
                yield

            with pe.Fori(0, NG) as g:
                in_turn(half(0, g), half(1, g))

        r1 = Space([pieces[0][:, 1024:], *pieces[1:]])
        sst = r1.take(4, NS, 64)
        by_sample = lambda k: xg[:, k:k + 2, 0:TP].rearrange("p q (s n) -> p q s n", s=NS)
        um, vm = by_sample(0), by_sample(2)
        rows3 = xg[:, 4:7, 0:TP].rearrange("p k (j n) -> p k j n", j=4)
        xk, xq, xn, xkk, xw, xa, xkp, xb, xan, xbo, xy, xyc, xr = [r1.take(4, NS) for _ in range(13)]
        RS_DVE = ["kkr", "floor", "rinv", "kk", "a1", "ka", "kp", "an", "b", "rk", "rkw", "bon"]
        RS_DVEJ = ["um", "vm", "sw", "s"]
        RS_DVE2 = ["yc", "rinv2", "yn", "yl", "yg", "out"]
        rs_sem = {k: sem(f"rwkv1_{k}") for k in ("pe", "dve", "act")}
        sd = Steps(rs_sem["dve"], RS_DVE)
        sdj = Steps(rs_sem["dve"], RS_DVEJ, len(RS_DVE))
        sd2 = Steps(rs_sem["dve"], RS_DVE2, len(RS_DVE) + 4 * len(RS_DVEJ))
        sa = Steps(rs_sem["act"], ["sq", "norm", "w", "rows", "y", "ysq", "ysd"])
        sp_ = Steps(rs_sem["pe"], ["norm", "bonus", "rows"])
        spj = Steps(rs_sem["pe"], ["sa", "outer"], 3)
        sp2 = Steps(rs_sem["pe"], ["y", "mean", "var"], 3 + 8)
        s_sst, s_cst = sem("rwkv_state_loaded"), sem("mlstm_state_loaded")
        s_cso = sem("mlstm_sample_state_stored")
        uas = lambda arr: ua[:, arr:arr + 4, TP + 1:]
        smp = lambda x: x[:, :, TP:]
        eight = C("ident")[0:NS, 0:NS]

        def dve_rwkv1(dve):
            v = nc.vector

            def after(steps, name, it=0):
                dve.wait_ge(*steps.at(name, it))
            v.tensor_tensor(xk, uas(4), bc(V("kk", 0, 4), NS), ALU.mult).then_inc(*sd.step("kkr"))
            after(sp_, "norm")
            v.tensor_scalar(xn, ps[:, 4, 0:32].rearrange("p (j t) -> p j t", j=4), 1e-24, None,
                            ALU.max).then_inc(*sd.step("floor"))
            yield
            after(sa, "norm")
            v.reciprocal(xn, xn).then_inc(*sd.step("rinv"))
            after(sd, "rinv")
            v.tensor_tensor(xkk, xk, xn, ALU.mult).then_inc(*sd.step("kk"))
            v.tensor_scalar(xa, smp(aa), -1.0, None, ALU.add).then_inc(*sd.step("a1"))
            after(sd, "a1")
            v.tensor_tensor(xa, xa, bc(V("ka", 0, 4), NS), ALU.mult).then_inc(*sd.step("ka"))
            after(sd, "ka")
            v.scalar_tensor_tensor(xkp, xa, 1.0, uas(4), ALU.add, ALU.mult).then_inc(*sd.step("kp"))
            v.tensor_scalar(xan, xkk, -1.0, None, ALU.mult).then_inc(*sd.step("an"))
            v.tensor_tensor(xb, xkk, smp(aa), ALU.mult).then_inc(*sd.step("b"))
            after(sd, "kp")
            v.tensor_tensor(xbo, uas(0), xkp, ALU.mult).then_inc(*sd.step("rk"))
            after(sd, "rk")
            v.tensor_tensor(xbo, xbo, bc(V("rk", 0, 4), NS), ALU.mult).then_inc(*sd.step("rkw"))
            yield
            after(sp_, "bonus")
            v.tensor_tensor(xbo, ps[:, 4, 32:64].rearrange("p (j t) -> p j t", j=4), uas(8),
                            ALU.mult).then_inc(*sd.step("bon"))
            yield
            dve.wait_ge(s_sst, 16)
            after(sa, "rows")
            for j in range(4):
                after(spj, "sa", j)
                v.tensor_tensor(um[0:NS], ps[0:NS, 6:8, :].rearrange("p q (s n) -> p q s n", s=NS),
                                eight.unsqueeze(1).unsqueeze(3).to_broadcast([NS, 2, NS, 64]),
                                ALU.mult).then_inc(*sdj.step("um"))
                vr = rows3[0:NS, 2, j, :].rearrange("p (q n) -> p q n", q=2)
                v.tensor_tensor(vm[0:NS], vr.unsqueeze(2).to_broadcast([NS, 2, NS, 64]),
                                eight.unsqueeze(1).unsqueeze(3).to_broadcast([NS, 2, NS, 64]),
                                ALU.mult).then_inc(*sdj.step("vm"))
                v.tensor_tensor(sst[:, j], sst[:, j], bc(xw[:, j, :], 64), ALU.mult).then_inc(*sdj.step("sw"))
                yield
                after(sdj, "sw", j)
                after(spj, "outer", j)
                v.tensor_tensor(sst[:, j], sst[:, j], ps[:, 4 + j % 2, :].rearrange("p (s n) -> p s n", s=NS),
                                ALU.add).then_inc(*sdj.step("s"))
                yield
            yield
            after(sp2, "mean")
            v.tensor_tensor(xyc, xy, ps[:, 4, 0:32].rearrange("p (j t) -> p j t", j=4),
                            ALU.subtract).then_inc(*sd2.step("yc"))
            yield
            after(sa, "ysd")
            v.reciprocal(xr, xr).then_inc(*sd2.step("rinv2"))
            after(sd2, "rinv2")
            v.tensor_tensor(xyc, xyc, xr, ALU.mult).then_inc(*sd2.step("yn"))
            after(sd2, "yn")
            v.tensor_tensor(xyc, xyc, bc(V("rln", 0, 4), NS), ALU.mult).then_inc(*sd2.step("yl"))
            after(sd2, "yl")
            v.tensor_tensor(xyc, xyc, xbo, ALU.add).then_inc(*sd2.step("yg"))
            after(sd2, "yg")
            v.tensor_tensor(uas(0), xyc, smp(gg), ALU.mult).then_inc(*sd2.step("out"))
            after(sd2, "out")
            yield

        def act_rwkv1(act):
            a = nc.scalar

            def after(steps, name, it=0):
                act.wait_ge(*steps.at(name, it))
            after(sd, "kkr")
            a.activation(xq, xk, ACT.Square).then_inc(*sa.step("sq"))
            yield
            after(sd, "floor")
            a.activation(xn, xn, ACT.Sqrt).then_inc(*sa.step("norm"))
            a.activation(xw, smp(sig), ACT.Exp, scale=-C0).then_inc(*sa.step("w"))
            yield
            after(sp_, "rows")
            a.activation(rows3[0:NS].rearrange("p k j n -> p k (j n)"), ps[0:NS, 5:8, :],
                         ACT.Copy).then_inc(*sa.step("rows"))
            yield
            for _ in range(8):
                yield
            after(sp2, "y")
            a.activation(xy[0:64], ps[0:64, 6, 0:32].rearrange("p (j t) -> p j t", j=4), ACT.Copy)
            a.activation(xy[64:P], ps[64:P, 7, 0:32].rearrange("p (j t) -> p j t", j=4),
                         ACT.Copy).then_inc(*sa.step("y"))
            yield
            after(sd2, "yc")
            a.activation(xq, xyc, ACT.Square).then_inc(*sa.step("ysq"))
            after(sp2, "var")
            a.activation(xr, ps[:, 5, 0:32].rearrange("p (j t) -> p j t", j=4), ACT.Sqrt,
                         bias=A_LN_EPS).then_inc(*sa.step("ysd"))
            yield
            yield

        def pe_rwkv1(pe):
            def after(steps, name, it=0):
                pe.wait_ge(*steps.at(name, it))
            flat = lambda x: x.rearrange("p j t -> p (j t)")
            after(sa, "sq")
            pe.matmul(ps[:, 4, 0:32], C("ones64"), flat(xq), start=True, stop=True).then_inc(*sp_.step("norm"))
            yield
            after(sd, "rkw")
            pe.matmul(ps[:, 4, 32:64], C("ones64"), flat(xbo), start=True, stop=True).then_inc(*sp_.step("bonus"))
            for k, src in enumerate([xb, xkp, uas(8)]):
                for j in range(4):
                    mm = pe.transpose(ps[0:NS, 5 + k, j * P:(j + 1) * P], src[:, j, :], C("ident"))
            mm.then_inc(*sp_.step("rows"))
            yield
            yield
            after(sd, "bon")
            pe.wait_ge(s_sst, 16)
            for j in range(4):
                if j:
                    after(sdj, "um", j - 1)
                else:
                    after(sa, "rows")
                for par in range(2):
                    r = slice(64 * par, 64 * par + 64)
                    mm = pe.matmul(ps[0:NS, 6 + par, :], xan[r, j, :],
                                   sst[r, j].rearrange("p s n -> p (s n)"), start=True, stop=True)
                mm.then_inc(*spj.step("sa"))
                yield
                after(sdj, "vm", j)
                if j >= 2:
                    after(sdj, "s", j - 2)
                after(sa, "rows")
                for par in range(2):
                    o = ps[64 * par:64 * par + 64, 4 + j % 2, :]
                    c = slice(64 * par, 64 * par + 64)
                    pe.matmul(o, rows3[0:NS, 0, j, c], um[0:NS, par].rearrange("p s n -> p (s n)"),
                              start=True, stop=False)
                    mm = pe.matmul(o, rows3[0:NS, 1, j, c], vm[0:NS, par].rearrange("p s n -> p (s n)"),
                                   start=False, stop=True)
                mm.then_inc(*spj.step("outer"))
                yield
            after(sdj, "s", 3)
            for j in range(4):
                for b in range(NS):
                    for par in range(2):
                        r = slice(64 * par, 64 * par + 64)
                        mm = pe.matmul(ps[r, 6 + par, NS * j + b:NS * j + b + 1], sst[r, j, b, :],
                                       ua[r, j, TP + 1 + b:TP + 2 + b], start=True, stop=True)
            mm.then_inc(*sp2.step("y"))
            after(sa, "y")
            pe.matmul(ps[:, 4, 0:32], C("mean64"), flat(xy), start=True, stop=True).then_inc(*sp2.step("mean"))
            yield
            after(sa, "ysq")
            pe.matmul(ps[:, 5, 0:32], C("mean64"), flat(xq), start=True, stop=True).then_inc(*sp2.step("var"))
            yield
            yield

        r2 = r1
        kS, vS2, PT, IW, QI, EN, HD, HB, E, KH = [r2.take(4, P) for _ in range(10)]
        cn = r2.take(4, 2 * P)
        vo = r2.take(4, 2 * P)
        mprev, wia, wi, wca, wc = [r2.take(4) for _ in range(5)]
        ml = part("mlstm", dict(
            pe=["nm", "nb", "rows", "sc", "den", "num", "st", "mean", "var"],
            dve=["wia", "wca", "e0", "e1", "e2", "e3", "iwa", "mprev", "kh", "pt", "qi", "hd",
                 "hr", "hb", "ho", "c0", "c1", "c2", "c3", "yc", "rinv", "yn", "out"],
            act=["k", "v", "en", "vo", "wi", "wc", "e", "iw", "abs", "ysq", "ysd"]))
        mp, md, ma = ml["pe"], ml["dve"], ml["act"]
        s_mz = sem("mlstm_zeroed")
        ubg = lambda arr, g: ub[:, arr:arr + 4, ds(L * g, L)]

        def dve_mlstm(dve):
            v = nc.vector
            v.memset(cn, 0.0).then_inc(s_mz, 1)
            v.memset(mprev, 0.0).then_inc(s_mz, 1)
            v.memset(vo[:, :, P:2 * P], 1.0).then_inc(s_mz, 1)
            dve.wait_ge(s_mz, 3)
            for g in range(NG):
                def after(steps, name):
                    dve.wait_ge(*steps.at(name, g))
                yield
                after(mp, "nm")
                nml = bk(0)[:, :, P - 1]
                v.tensor_tensor(wia, ct[:, ds(4 * g, 4)], nml, ALU.add).then_inc(*md.step("wia"))
                v.tensor_tensor(wca, mprev, nml, ALU.add).then_inc(*md.step("wca"))
                for h in range(4):
                    v.scalar_tensor_tensor(E[:, h, :], bk(0)[:, h, :], ct[:, ds(4 * g + h, 1)], C("neg"),
                                           ALU.add, ALU.min).then_inc(*md.step(f"e{h}"))
                v.tensor_tensor(IW, bk(0), bc(mprev, P), ALU.add).then_inc(*md.step("iwa"))
                after(md, "iwa")
                v.tensor_scalar(mprev, nml, -1.0, None, ALU.mult).then_inc(*md.step("mprev"))
                yield
                after(mp, "rows")
                after(ma, "wc")
                v.tensor_tensor(KH, bk(2), bc(wi, P), ALU.mult).then_inc(*md.step("kh"))
                after(mp, "sc")
                after(ma, "iw")
                v.tensor_tensor(PT, bk(1), E, ALU.mult).then_inc(*md.step("pt"))
                v.tensor_tensor(QI, ubg(0, g), IW, ALU.mult).then_inc(*md.step("qi"))
                yield
                after(ma, "abs")
                v.tensor_tensor(HD, HD, EN, ALU.max).then_inc(*md.step("hd"))
                after(md, "hd")
                v.reciprocal(HD, HD).then_inc(*md.step("hr"))
                yield
                after(md, "hr")
                after(mp, "num")
                v.tensor_tensor(HB, bk(0), HD, ALU.mult).then_inc(*md.step("hb"))
                after(md, "hb")
                v.tensor_tensor(HB, HB, ubg(12, g), ALU.mult).then_inc(*md.step("ho"))
                yield
                after(mp, "st")
                for h in range(4):
                    v.scalar_tensor_tensor(cn[:, h, :], cn[:, h, :], wc[:, h:h + 1],
                                           ps[:, 1 + h // 2, 256 * (h % 2):256 * (h % 2) + 256],
                                           ALU.mult, ALU.add).then_inc(*md.step(f"c{h}"))
                after(mp, "mean")
                v.tensor_tensor(HB, HB, bk(3), ALU.subtract).then_inc(*md.step("yc"))
                yield
                after(ma, "ysd")
                v.reciprocal(HD, HD).then_inc(*md.step("rinv"))
                yield
                after(md, "rinv")
                v.tensor_tensor(HB, HB, HD, ALU.mult).then_inc(*md.step("yn"))
                after(md, "yn")
                v.tensor_tensor(ubg(0, g), HB, bc(V("mgn", 0, 4), P), ALU.mult).then_inc(*md.step("out"))
                after(md, "out")
                yield

        def act_mlstm(act):
            a = nc.scalar
            for g in range(NG):
                def after(steps, name, back=0):
                    act.wait_ge(*steps.at(name, g - back))
                a.activation(kS, ubg(4, g), ACT.Copy, scale=BHD ** -0.5).then_inc(*ma.step("k"))
                a.activation(vS2, ubg(8, g), ACT.Copy).then_inc(*ma.step("v"))
                after(mp, "nb")
                a.activation(EN, bk(1), ACT.Exp).then_inc(*ma.step("en"))
                after(mp, "rows")
                a.activation(vo[:, :, 0:P], bk(3), ACT.Copy).then_inc(*ma.step("vo"))
                yield
                after(md, "wca")
                a.activation(wi, wia, ACT.Exp).then_inc(*ma.step("wi"))
                a.activation(wc, wca, ACT.Exp).then_inc(*ma.step("wc"))
                after(md, "e3")
                a.activation(E, E, ACT.Exp).then_inc(*ma.step("e"))
                after(md, "iwa")
                a.activation(IW, IW, ACT.Exp).then_inc(*ma.step("iw"))
                yield
                yield
                after(mp, "den")
                a.activation(HD, bk(3), ACT.Abs).then_inc(*ma.step("abs"))
                yield
                yield
                after(md, "yc")
                a.activation(E, HB, ACT.Square).then_inc(*ma.step("ysq"))
                yield
                after(mp, "var")
                a.activation(HD, bk(0), ACT.Sqrt, bias=GN_EPS).then_inc(*ma.step("ysd"))
                yield
                yield

        def pe_mlstm(pe):
            sel = lambda h: C("sel", h * P, P)[0:4]
            for g in range(NG):
                def after(steps, name, back=0):
                    pe.wait_ge(*steps.at(name, g - back))
                if g:
                    after(ma, "ysd", 1)
                for h in range(4):
                    mm = pe.matmul(bk(0)[:, h, :], sel(h), nmrow[0:4, ds(L * g, L)], start=True, stop=True)
                mm.then_inc(*mp.step("nm"))
                for h in range(4):
                    mm = pe.matmul(bk(1)[:, h, :], sel(h), nmtrow[0:4, ds(L * g, L)], start=True, stop=True)
                mm.then_inc(*mp.step("nb"))
                after(ma, "v")
                for h in range(4):
                    pe.transpose(bk(2)[:, h, :], kS[:, h, :], C("ident"))
                    mm = pe.transpose(bk(3)[:, h, :], vS2[:, h, :], C("ident"))
                mm.then_inc(*mp.step("rows"))
                after(ma, "en")
                for h in range(4):
                    mm = pe.matmul(bk(1)[:, h, :], kS[:, h, :], ub[:, h, ds(L * g, L)], start=True, stop=True)
                mm.then_inc(*mp.step("sc"))
                yield
                yield
                after(md, "qi")
                after(ma, "vo")
                pe.wait_ge(s_mz, 3)
                for h in range(4):
                    pe.matmul(bk(3)[:, h, :], C("ones"), PT[:, h, :], start=True, stop=False)
                    mm = pe.matmul(bk(3)[:, h, :], cn[:, h, P:2 * P], QI[:, h, :], start=False, stop=True)
                mm.then_inc(*mp.step("den"))
                for h in range(4):
                    pe.matmul(bk(0)[:, h, :], vo[:, h, 0:P], PT[:, h, :], start=True, stop=False)
                    mm = pe.matmul(bk(0)[:, h, :], cn[:, h, 0:P], QI[:, h, :], start=False, stop=True)
                mm.then_inc(*mp.step("num"))
                for h in range(4):
                    mm = pe.matmul(ps[:, 1 + h // 2, 256 * (h % 2):256 * (h % 2) + 256], KH[:, h, :], vo[:, h, :],
                                   start=True, stop=True)
                mm.then_inc(*mp.step("st"))
                yield
                yield
                after(md, "ho")
                pe.matmul(bk(3), C("mean128"), HB, start=True, stop=True).then_inc(*mp.step("mean"))
                yield
                after(ma, "ysq")
                pe.matmul(bk(0), C("mean128"), E, start=True, stop=True).then_inc(*mp.step("var"))
                yield
                yield
                yield

        r3 = r2
        vm3 = r3.take(NS, P)
        rows2 = r3.take(2, 4, P)
        n_new, khs, qn, hs, dn, ys = [r3.take(4, NS) for _ in range(6)]
        sb3 = r3.take(4, 24)
        cst = slot[1][:, :].rearrange("p (h s n) -> p h s n", h=4, s=NS)
        m1_sem = {k: sem(f"mlstm1_{k}") for k in ("pe", "dve", "act")}
        nd = Steps(m1_sem["dve"], ["kh", "nw", "n", "qn"])
        ndj = Steps(m1_sem["dve"], ["vm", "cw", "c"], 4)
        nd2 = Steps(m1_sem["dve"], ["dn", "dr", "h", "ho", "yc", "rinv", "yn", "out"], 4 + 12)
        na = Steps(m1_sem["act"], ["exp", "bc", "rows", "abs", "ysq", "ysd"])
        np_ = Steps(m1_sem["pe"], ["bc", "rows", "qn"])
        npj = Steps(m1_sem["pe"], ["outer"], 3)
        np2 = Steps(m1_sem["pe"], ["num", "mean", "var"], 3 + 4)
        ubs = lambda arr: ub[:, arr:arr + 4, TP:]
        p32 = lambda b: ps[:, b, 0:32].rearrange("p (h s) -> p h s", h=4)

        def dve_mlstm1(dve):
            v = nc.vector

            def after(steps, name, it=0):
                dve.wait_ge(*steps.at(name, it))
            yield
            after(na, "bc")
            iw, wi1, en1 = [sb3[:, :, 8 * k:8 * k + 8] for k in range(3)]
            v.scalar_tensor_tensor(khs, ubs(4), BHD ** -0.5, wi1, ALU.mult, ALU.mult).then_inc(*nd.step("kh"))
            v.tensor_tensor(n_new, V("n", 0, 32).rearrange("p (h s) -> p h s", h=4), iw,
                            ALU.mult).then_inc(*nd.step("nw"))
            after(nd, "nw")
            v.tensor_tensor(n_new, n_new, khs, ALU.add).then_inc(*nd.step("n"))
            after(nd, "n")
            v.tensor_tensor(qn, n_new, ubs(0), ALU.mult).then_inc(*nd.step("qn"))
            yield
            after(na, "rows")
            dve.wait_ge(s_cst, 16)
            for h in range(4):
                if h:
                    after(npj, "outer", h - 1)
                v.tensor_tensor(vm3[0:NS], mid(rows2[0:NS, 1, h, :], NS), bc(eight, P),
                                ALU.mult).then_inc(*ndj.step("vm"))
                v.tensor_tensor(cst[:, h], cst[:, h], bc(iw[:, h, :], P), ALU.mult).then_inc(*ndj.step("cw"))
                yield
                after(ndj, "cw", h)
                after(npj, "outer", h)
                v.tensor_tensor(cst[:, h], cst[:, h],
                                ps[:, 4:6, :].rearrange("p q (s n) -> p (q s) n", n=P),
                                ALU.add).then_inc(*ndj.step("c"))
                yield
            after(na, "abs")
            v.tensor_tensor(dn, dn, en1, ALU.max).then_inc(*nd2.step("dn"))
            after(nd2, "dn")
            v.reciprocal(dn, dn).then_inc(*nd2.step("dr"))
            after(nd2, "dr")
            after(np2, "num")
            v.tensor_tensor(hs, p32(6), dn, ALU.mult).then_inc(*nd2.step("h"))
            after(nd2, "h")
            v.tensor_tensor(hs, hs, ubs(12), ALU.mult).then_inc(*nd2.step("ho"))
            yield
            after(np2, "mean")
            v.tensor_tensor(hs, hs, p32(7), ALU.subtract).then_inc(*nd2.step("yc"))
            yield
            after(na, "ysd")
            v.reciprocal(dn, dn).then_inc(*nd2.step("rinv"))
            after(nd2, "rinv")
            v.tensor_tensor(hs, hs, dn, ALU.mult).then_inc(*nd2.step("yn"))
            after(nd2, "yn")
            v.tensor_tensor(ubs(0), hs, bc(V("mgn", 0, 4), NS), ALU.mult).then_inc(*nd2.step("out"))
            yield

        def act_mlstm1(act):
            a = nc.scalar

            def after(steps, name, it=0):
                act.wait_ge(*steps.at(name, it))
            act.wait_ge(*row_d.at("en"))
            a.activation(sr[0:4], sr[0:4], ACT.Exp).then_inc(*na.step("exp"))
            after(np_, "bc")
            a.activation(sb3, ps[:, 4, 0:96].rearrange("p (h n) -> p h n", h=4), ACT.Copy).then_inc(*na.step("bc"))
            yield
            after(np_, "rows")
            a.activation(rows2[0:NS].rearrange("p k h n -> p k (h n)"), ps[0:NS, 5:7, :],
                         ACT.Copy).then_inc(*na.step("rows"))
            yield
            for _ in range(8):
                yield
            after(np_, "qn")
            a.activation(dn, p32(7), ACT.Abs).then_inc(*na.step("abs"))
            yield
            after(nd2, "yc")
            a.activation(ys, hs, ACT.Square).then_inc(*na.step("ysq"))
            after(np2, "var")
            a.activation(dn, p32(4), ACT.Sqrt, bias=GN_EPS).then_inc(*na.step("ysd"))
            yield
            yield

        def pe_mlstm1(pe):
            def after(steps, name, it=0):
                pe.wait_ge(*steps.at(name, it))
            flat = lambda x: x.rearrange("p j t -> p (j t)")
            after(sd2, "out")
            after(na, "exp")
            for h in range(4):
                mm = pe.matmul(ps[:, 4, 24 * h:24 * h + 24], C("sel", h * P, P)[0:4], sr[0:4, :],
                               start=True, stop=True)
            mm.then_inc(*np_.step("bc"))
            yield
            after(nd, "kh")
            for h in range(4):
                pe.transpose(ps[0:NS, 5, h * P:(h + 1) * P], khs[:, h, :], C("ident"))
                mm = pe.transpose(ps[0:NS, 6, h * P:(h + 1) * P], ubs(8)[:, h, :], C("ident"))
            mm.then_inc(*np_.step("rows"))
            after(nd, "qn")
            pe.matmul(ps[:, 7, 0:32], C("ones"), flat(qn), start=True, stop=True).then_inc(*np_.step("qn"))
            yield
            after(na, "rows")
            for h in range(4):
                after(ndj, "vm", h)
                if h:
                    after(ndj, "c", h - 1)
                for q in range(2):
                    mm = pe.matmul(ps[:, 4 + q, :], rows2[0:NS, 0, h, :],
                                   vm3[0:NS, 4 * q:4 * q + 4, :], start=True, stop=True)
                mm.then_inc(*npj.step("outer"))
                yield
                yield
            after(ndj, "c", 3)
            for h in range(4):
                for b in range(NS):
                    mm = pe.matmul(ps[:, 6, NS * h + b:NS * h + b + 1], cst[:, h, b, :],
                                   ub[:, h, TP + b:TP + b + 1], start=True, stop=True)
            mm.then_inc(*np2.step("num"))
            after(nd2, "ho")
            pe.matmul(ps[:, 7, 0:32], C("mean128"), flat(hs), start=True, stop=True).then_inc(*np2.step("mean"))
            yield
            after(na, "ysq")
            pe.matmul(ps[:, 4, 0:32], C("mean128"), flat(ys), start=True, stop=True).then_inc(*np2.step("var"))
            yield
            yield

        def one_step(first, second):
            yield from first
            yield from second

        s_ev, s_sub, s_shf = sem("in_evacuated"), sem("shift_difference"), sem("shift_mixed")
        s_raw = sem("raw_saved")
        s_tn, s_lp, s_lc = sem("lora_inputs"), sem("lora_products"), sem("lora_outputs")
        s_cv, s_cvd = sem("convolution_step"), sem("silu_done")
        s_zc = sem("zero_column")
        acc = [sqr[0], sqr[1]]
        RD = ["i", "ib", "f", "fb", "abs", "lf", "zero", "b", "c", "m", "nm", "nmt", "mo", "t", "tm", "iw", "wi",
              "en", "ct"]
        row_d, row_a, row_p = (Steps(sem(f"rows_{k}"), n) for k, n in
                               [("dve", RD), ("act", ["gate", "exp", "ln"]), ("pe", ["if", "ct"])])

        def dve_in0(dve):
            v = nc.vector
            v.memset(ua[:, :, 0:1], 0.0).then_inc(s_zc, 1)
            dve.wait_ge(s_zc, 1)
            dve.wait_ge(s_vec, 16)
            def shifted(m, i=0):
                t, s = 4 * i + m, m % 2
                dve.wait_ge(s_tile, t + 1)
                v.tensor_tensor(two(ua[:, ds(t, 1), 1:].squeeze(1)), bank(s), two(rb), ALU.mult).then_inc(s_bank, 1)
                dve_low(dve, 0, m + 2, i)
                dve.wait_ge(s_bank, t + 3)
                dve.wait_ge(s_shf, t + 1)
                v.tensor_tensor(tmp[0][:, 0:TP], ua[:, ds(t, 1), 0:TP].squeeze(1),
                                ua[:, ds(t, 1), 1:TP + 1].squeeze(1), ALU.subtract)
                v.tensor_tensor(tmp[0][:, TP:], vec[:, ds(VEC["shift"][0] + NS * t, NS)],
                                ua[:, ds(t, 1), TP + 1:].squeeze(1), ALU.subtract).then_inc(s_sub, 1)
                dve.wait_ge(s_sub, t + 1)
                dve.wait_ge(s_raw, t + 1)
                v.scalar_tensor_tensor(ua[:, ds(t, 1), 1:].squeeze(1), tmp[0], vec[:, ds(VEC["mu"][0] + t, 1)],
                                       ua[:, ds(t, 1), 1:].squeeze(1), ALU.mult, ALU.add).then_inc(s_shf, 1)
            with dve.Fori(0, NA // 4) as i:
                for m in range(4):
                    shifted(m, i)
            for m in range(NA - NA % 4, NA):
                shifted(m)
            with dve.Fori(0, 2) as i:
                for m in range(4):
                    t, s = 4 * i + m, m % 2
                    u = lambda a, b: ub[:, ds(t, 1), a:b].squeeze(1)
                    dve.wait_ge(s_tile, t + NA + 1)
                    v.tensor_tensor(two(u(0, T)), bank(s), two(rb), ALU.mult).then_inc(s_bank, 1)
                    dve.wait_ge(s_bank, t + NA + 3)
                    dve.wait_ge(s_cvd, t + 1)
                    w = lambda j: vec[:, ds(VEC["cw"][0] + 8 * j + t, 1)]
                    o = acc[s]
                    v.tensor_scalar(o, u(0, T), w(3), vec[:, ds(VEC["cb"][0] + t, 1)], ALU.mult,
                                    ALU.add).then_inc(s_cv, 1)
                    for k in range(1, 4):
                        dve.wait_ge(s_cv, 4 * t + k)
                        v.scalar_tensor_tensor(o[:, TP:], vec[:, ds(VEC["conv"][0] + 24 * t + 8 * (3 - k), 8)],
                                               w(3 - k), o[:, TP:], ALU.mult, ALU.add)
                        v.scalar_tensor_tensor(o[:, k:TP], u(0, TP - k), w(3 - k), o[:, k:TP],
                                               ALU.mult, ALU.add).then_inc(s_cv, 1)
                        if k == 1:
                            dve_low(dve, 0, NA + m + 2, i)
            with dve.Fori(0, 2) as i:
                for m in range(4):
                    t = 4 * i + m
                    dve.wait_ge(s_tile, t + NA + 8 + 1)
                    v.tensor_tensor(two(ub[:, ds(t + 8, 1), :].squeeze(1)), bank(m % 2), two(rb),
                                    ALU.mult).then_inc(s_bank, 1)
                    dve_low(dve, 0, NA + 8 + m + 2, i)
            def after(steps, name):
                dve.wait_ge(*steps.at(name))
            ir, fr, er, zr = hbuf[0][0:4, 1024:1024 + T], hbuf[0][0:4, 2048:2048 + T], hbuf[0][0:4, 3072:3072 + T], \
                hbuf[0][0:4, 3600:3600 + TP]
            cr, nr, tr = crow[0:4], nmrow[0:4], nmtrow[0:4]
            after(row_p, "if")
            v.tensor_tensor(two(ir), ps[0:4, 6:8, 0:HALF], two(rb[0:4]), ALU.mult).then_inc(*row_d.step("i"))
            after(row_d, "i")
            v.tensor_scalar(ir, ir, V("ib")[0:4], None, ALU.add).then_inc(*row_d.step("ib"))
            v.tensor_tensor(two(fr), ps[32:36, 6:8, 0:HALF], two(rb[32:36]), ALU.mult).then_inc(*row_d.step("f"))
            after(row_d, "f")
            v.tensor_scalar(fr, fr, V("fb")[0:4], None, ALU.add).then_inc(*row_d.step("fb"))
            after(row_d, "fb")
            v.scalar_tensor_tensor(er, fr, -1.0, fr, ALU.mult, ALU.max).then_inc(*row_d.step("abs"))
            after(row_a, "ln")
            v.scalar_tensor_tensor(fr, fr, 0.0, er, ALU.min, ALU.subtract).then_inc(*row_d.step("lf"))
            v.memset(zr, 0.0).then_inc(*row_d.step("zero"))
            after(row_d, "zero")
            v.tensor_tensor_scan(er[:, 0:TP], fr[:, 0:TP], zr, 0.0, ALU.add, ALU.add).then_inc(*row_d.step("b"))
            after(row_d, "b")
            v.tensor_tensor(cr[:, 0:TP], ir[:, 0:TP], er[:, 0:TP], ALU.subtract).then_inc(*row_d.step("c"))
            after(row_d, "c")
            v.tensor_tensor_scan(tr[:, 0:TP], cr[:, 0:TP], cr[:, 0:TP], 0.0, ALU.max,
                                 ALU.max).then_inc(*row_d.step("m"))
            after(row_d, "m")
            v.tensor_scalar(nr[:, 0:TP], tr[:, 0:TP], -1.0, None, ALU.mult).then_inc(*row_d.step("nm"))
            v.scalar_tensor_tensor(tr[:, 0:TP], er[:, 0:TP], -1.0, tr[:, 0:TP], ALU.mult,
                                   ALU.subtract).then_inc(*row_d.step("nmt"))
            after(row_d, "nmt")
            v.tensor_scalar(mo[0:4, 0:1], tr[:, TP - 1:TP], -1.0, None, ALU.mult).then_inc(*row_d.step("mo"))
            t_, m_ = zr[:, 0:NS], mo[0:4, 1:]
            v.tensor_tensor(t_, fr[:, TP:], V("m", 0, NS)[0:4], ALU.add).then_inc(*row_d.step("t"))
            after(row_d, "t")
            v.tensor_tensor(m_, t_, ir[:, TP:], ALU.max).then_inc(*row_d.step("tm"))
            after(row_d, "tm")
            v.tensor_tensor(sr[0:4, 0:8], t_, m_, ALU.subtract).then_inc(*row_d.step("iw"))
            v.tensor_tensor(sr[0:4, 8:16], ir[:, TP:], m_, ALU.subtract).then_inc(*row_d.step("wi"))
            v.tensor_scalar(sr[0:4, 16:24], m_, -1.0, None, ALU.mult).then_inc(*row_d.step("en"))
            after(row_d, "en")
            after(row_p, "ct")
            v.tensor_copy(ct, ps[:, 4, 0:16]).then_inc(*row_d.step("ct"))
            after(row_d, "ct")

        def pool_in0(pool):
            with pool.Fori(0, NA // 2) as i:
                for s in range(2):
                    t = 2 * i + s
                    pool.wait_ge(s_bank, t + 3)
                    nc.gpsimd.tensor_copy(sho[:, ds(t, 1), :].squeeze(1),
                                          ua[:, ds(t, 1), TP:].squeeze(1)).then_inc(s_raw, 1)
            with pool.Fori(0, 4) as i:
                for s in range(2):
                    t = 2 * i + s
                    pool.wait_ge(s_bank, t + NA + 3)
                    nc.gpsimd.tensor_copy(cvo[:, ds(t, 1), :].squeeze(1),
                                          ub[:, ds(t, 1), TP - 3:].squeeze(1)).then_inc(s_raw, 1)

        def act_in0(act):
            a = nc.scalar
            act.wait_ge(s_vec, 16)
            with act.Fori(0, NA // 4) as i:
                for m in range(4):
                    act_high(act, 0, m + 2, i, (s_tile, (m + 1) + 4 * i))
            for m in range(NA - NA % 4, NA):
                act_high(act, 0, m + 2, 0, (s_tile, m + 1))
            act.wait_ge(s_shf, NA + 1)
            a.activation(ua[0:64, 12, 1:], ua[0:64, 12, 1:], ACT.Tanh).then_inc(s_tn, 1)
            a.activation(ua[:, 13, 1:], ua[:, 13, 1:], ACT.Sigmoid).then_inc(s_tn, 1)
            with act.Fori(0, 2) as i:
                for m in range(4):
                    t = 4 * i + m
                    act_high(act, 0, NA + m + 2, i, (s_tile, (NA + m + 1) + 4 * i))
                    act.wait_ge(s_cv, 4 * t + 4)
                    act.wait_ge(s_raw, t + 15)
                    a.activation(ub[:, ds(t, 1), :].squeeze(1), acc[m % 2], ACT.Silu).then_inc(s_cvd, 1)
            with act.Fori(0, 2) as i:
                for m in range(4):
                    act_high(act, 0, NA + 8 + m + 2, i, (s_tile, (NA + 8 + m + 1) + 4 * i))
            er = hbuf[0][0:4, 3072:3072 + T]
            act.wait_ge(s_bank, NA + NB + 2)
            a.activation(ub[:, 12:16, :], ub[:, 12:16, :], ACT.Sigmoid).then_inc(*row_a.step("gate"))
            for k in range(12):
                act.wait_ge(s_lp, k + 1)
                src = ps[:, 4 + 2 * (k % 2):6 + 2 * (k % 2), 0:HALF]
                j = k % 4
                if k < 4:
                    a.activation(two(sig[:, j, :]), src, ACT.Sigmoid, bias=V("w0", j)).then_inc(s_lc, 1)
                elif k < 8:
                    a.activation(two(aa[:, j, :]), src, ACT.Sigmoid, bias=V("a0", j)).then_inc(s_lc, 1)
                else:
                    a.activation(two(gg[:, j, :]), src, ACT.Copy).then_inc(s_lc, 1)
            act.wait_ge(*row_d.at("abs"))
            a.activation(er, er, ACT.Exp, scale=-1.0).then_inc(*row_a.step("exp"))
            act.wait_ge(*row_a.at("exp"))
            a.activation(er, er, ACT.Ln, bias=1.0).then_inc(*row_a.step("ln"))

        def pe_in0(pe):
            pe.wait_ge(s_con, 16)
            pe.wait_ge(s_vec, 16)
            for kt in range(KD):
                for hf in range(2):
                    for x in (xh, xl):
                        mm = pe.matmul(ps[0:36, 6 + hf, 0:HALF], V("wif", 36 * kt, 36),
                                       x[:, kt, hf * HALF:(hf + 1) * HALF].bitcast(F32),
                                       start=(kt == 0 and x is xh), stop=(kt == KD - 1 and x is xl))
            mm.then_inc(*row_p.step("if"))
            pe.wait_ge(s_tn, 2)
            for k in range(12):
                j = k % 4
                if k == 0:
                    pe.wait_ge(s_rt, 1)
                if k == 1:
                    pe.wait_ge(*row_d.at("f"))
                if k >= 2:
                    pe.wait_ge(s_lc, k - 1)
                w = (V("w2a2", j * P, P)[0:64] if k < 4 else V("w2a2", j * P, P)[64:P] if k < 8 else V("g2", j * P, P))
                for hf in range(2):
                    cols = slice(1 + hf * HALF, 1 + hf * HALF + HALF)
                    x = ua[0:64, 12, cols] if k < 4 else ua[64:P, 12, cols] if k < 8 else ua[:, 13, cols]
                    mm = pe.matmul(ps[:, 4 + 2 * (k % 2) + hf, 0:HALF], w, x, start=True, stop=True)
                mm.then_inc(s_lp, 1)
            pe.wait_ge(s_lc, 11)
            pe.wait_ge(*row_d.at("c"))
            for g in range(NG):
                mm = pe.transpose(ps[:, 4, 4 * g:4 * g + 4], crow[0:4, g * P:(g + 1) * P], C("ident")[0:4, 0:4])
            mm.then_inc(*row_p.step("ct"))
            pe.wait_ge(s_lc, 12)

        h1 = hb[1]
        r4_ = Space([hbuf[0][:, :], pjw[:, :], free[:, :], spare[:, :], slot[1][:, :]])
        rS = r4_.take(4, 2, CDV)
        vrow = [r4_.take(CDV) for _ in range(4)]
        vm1 = [r4_.take(CDV) for _ in range(2)]
        ks = r4_.take(8, NS)
        kR, QD = r4_.take(2, P), r4_.take(2, P)
        vR, YC, YQ, YB = [r4_.take(4, P) for _ in range(4)]
        kTk, vTk = r4_.take(2 * P), r4_.take(CDV)
        PR, RI = r4_.take(P), r4_.take(P)
        ys1, yc1, yq1 = [r4_.take(16, NS) for _ in range(3)]
        ri1 = r4_.take(4, NS)
        ring = [r4_.take(2, CDV) for _ in range(4)]
        s_rin = [sem(f"ret_state_loaded{i}") for i in range(4)]
        s_prs = sem("prompt_ret_stored")
        s_up, s_read = sem("sample_ret_updated"), sem("sample_ret_read")
        rp_x, s_rope, s_pair = [tmp[0], tmp[1], sqr[0], sqr[1]], sem("rope_step"), sem("rope_pair")
        def by_head(names, last):
            heads = [f"{n[1:]}{h - 1}" if n[0] == "-" else f"{n}{h}"
                     for h in range(CH) for n in names if h or n[0] != "-"]
            return heads + [f"{n}{CH - 1}" for n in last]
        re = part("ret", dict(
            pe=by_head(["sc", "vr", "-mean", "o", "-var", "v0", "v1", "st"], ["mean", "var"]),
            dve=by_head(["kt", "pt", "qd", "-yc", "-ri", "-yn", "-out", "s"],
                        ["yc", "ri", "yn", "out"]),
            act=by_head(["k", "v", "vt", "vm0", "vm1", "-ysq", "y", "-sd", "dec0", "dec1"], ["ysq", "sd"])))
        ep, ed, ea = re["pe"], re["dve"], re["act"]
        s_rz = sem("ret_zeroed")
        e1 = {k: sem(f"ret1_{k}") for k in ("pe", "dve", "act")}
        ep1 = Steps(e1["pe"], ["vrows"])
        ep2 = Steps(e1["pe"], ["mean", "var"], 1)
        ed2 = Steps(e1["dve"], ["yc", "ri", "yn", "out"])
        ea1 = Steps(e1["act"], ["ks", "vrows", "y", "ysq", "sd"])

        def dve_qkv(dve):
            v = nc.vector
            t0, base = GEMMS["qkv"][1], CHUNKS["qkv"]
            with dve.Fori(0, 4) as i:
                for pair in range(2):
                    x1, x2, p1, p2 = rp_x
                    t = t0 + 2 * pair
                    n = 8 * pair
                    dve.wait_ge(s_tile, (t + 1) + 4 * i)
                    dve.wait_ge(s_rope, 16 * i + (n + 1))
                    v.tensor_tensor(two(x1), bank(0), two(rb), ALU.mult).then_inc(s_bank, 1)
                    dve_low(dve, base, 2 * pair + 2, i)
                    dve.wait_ge(s_tile, (t + 2) + 4 * i)
                    v.tensor_tensor(two(x2), bank(1), two(rb), ALU.mult).then_inc(s_bank, 1)
                    dve.wait_ge(s_bank, (t + 4) + 4 * i)
                    dve_low(dve, base, 2 * pair + 3, i)
                    y = lambda k: hid[:, ds(4 * i + (2 * pair + k), 1), :].squeeze(1)
                    v.tensor_tensor(p1, x1, C("cos"), ALU.mult).then_inc(s_rope, 1)
                    v.tensor_tensor(p2, x2, C("sin"), ALU.mult).then_inc(s_rope, 1)
                    dve.wait_ge(s_rope, 16 * i + (n + 3))
                    v.tensor_tensor(y(0), p1, p2, ALU.subtract).then_inc(s_rope, 1)
                    dve.wait_ge(s_rope, 16 * i + (n + 4))
                    v.tensor_tensor(p1, x1, C("sin"), ALU.mult).then_inc(s_rope, 1)
                    v.tensor_tensor(p2, x2, C("cos"), ALU.mult).then_inc(s_rope, 1)
                    dve.wait_ge(s_rope, 16 * i + (n + 6))
                    v.tensor_tensor(y(1), p1, p2, ALU.add).then_inc(s_rope, 1)
                    dve.wait_ge(s_rope, 16 * i + (n + 7))
                    v.memset(PR[:, 0:1], 0.0).then_inc(s_rope, 2)

            def values(i, last=False):
                for m in range(4):
                    dve.wait_ge(s_tile, (t0 + 16 + m + 1) + 4 * i)
                    v.tensor_tensor(two(hid[:, ds(4 * i + (16 + m), 1), :].squeeze(1)), bank(m % 2), two(rb),
                                    ALU.mult).then_inc(s_bank, 1)
                    if not last or m < 2:
                        dve_low(dve, base, 16 + m + 2, i)
            with dve.Fori(0, 3) as i:
                values(i)
            values(3, True)
            v.memset(rS, 0.0).then_inc(s_rz, 1)
            dve.wait_ge(s_rz, 1)

        def hg(tile, n, g):
            return hid[:, tile:tile + n, ds(L * g, L)]

        def dve_ret(dve):
            v = nc.vector
            with dve.Fori(0, NG) as g:
                def after(steps, name):
                    dve.wait_ge(*steps.at(name, g))

                def sample(h, n):
                    x = 2 * (h % 2) + n
                    after(ep, f"v{n}{h}")
                    after(ea, f"dec{n}{h}")
                    for k in range(2):
                        up = v.scalar_tensor_tensor(ring[x][:, k, :], ps[:, 6 + n, :],
                                                    ks[:, 2 * h + k, ds(2 * g + n, 1)], ring[x][:, k, :],
                                                    ALU.mult, ALU.add)
                    up.then_inc(s_up, 1)

                def center(h):
                    after(ep, f"mean{h}")
                    v.tensor_tensor(YC, YB, mid(ps[:, 4, 0:P], 4), ALU.subtract).then_inc(*ed.step(f"yc{h}"))

                def scale(h):
                    after(ea, f"sd{h}")
                    v.reciprocal(RI, RI).then_inc(*ed.step(f"ri{h}"))
                    after(ed, f"ri{h}")
                    v.tensor_tensor(YC, YC, mid(RI, 4), ALU.mult).then_inc(*ed.step(f"yn{h}"))
                    after(ed, f"yn{h}")
                    v.tensor_tensor(hg(16 + 4 * h, 4, g), YC, bc(V("rgn", 4 * h, 4), P),
                                    ALU.mult).then_inc(*ed.step(f"out{h}"))

                for h in range(CH):
                    after(ep, f"sc{h}")
                    v.tensor_scalar(kTk, ps[:, 0, 0:256], C("kdec", h, 1), None, ALU.mult).then_inc(*ed.step(f"kt{h}"))
                    v.tensor_tensor(PR, ps[:, 0, 256:384], C("rmask", h * P, P), ALU.mult).then_inc(*ed.step(f"pt{h}"))
                    v.tensor_tensor(QD, hg(2 * h, 2, g), mid(C("qdec", h * P, P), 2),
                                    ALU.mult).then_inc(*ed.step(f"qd{h}"))
                    if h:
                        center(h - 1)
                        scale(h - 1)
                    sample(h, 0)
                    after(ep, f"st{h}")
                    v.scalar_tensor_tensor(rS[:, h], rS[:, h], CDEC_CHUNK[h], ps[:, 4:6, :], ALU.mult,
                                           ALU.add).then_inc(*ed.step(f"s{h}"))
                    sample(h, 1)
                center(CH - 1)
                scale(CH - 1)

        def act_ret(act):
            a = nc.scalar
            act.wait_ge(s_bank, GEMMS["qkv"][1] + 34)
            act.wait_ge(s_rope, 65)
            a.activation(ks, hid[:, 8:16, TP:], ACT.Copy, scale=CDK ** -0.5).then_inc(*ea1.step("ks"))
            act.wait_ge(*ep1.at("vrows"))
            for k in range(3):
                a.activation(vrow[k][0:NS], ps[0:NS, 2 + k, :], ACT.Copy)
            a.activation(vrow[3][0:NS], ps[0:NS, 5, :], ACT.Copy).then_inc(*ea1.step("vrows"))
            with act.Fori(0, NG) as g:
                def after(steps, name):
                    act.wait_ge(*steps.at(name, g))

                def square(h):
                    after(ed, f"yc{h}")
                    a.activation(YQ, YC, ACT.Square).then_inc(*ea.step(f"ysq{h}"))

                def deviation(h):
                    after(ep, f"var{h}")
                    a.activation(RI, ps[:, 1, 0:P], ACT.Sqrt, bias=GN_EPS).then_inc(*ea.step(f"sd{h}"))

                for h in range(CH):
                    a.activation(kR, hg(8 + 2 * h, 2, g), ACT.Copy, scale=CDK ** -0.5).then_inc(*ea.step(f"k{h}"))
                    a.activation(vR, hg(16 + 4 * h, 4, g), ACT.Copy).then_inc(*ea.step(f"v{h}"))
                    after(ep, f"vr{h}")
                    a.activation(vTk, ps[:, 1, :], ACT.Copy).then_inc(*ea.step(f"vt{h}"))
                    for n in range(2):
                        a.activation(vm1[n][0:NS], vrow[h][0:NS], ACT.Copy,
                                     scale=con[0:NS, ds(CON["ident"][0] + n + 2 * g, 1)]).then_inc(*ea.step(f"vm{n}{h}"))
                    if h:
                        square(h - 1)
                    after(ep, f"o{h}")
                    a.activation(YB, bk(3), ACT.Copy).then_inc(*ea.step(f"y{h}"))
                    if h:
                        deviation(h - 1)
                    for n in range(2):
                        x = 2 * (h % 2) + n
                        act.wait_ge(s_rin[x], (16 * (h // 2) + 16) + 32 * g)
                        a.activation(ring[x], ring[x], ACT.Copy, scale=CDEC_ONE[h]).then_inc(*ea.step(f"dec{n}{h}"))
                square(CH - 1)
                deviation(CH - 1)

        def pe_ret(pe):
            pe.wait_ge(s_bank, GEMMS["qkv"][1] + 34)
            pe.wait_ge(s_rope, 65)
            for e in range(16):
                mm = pe.transpose(ps[0:NS, 2 + e // 4, (e % 4) * P:(e % 4 + 1) * P], hid[:, 16 + e, TP:], C("ident"))
            mm.then_inc(*ep1.step("vrows"))
            pe.wait_ge(s_rz, 1)
            pe.wait_ge(*ea1.at("vrows"))
            with pe.Fori(0, NG) as g:
                def after(steps, name):
                    pe.wait_ge(*steps.at(name, g))

                def broadcast(h, n):
                    after(ea, f"vm{n}{h}")
                    pe.matmul(ps[:, 6 + n, :], C("ones")[0:NS], vm1[n][0:NS], start=True,
                              stop=True).then_inc(*ep.step(f"v{n}{h}"))

                def o_product(h, n):
                    pe.wait_ge(s_up, (2 * h + n + 1) + 8 * g)
                    for e in range(4):
                        for k in range(2):
                            mm = pe.matmul(ps[:, 2, ds((4 * NS * h + NS * e + n) + 2 * g, 1)],
                                           ring[2 * (h % 2) + n][:, k, e * P:(e + 1) * P],
                                           hid[:, 2 * h + k, ds((TP + n) + 2 * g, 1)],
                                           start=(k == 0), stop=(k == 1), skip_group_check=True)
                    mm.then_inc(s_read, 1)

                def mean(h):
                    after(ea, f"y{h}")
                    for e in range(4):
                        mm = pe.matmul(ps[:, 4, 0:P], C("mean512"), YB[:, e, :], start=(e == 0), stop=(e == 3))
                    mm.then_inc(*ep.step(f"mean{h}"))

                def var(h):
                    after(ea, f"ysq{h}")
                    for e in range(4):
                        mm = pe.matmul(ps[:, 1, 0:P], C("mean512"), YQ[:, e, :], start=(e == 0), stop=(e == 3))
                    mm.then_inc(*ep.step(f"var{h}"))

                for h in range(CH):
                    after(ea, f"k{h}")
                    for k in range(2):
                        pe.transpose(ps[:, 0, k * P:(k + 1) * P], kR[:, k, :], C("ident"))
                    for k in range(2):
                        mm = pe.matmul(ps[:, 0, 256:384], kR[:, k, :], hid[:, 2 * h + k, ds(L * g, L)],
                                       start=(k == 0), stop=(k == 1))
                    mm.then_inc(*ep.step(f"sc{h}"))
                    after(ea, f"v{h}")
                    for e in range(4):
                        mm = pe.transpose(bk(1)[:, e, :], vR[:, e, :], C("ident"))
                    mm.then_inc(*ep.step(f"vr{h}"))
                    if h:
                        o_product(h - 1, 1)
                        mean(h - 1)
                    after(ea, f"vt{h}")
                    after(ed, f"qd{h}")
                    for e in range(4):
                        pe.matmul(bk(3)[:, e, :], vTk[:, e * P:(e + 1) * P], PR, start=True, stop=False)
                        for k in range(2):
                            mm = pe.matmul(bk(3)[:, e, :], rS[:, h, k, e * P:(e + 1) * P], QD[:, k, :],
                                           start=False, stop=(k == 1))
                    mm.then_inc(*ep.step(f"o{h}"))
                    if h:
                        var(h - 1)
                    broadcast(h, 0)
                    broadcast(h, 1)
                    for k in range(2):
                        mm = pe.matmul(ps[:, 4 + k, :], kTk[:, k * P:(k + 1) * P], vTk, start=True, stop=True)
                    mm.then_inc(*ep.step(f"st{h}"))
                    o_product(h, 0)
                o_product(CH - 1, 1)
                mean(CH - 1)
                var(CH - 1)

        def dve_ret1(dve):
            v = nc.vector

            def after(steps, name):
                dve.wait_ge(*steps.at(name))
            after(ep2, "mean")
            four = lambda x: x.rearrange("p (h e) s -> p h e s", h=4)
            b4 = lambda x: x.unsqueeze(2).to_broadcast([P, 4, 4, NS])
            mean = ps[:, 4, 0:32].rearrange("p (h s) -> p h s", h=4)
            v.tensor_tensor(four(yc1), four(ys1), b4(mean), ALU.subtract).then_inc(*ed2.step("yc"))
            after(ea1, "sd")
            v.reciprocal(ri1, ri1).then_inc(*ed2.step("ri"))
            after(ed2, "ri")
            v.tensor_tensor(four(yc1), four(yc1), b4(ri1), ALU.mult).then_inc(*ed2.step("yn"))
            after(ed2, "yn")
            v.tensor_tensor(hid[:, 16:32, TP:], yc1, bc(V("rgn", 0, 16), NS), ALU.mult).then_inc(*ed2.step("out"))
            after(ed2, "out")

        def act_ret1(act):
            a = nc.scalar
            act.wait_ge(*ep.at("var3", NG - 1))
            a.activation(ys1, ps[:, 2, 0:P].rearrange("p (k s) -> p k s", s=NS), ACT.Copy).then_inc(*ea1.step("y"))
            act.wait_ge(*ed2.at("yc"))
            a.activation(yq1, yc1, ACT.Square).then_inc(*ea1.step("ysq"))
            act.wait_ge(*ep2.at("var"))
            a.activation(ri1, ps[:, 5, 0:32].rearrange("p (h s) -> p h s", h=4), ACT.Sqrt,
                         bias=GN_EPS).then_inc(*ea1.step("sd"))

        def pe_ret1(pe):
            pe.wait_ge(*ea1.at("y"))
            for h in range(4):
                for e in range(4):
                    mm = pe.matmul(ps[:, 4, NS * h:NS * h + NS], C("mean512"), ys1[:, 4 * h + e, :],
                                   start=(e == 0), stop=(e == 3))
            mm.then_inc(*ep2.step("mean"))
            pe.wait_ge(*ea1.at("ysq"))
            for h in range(4):
                for e in range(4):
                    mm = pe.matmul(ps[:, 5, NS * h:NS * h + NS], C("mean512"), yq1[:, 4 * h + e, :],
                                   start=(e == 0), stop=(e == 3))
            mm.then_inc(*ep2.step("var"))

        def act_high(act, base, c, i=0, free=None):
            act.wait_ge(s_chunk[c % 4], 16 * (base // 4 + c // 4 + 1) + 16 * i)
            if free:
                act.wait_ge(*free)
            nc.scalar.activation(wh[c % 2], raw[c % 4], ACT.Copy).then_inc(s_wh, 1)

        def dve_low(dve, base, c, i=0):
            dve.wait_ge(s_wh, (base + c + 1) + 4 * i)
            nc.vector.tensor_tensor(wl[c % 2], raw[c % 4], wh[c % 2].bitcast(F32), ALU.subtract).then_inc(s_wl, 1)

        def pe_chunk(pe, base, c, i, par, x, lo, start, stop, waits=None):
            pe.wait_ge(s_wl, (base + c + 1) + 4 * i)
            for kt in range(8):
                if waits:
                    for w in waits(kt):
                        pe.wait_ge(*w)
                at = slice(kt * P, (kt + 1) * P)
                for w, y in [(wh, x), (wh, lo), (wl, x)]:
                    for hf in range(2):
                        mm = pe.matmul(ps[:, 2 * par + hf, 0:HALF], w[c % 2][:, at], y(kt, hf),
                                       start=(start and kt == 0 and w is wh and y is x),
                                       stop=(stop and kt == 7 and w is wl))
            return mm

        part_of = lambda t, k0=0: (lambda kt, hf: t[:, k0 + kt, hf * HALF:(hf + 1) * HALF])

        def pe_split(pe, name, waits):
            t0, n = GEMMS[name][1], GEMMS[name][3]

            def tile(m, i=0, waits=None):
                pe.wait_ge(s_bank, (t0 + m + 1) + 4 * i)
                pe_chunk(pe, CHUNKS[name], m, i, m % 2, part_of(xh), part_of(xl), True, True,
                         waits).then_inc(s_tile, 1)
            with pe.Fori(0, n // 4) as i:
                for m in range(4):
                    tile(m, i, waits if m == 0 else None)
            for m in range(n - n % 4, n):
                tile(m)

        def act_qkv(act):
            t0, base = GEMMS["qkv"][1], CHUNKS["qkv"]
            with act.Fori(0, 7) as i:
                for m in range(4):
                    act_high(act, base, m + 2, i, (s_tile, (t0 + m + 1) + 4 * i))
            for c in (30, 31):
                act_high(act, base, c, 0, (s_tile, t0 + c - 1))

        def dve_x_low(dve, x, gain, kt):
            nc.vector.scalar_tensor_tensor(xl[:, kt, :], x[:, kt, :], V("norm_g", gain * 8 + kt),
                                           xh[:, kt, :].bitcast(F32), ALU.mult, ALU.subtract).then_inc(s_xl, 1)

        def pe_ffn(pe, lyr):
            for part in range(2):
                up, down = f"up{lyr}{'ab'[part]}", f"down{lyr}{'ab'[part]}"
                t0 = GEMMS[up][1]
                with pe.Fori(0, HH // 4) as i:
                    for m in range(4):
                        pe.wait_ge(s_bank, (t0 + m + 1) + 4 * i)
                        waits = None
                        if part == 0 and m == 0:
                            waits = lambda kt: [(s_xg, 8 * (2 * lyr + 1) + kt + 1), (s_xl, 8 + 24 * lyr + kt + 1)]
                        pe_chunk(pe, FFN_CHUNKS[lyr], 32 * part + m, i, m % 2, part_of(xh), part_of(xl), True, True,
                                 waits).then_inc(s_tile, 1)
                t0 = GEMMS[down][1]
                with pe.Fori(0, KD // 2) as i:
                    for m in range(2):
                        pe.wait_ge(s_bank, (t0 + m + 1) + 2 * i)
                        for k in range(2):
                            waits = None
                            if m == 0:
                                waits = lambda kt, k=k: [(s_hl, 32 * lyr + 16 * part + 8 * k + kt + 3)]
                            mm = pe_chunk(pe, FFN_CHUNKS[lyr], 32 * part + 16 + 2 * m + k, i, m, part_of(hh, 8 * k),
                                          part_of(hl, 8 * k), k == 0, k == 1, waits)
                            mm.then_inc([s_half, s_tile][k], 1)

        def act_ffn(act, lyr, out):
            a = nc.scalar
            for part in range(2):
                up, down = f"up{lyr}{'ab'[part]}", f"down{lyr}{'ab'[part]}"
                t0 = GEMMS[up][1]
                with act.Fori(0, HH // 4) as i:
                    for m in range(4):
                        act_high(act, FFN_CHUNKS[lyr], 32 * part + m + 2, i, (s_tile, (t0 + m + 1) + 4 * i))
                        act.wait_ge(s_bank, (t0 + m + 3) + 4 * i)
                        act.wait_ge(s_hl, (32 * lyr + 16 * part + m + 1) + 4 * i)
                        a.activation(sqr[m % 2], tmp[m % 2], ACT.Square).then_inc(s_hid, 1)
                        act.wait_ge(s_hid, (32 * lyr + 16 * part + m + 3) + 4 * i)
                        a.activation(hh[:, ds(4 * i + m, 1), :].squeeze(1), sqr[m % 2], ACT.Copy).then_inc(s_hh, 1)
                t0 = GEMMS[down][1]

                def down_tile(m, i, last):
                    c = 32 * part + 16 + 2 * m + 2
                    if not last:
                        act_high(act, FFN_CHUNKS[lyr], c, i, (s_half, (16 * lyr + 8 * part + m + 1) + 2 * i))
                        act_high(act, FFN_CHUNKS[lyr], c + 1, i, (s_tile, (t0 + m + 1) + 2 * i))
                    if part == 0:
                        act.wait_ge(s_tile, (t0 + m + 1) + 2 * i)
                        act.wait_ge(s_bank, (t0 + m + 2) + 2 * i)
                        a.activation(two(out[:, ds(2 * i + m, 1), :].squeeze(1)), bank(m), ACT.Copy).then_inc(s_bank, 1)
                    else:
                        n = 8 * (2 * lyr + 1)
                        act.wait_ge(s_bank, (t0 + m + 3) + 2 * i)
                        act.wait_ge(s_ss, (n + m - 1) + 2 * i)
                        a.activation(sqr[m], out[:, ds(2 * i + m, 1), :].squeeze(1), ACT.Square).then_inc(s_sq, 1)
                with act.Fori(0, KD // 2 - part) as i:
                    for m in range(2):
                        down_tile(m, i, False)
                if part:
                    down_tile(0, KD // 2 - 1, False)
                    down_tile(1, KD // 2 - 1, True)

        def dve_ffn(dve, lyr, out):
            v = nc.vector
            for part in range(2):
                up, down = f"up{lyr}{'ab'[part]}", f"down{lyr}{'ab'[part]}"
                t0 = GEMMS[up][1]
                with dve.Fori(0, HH // 4) as i:
                    for m in range(4):
                        dve.wait_ge(s_tile, (t0 + m + 1) + 4 * i)
                        dve.wait_ge(s_bank, (t0 + m + 2) + 4 * i)
                        dve.wait_ge(s_hid, (32 * lyr + 16 * part + m + 1) + 4 * i)
                        v.scalar_tensor_tensor(two(tmp[m % 2]), bank(m % 2), 0.0, two(rb), ALU.max,
                                               ALU.mult).then_inc(s_bank, 1)
                        dve_low(dve, FFN_CHUNKS[lyr], 32 * part + m + 2, i)
                        dve.wait_ge(s_hh, (32 * lyr + 16 * part + m + 1) + 4 * i)
                        at = ds(4 * i + m, 1)
                        v.tensor_tensor(hl[:, at, :].squeeze(1), sqr[m % 2], hh[:, at, :].squeeze(1).bitcast(F32),
                                        ALU.subtract).then_inc(s_hl, 1)
                t0 = GEMMS[down][1]

                def down_tile(m, i, last):
                    c = 32 * part + 16 + 2 * m + 2
                    if not last:
                        dve_low(dve, FFN_CHUNKS[lyr], c, i)
                        dve_low(dve, FFN_CHUNKS[lyr], c + 1, i)
                    if part:
                        dve.wait_ge(s_tile, (t0 + m + 1) + 2 * i)
                        o = two(out[:, ds(2 * i + m, 1), :].squeeze(1))
                        v.tensor_tensor(o, bank(m), o, ALU.add).then_inc(s_bank, 1)
                with dve.Fori(0, KD // 2 - part) as i:
                    for m in range(2):
                        down_tile(m, i, False)
                if part:
                    down_tile(0, KD // 2 - 1, False)
                    down_tile(1, KD // 2 - 1, True)

        def pe_proj(pe, lyr):
            pe.wait_ge(s_pj_w, 16 * (lyr + 1))
            pe.wait_ge(s_pt, 16 * (lyr + 1))
            pe.wait_ge(s_rt, 4 * lyr + 4)
            for mt in range(KD):
                if mt >= 2:
                    pe.wait_ge(s_pjc, 8 * lyr + mt - 1)
                for kt in range(KP):
                    for hf in range(2):
                        at = (mt * KP + kt) * P
                        mm = pe.matmul(ps[:, 4 + 2 * (mt % 2) + hf, 0:HALF], pjw[:, at:at + P],
                                       pt[:, kt, hf * HALF:(hf + 1) * HALF], start=(kt == 0), stop=(kt == KP - 1))
                mm.then_inc(s_pj, 1)

        def act_ple(act, lyr, hn, more):
            a = nc.scalar
            for mt in range(KD):
                act.wait_ge(s_pj, 8 * lyr + mt + 1)
                p4 = 4 + 2 * (mt % 2)
                a.activation(two(hid[:, mt, :]), ps[:, p4:p4 + 2, 0:HALF], ACT.Copy).then_inc(s_pjc, 1)
            for mt in range(KD + 1):
                if mt < KD:
                    act.wait_ge(s_tile, tile_at(f"gate{lyr}", mt))
                    if mt >= 2:
                        act.wait_ge(s_hn, 8 * lyr + mt - 1)
                    a.activation(two(sqr[mt % 2]), bank(mt % 2), ACT.Exp, scale=-1.0).then_inc(s_bank, 1)
                if mt and more:
                    kt = mt - 1
                    act.wait_ge(s_hn, 8 * lyr + mt)
                    a.activation(xh[:, kt, :], hn[:, kt, :], ACT.Copy, scale=V("norm_g", 32 + kt))
                    a.activation(hid[:, 24 + kt, :], hn[:, kt, :], ACT.Square).then_inc(s_xg, 1)

        def dve_ple(dve, lyr, h, hn):
            v = nc.vector
            _, t0, _, _, _ = GEMMS[f"gate{lyr}"]
            for mt in range(KD):
                e = sqr[mt % 2]
                n = 24 * lyr + 3 * mt
                dve.wait_ge(s_bank, t0 + mt + 3)
                v.tensor_scalar(e, e, 1.0, None, ALU.add).then_inc(s_pl, 1)
                dve.wait_ge(s_pl, n + 1)
                v.reciprocal(e, e).then_inc(s_pl, 1)
                dve.wait_ge(s_pl, n + 2)
                dve.wait_ge(s_pjc, 8 * lyr + mt + 1)
                v.tensor_tensor(e, e, hid[:, mt, :], ALU.mult).then_inc(s_pl, 1)
                dve.wait_ge(s_pl, n + 3)
                v.tensor_tensor(hn[:, mt, :], h[:, mt, :], e, ALU.add).then_inc(s_hn, 1)

        def dve_gate_g(dve):
            v = nc.vector
            t0, base = GEMMS["g"][1], CHUNKS["g"]

            def four(i, last=False):
                for m in range(4):
                    dve.wait_ge(s_tile, (t0 + m + 1) + 4 * i)
                    v.tensor_tensor(two(tmp[m % 2]), bank(m % 2), two(rb), ALU.mult).then_inc(s_bank, 1)
                    if not last or m < 2:
                        dve_low(dve, base, m + 2, i)
                    dve.wait_ge(s_silu, (m + 1) + 4 * i)
                    y = hid[:, ds(4 * i + (16 + m), 1), :].squeeze(1)
                    v.tensor_tensor(y, y, tmp[m % 2], ALU.mult).then_inc(s_yg, 1)
            with dve.Fori(0, 3) as i:
                four(i)
            four(3, True)

        def act_gate_g(act):
            t0, base = GEMMS["g"][1], CHUNKS["g"]

            def four(i, last=False):
                for m in range(4):
                    if not last or m < 2:
                        act_high(act, base, m + 2, i, (s_tile, (t0 + m + 1) + 4 * i))
                    act.wait_ge(s_bank, (t0 + m + 3) + 4 * i)
                    nc.scalar.activation(tmp[m % 2], tmp[m % 2], ACT.Silu).then_inc(s_silu, 1)
            with act.Fori(0, 3) as i:
                four(i)
            four(3, True)
        s_silu, s_yg = sem("gate_silu"), sem("gated")
        s_x2, s_st1 = sem("x_reloaded"), sem("rwkv_sample_state_stored")
        s_ro = [sem(f"ret_state_stored{i}") for i in range(4)]

        block = ctx.enter_context(nc.Block())
        cols = lambda hf, off=0: slice(off + hf * HALF, off + (hf + 1) * HALF)

        @block.sync
        def _(sp):
            ng = VEC["norm_g"][1]
            sp.dma_start(vec[:, 0:ng], dram["vec"][:, 0:ng]).then_inc(s_first, 16)
            sp.dma_start(con[:, 0:P], dram["con"][:, 0:P]).then_inc(s_first, 16)
            for k in range(4):
                part_k = slice(2 * T * k, 2 * T * (k + 1))
                sp.dma_start(hbuf[0][:, part_k], dram["x"][:, part_k]).then_inc(s_x[k], 16)

            def slabs(name, first=0, last=None, prev=None):
                slab0, tile0, n, ntiles, per = GEMMS[name]
                last = n // 2 if last is None else last
                if first == 0:
                    for s in range(2):
                        if prev:
                            _, pt0, pn, ptiles, pper = GEMMS[prev]
                            sp.wait_ge(s_tile, pt0 + min(ptiles, (pn - 1 + s) * pper))
                        sp.dma_start(slot[s][:, :], dram["w"][slab0 + s]).then_inc(s_w[s], 16)
                if last > max(first, 1):
                    with sp.Fori(max(first, 1), last) as i:
                        for s in range(2):
                            sp.wait_ge(s_tile, (tile0 + (s + 1) * per - 2 * per) + 2 * per * i)
                            sp.dma_start(slot[s][:, :], dram["w"][slab0 + 2 * i + s]).then_inc(s_w[s], 16)

            def chunks(name, slabs, before=None, first=0):
                slab0, base = GEMMS[name][0], CHUNKS[name]
                if first == 0:
                    if before:
                        sp.wait_ge(s_tile, before)
                    for c in range(4):
                        sp.dma_start(raw[c], dram["w"][slab0][:, c * CHUNK:(c + 1) * CHUNK]).then_inc(s_chunk[c], 16)
                if slabs > 1:
                    with sp.Fori(1, slabs) as i:
                        for c in range(4):
                            sp.wait_ge(s_wl, (base + c - 3) + 4 * i)
                            sp.dma_start(raw[c], dram["w"][slab0 + i][:, c * CHUNK:(c + 1) * CHUNK]).then_inc(s_chunk[c], 16)

            def mlp_weights(lyr, before):
                chunks(f"up{lyr}a", 16, before)
                _, t0, _, n, _ = GEMMS[f"up{lyr}b"]
                sp.wait_ge(s_tile, t0 + n)
                sp.dma_start(pjw[:, :], dram["pjw"][lyr]).then_inc(s_pj_w, 16)
                sp.wait_ge(s_wl, FFN_CHUNKS[lyr] + 64)
                g0 = GEMMS[f"gate{lyr}"][0]
                sp.dma_start(slot[0][:, :], dram["w"][g0]).then_inc(s_w[0], 16)
                _, t0, _, n, _ = GEMMS[f"down{lyr}b"]
                sp.wait_ge(s_tile, t0 + n)
                sp.dma_start(slot[1][:, :], dram["w"][g0 + 1]).then_inc(s_w[1], 16)

            chunks("in0", 1)
            sp.dma_start(vec[:, ng:], dram["vec"][:, ng:]).then_inc(s_vec, 16)
            sp.dma_start(con[:, P:], dram["con"][:, P:]).then_inc(s_con, 16)
            chunks("in0", 8, first=1)
            sp.wait_ge(s_raw, NA + 8)
            store(sp, dram["sho"], sho.rearrange("p a b -> p (a b)"))
            store(sp, dram["cvo"], cvo.rearrange("p a b -> p (a b)"))
            store(sp, dram["conv_o"], V("conv", 0, 192))
            sp.wait_ge(*row_d.at("tm"))
            store(sp, dram["mo"], mo[0:4])
            for h in range(2):
                sp.wait_ge(*rw[h]["dve"].at("out", NG - 1))
                sp.dma_start(dram["rs_o"][h], s_end[h].rearrange("p a b -> p (a b)")).then_inc(s_rs, 16)
            sp.dma_start(sst.rearrange("p j s n -> p (j s n)"), dram["sst"]).then_inc(s_sst, 16)
            sp.dma_start(cst.rearrange("p h s n -> p (h s n)"), dram["cst"]).then_inc(s_cst, 16)
            w0 = GEMMS["out0"][0]
            sp.dma_start(slot[0][:, :], dram["w"][w0]).then_inc(s_w[0], 16)
            sp.wait_ge(*sdj.at("s", 3))
            sp.dma_start(dram["sst_o"], sst.rearrange("p j s n -> p (j s n)")).then_inc(s_st1, 16)
            sp.wait_ge(*nd.at("n"))
            store(sp, dram["n_o"], n_new.rearrange("p h n -> p (h n)"))
            sp.wait_ge(*md.at("out", NG - 1))
            store(sp, dram["cn_o"], cn.rearrange("p h n -> p (h n)"))
            sp.wait_ge(*ndj.at("c", 3))
            sp.dma_start(dram["cst_o"], cst.rearrange("p h s n -> p (h s n)")).then_inc(s_cso, 16)
            sp.wait_ge(*nd2.at("out"))
            sp.wait_ge(s_cso, 16)
            sp.dma_start(slot[1][:, :], dram["w"][w0 + 1]).then_inc(s_w[1], 16)
            assert outs[0] == MIXER_STORES
            sp.wait_ge(s_out, MIXER_STORES)
            sp.wait_ge(s_rs, 32)
            sp.dma_start(hbuf[0][:, :], dram["x"]).then_inc(s_x2, 16)
            sp.dma_start(pt.rearrange("p k t -> p (k t)"), dram["pt"][0]).then_inc(s_pt, 16)
            mlp_weights(0, GEMMS["out0"][1] + 4)
            chunks("qkv", 8, GEMMS["gate0"][1] + 4)
            sp.wait_ge(s_wl, CHUNKS["g"])
            chunks("g", 1)
            sp.wait_ge(s_tile, GEMMS["qkv"][1] + GEMMS["qkv"][3])

            def ret_load(it, s):
                sp.dma_start(ring[s].rearrange("p k n -> p (k n)"), dram["rst"][it]).then_inc(s_rin[s], 16)

            def ret_store(it, s):
                sp.wait_ge(s_up, it + 1)
                sp.dma_start(dram["rst_o"][it], ring[s].rearrange("p k n -> p (k n)")).then_inc(s_ro[s], 16)
            for s in range(4):
                ret_load(s, s)
            ret_store(0, 0)
            ret_store(1, 1)
            with sp.Fori(0, 7) as i:
                for s in range(4):
                    ret_store(4 * i + (2 + s), (2 + s) % 4)
                    sp.wait_ge(s_read, 4 * i + (s + 1))
                    sp.wait_ge(s_ro[s], 16 * i + 16)
                    ret_load(4 * i + (4 + s), s)
            ret_store(30, 2)
            ret_store(31, 3)
            sp.wait_ge(*ed.at("out3", NG - 1))
            sp.dma_start(dram["rS_o"], rS.rearrange("p h k n -> p (h k n)")).then_inc(s_prs, 16)
            chunks("g", 4, first=1)
            sp.wait_ge(s_wl, CHUNKS["g"] + 16)
            o0 = GEMMS["out1"][0]
            sp.dma_start(slot[0][:, :], dram["w"][o0]).then_inc(s_w[0], 16)
            sp.wait_ge(s_tile, GEMMS["out1"][1])
            sp.dma_start(slot[1][:, :], dram["w"][o0 + 1]).then_inc(s_w[1], 16)
            slabs("out1", 1)
            sp.wait_ge(*ea1.at("sd"))
            sp.wait_ge(*ed2.at("out"))
            sp.wait_ge(s_pj, 8)
            sp.dma_start(pt.rearrange("p k t -> p (k t)"), dram["pt"][1]).then_inc(s_pt, 16)
            mlp_weights(1, GEMMS["out1"][1] + 6)
            for mt in range(KD):
                sp.wait_ge(s_hn, 8 + mt + 1)
                store(sp, dram["y"][:, mt * T:(mt + 1) * T], hb[0][:, mt, :])
            sp.wait_ge(s_out, outs[0])
            sp.wait_ge(s_rs, 32)
            sp.wait_ge(s_st1, 16)
            sp.wait_ge(s_cso, 16)
            sp.wait_ge(s_prs, 16)
            for s in range(4):
                sp.wait_ge(s_ro[s], 128)

        @block.tensor
        def _(pe):
            stream = lambda t: (lambda kt, hf: t[:, kt, cols(hf)])
            pe.wait_ge(s_first, 32)
            pe_prenorm(pe, 0)
            pe_split(pe, "in0", lambda kt: [(s_xl, kt + 1)])
            pe_in0(pe)
            pe_rwkv(pe)
            in_turn(one_step(pe_rwkv1(pe), pe_mlstm1(pe)), pe_mlstm(pe))
            pe.wait_ge(*nd2.at("out"))
            pe.wait_ge(*md.at("out", NG - 1))
            gemm(pe, "out0", KD, lambda kt, hf: ua[:, kt, cols(hf, 1)] if kt < 4 else ub[:, kt - 4, cols(hf)])
            pe_postnorm(pe, 0)
            pe_prenorm(pe, 1)
            pe_ffn(pe, 0)
            pe_postnorm(pe, 1)
            pe_proj(pe, 0)
            gemm(pe, "gate0", KD, stream(hb[0]), lambda kt: (s_h, 8 + kt + 1))
            pe_prenorm(pe, 2)
            pe_split(pe, "qkv", lambda kt: [(s_xl, 16 + kt + 1)])
            pe_ret(pe)
            pe_ret1(pe)
            pe_split(pe, "g", lambda kt: [(s_xl, 24 + kt + 1)])
            gemm(pe, "out1", 16, lambda kt, hf: hid[:, 16 + kt, cols(hf)], lambda kt: (s_yg, kt + 1))
            pe_postnorm(pe, 2)
            pe_prenorm(pe, 3)
            pe_ffn(pe, 1)
            pe_postnorm(pe, 3)
            pe_proj(pe, 1)
            gemm(pe, "gate1", KD, stream(hb[1]), lambda kt: (s_h, 24 + kt + 1))

        @block.scalar
        def _(act):
            act.wait_ge(s_first, 32)
            act_prenorm(act, 0, hb[0], 0, lambda kt: (s_x[kt // 2], 16), xh)
            for c in range(2):
                act_high(act, 0, c)
            act_rms(act, 0)
            act_in0(act)
            act_rwkv(act)
            in_turn(one_step(act_rwkv1(act), act_mlstm1(act)), act_mlstm(act))
            act.wait_ge(s_out, MIXER_STORES)
            act_outproj(act, "out0", 0, hb[1])
            for c in range(2):
                act_high(act, FFN_CHUNKS[0], c, 0, (s_tile, GEMMS["up0a"][1]))
            act_rms(act, 1)
            act_prenorm(act, 1, hb[0], 2, lambda kt: (s_h, kt + 1), xh)
            act_rms(act, 2)
            act_ffn(act, 0, hb[1])
            act_rms(act, 3)
            act_ple(act, 0, hb[1], True)
            for c in range(2):
                act_high(act, CHUNKS["qkv"], c, 0, (s_tile, GEMMS["qkv"][1]))
            act_rms(act, 4)
            act_qkv(act)
            act_ret(act)
            act_ret1(act)
            act.wait_ge(s_read, 32)
            for s in range(4):
                act.wait_ge(s_ro[s], 128)
            for c in range(2):
                act_high(act, CHUNKS["g"], c)
            act_gate_g(act)
            act.wait_ge(s_prs, 16)
            act_outproj(act, "out1", 2, hb[0])
            for c in range(2):
                act_high(act, FFN_CHUNKS[1], c, 0, (s_tile, GEMMS["up1a"][1]))
            act_rms(act, 5)
            act_prenorm(act, 3, hb[1], 6, lambda kt: (s_h, 16 + kt + 1), xh)
            act_rms(act, 6)
            act_ffn(act, 1, hb[0])
            act_rms(act, 7)
            act_ple(act, 1, hb[0], False)

        @block.vector
        def _(dve):
            nc.vector.memset(tmp[0][:, 0:1], 0.0).then_inc(s_bank, 2)
            nc.vector.memset(tmp[1][:, 0:1], 0.0).then_inc(s_hid, 2)
            nc.vector.memset(tmp[1][:, 1:2], 0.0).then_inc(s_hl, 2)
            for n, s in enumerate([rw[0]["dve"].sem, rw[1]["dve"].sem, md.sem, ed.sem, s_shf, s_cvd, s_cvd, s_rope]):
                nc.vector.memset(tmp[0][:, n + 1:n + 2], 0.0).then_inc(s, 1)
            for kt in range(KD):
                dve.wait_ge(s_xg, kt + 1)
                dve_x_low(dve, hb[0], 0, kt)
            for c in range(2):
                dve_low(dve, 0, c)
            dve_rinv(dve, 0)
            dve_in0(dve)
            dve_rwkv(dve)
            in_turn(one_step(dve_rwkv1(dve), dve_mlstm1(dve)), dve_mlstm(dve))
            for c in range(2):
                dve_low(dve, FFN_CHUNKS[0], c)
            dve_rinv(dve, 1)
            dve.wait_ge(s_x2, 16)
            dve_residual(dve, 0, hb[1], hb[0], 1, (0, 2))
            dve_rinv(dve, 2)
            dve_ffn(dve, 0, hb[1])
            dve_rinv(dve, 3)
            dve_residual(dve, 1, hb[1], hb[0], 3)
            dve_ple(dve, 0, hb[0], hb[1])
            for c in range(2):
                dve_low(dve, CHUNKS["qkv"], c)
            dve.wait_ge(s_xg, 24)
            for kt in range(KD):
                dve_x_low(dve, hb[1], 4, kt)
            dve_rinv(dve, 4)
            dve_qkv(dve)
            dve_ret(dve)
            dve_ret1(dve)
            for kt in range(KD):
                dve_x_low(dve, hb[1], 4, kt)
            for c in range(2):
                dve_low(dve, CHUNKS["g"], c)
            dve_gate_g(dve)
            for c in range(2):
                dve_low(dve, FFN_CHUNKS[1], c)
            dve_rinv(dve, 5)
            dve_residual(dve, 2, hb[0], hb[1], 5, (1, 6))
            dve_rinv(dve, 6)
            dve_ffn(dve, 1, hb[0])
            dve_rinv(dve, 7)
            dve_residual(dve, 3, hb[0], hb[1], 7)
            dve_ple(dve, 1, hb[1], hb[0])

        @block.gpsimd
        def _(pool):
            pool_in0(pool)
            pool_rwkv(pool)
            for n in range(4):
                pool_sum(pool, n)


INS = {"vec": (P, NVEC), "con": (P, NCON), "x": (P, KD * T), "w": (NSLAB, P, SLAB), "pjw": (2, P, KP * KD * P),
       "pt": (2, P, KP * T), "sst": (P, 4 * NS * 64), "cst": (P, 4 * NS * P), "rst": (32, P, 2 * CDV)}
OUTS = {"y": (P, KD * T), "sho": (P, NA * (NS + 1)), "cvo": (P, 88), "conv_o": (P, 192), "mo": (4, NS + 1),
        "rs_o": (2, P, 2 * P), "sst_o": (P, 4 * NS * 64), "cn_o": (P, BH * 2 * P), "n_o": (P, BH * NS),
        "cst_o": (P, 4 * NS * P), "rS_o": (P, 4 * 2 * CDV), "rst_o": (32, P, 2 * CDV)}


def lay_out(i):
    def fm(v):
        v = np.asarray(v)
        return v.reshape(-1, P).T

    def slabs(w):
        k, n = w.shape
        b = w.reshape(k // P, P, n // P, P).transpose(2, 0, 1, 3).reshape(-1, P, P)
        pad = -len(b) % 32
        b = np.concatenate([b, np.zeros((pad, P, P), b.dtype)]) if pad else b
        return b.reshape(-1, 32, P, P).transpose(0, 2, 1, 3).reshape(-1, P, SLAB)

    f = np.float32
    vec = np.zeros((P, NVEC), f)

    def put(name, a, rows=P):
        at, n = VEC[name]
        vec[:rows, at:at + n] = np.asarray(a).reshape(rows, n)

    put("norm_g", np.concatenate([fm(i["norm_g"][l, k]) for l in range(2) for k in range(4)], 1))
    put("mu", fm(i["rw_mu"][0]))
    for name, key in [("w0", "rw_w0"), ("a0", "rw_a0"), ("kk", "rw_kk"), ("ka", "rw_ka"), ("rk", "rw_rk"),
                      ("rln", "rw_ln"), ("mgn", "ml_gn"), ("cb", "ml_conv_b"), ("rgn", "ret_gn")]:
        put(name, fm(i[key][0]))
    put("cw", np.concatenate([fm(i["ml_conv_w"][0, j]) for j in range(4)], 1))
    put("ib", i["ml_i_bias"][0], 4)
    put("fb", i["ml_f_bias"][0], 4)
    put("m", i["state_mlstm_m"][0].T, 4)
    put("shift", i["state_rwkv_shift"][0].reshape(NS, NA, P).transpose(2, 1, 0))
    put("conv", i["state_mlstm_conv"][0].reshape(NS, 3, 8, P).transpose(3, 2, 1, 0))
    put("n", i["state_mlstm_n"][0].transpose(2, 1, 0))
    w_in = i["mix0_w_in"][0]
    na, nb = NA * P, (NA + NB) * P
    wif = np.zeros((KD, P, 36), f)
    wif[:, :, 0:4] = w_in[:, nb:nb + 4].reshape(KD, P, 4)
    wif[:, :, 32:36] = w_in[:, nb + 4:nb + 8].reshape(KD, P, 4)
    put("wif", wif.transpose(1, 0, 2))
    put("w2a2", np.concatenate([i["rw_w2"][0], i["rw_a2"][0]], 0))
    put("g2", i["rw_g2"][0])
    hf = HH * P

    def mlp(l):
        up, down = i["ffn_up"][l], i["ffn_down"][l]
        return up[:, :hf], down[:hf], up[:, hf:], down[hf:]
    big = [w_in[:, :nb], i["mix0_w_out"][0], *mlp(0), i["ple_gate"][0], i["ret_w_in"][0], i["ret_w_out"][0],
           *mlp(1), i["ple_gate"][1]]

    def tokens(a, b):
        t = np.concatenate([a[0], b[:, 0]], 0).T
        return t.reshape(-1, P, T).transpose(1, 0, 2).reshape(P, -1)

    return {
        "vec": vec, "con": shape_constants(), "x": tokens(i["x_prompt"], i["x_sample"]),
        "w": np.concatenate([slabs(w) for w in big]),
        "pjw": np.stack([slabs(i["ple_proj"][l])[0][:, :KP * KD * P] for l in range(2)]),
        "pt": np.stack([tokens(i["p_prompt"][l], i["p_sample"][l]) for l in range(2)]),
        "sst": i["state_rwkv_S"][0].reshape(NS, 4, 2, 64, 64).transpose(2, 4, 1, 0, 3).reshape(P, -1),
        "cst": i["state_mlstm_C"][0].transpose(2, 1, 0, 3).reshape(P, -1),
        "rst": i["state_ret_S"][0].reshape(4, 2, 4, 2, P, CDV).transpose(0, 2, 1, 4, 3, 5).reshape(32, P, -1),
    }


def unpack(o):
    y = o["y"].reshape(P, KD, T).transpose(2, 1, 0).reshape(T, D)
    sho = o["sho"].reshape(P, NA, NS + 1).transpose(2, 1, 0).reshape(NS + 1, NA * P)
    cvo = o["cvo"].reshape(P, 8, 11).transpose(2, 1, 0).reshape(11, 8 * P)
    conv = o["conv_o"].reshape(P, 8, 3, NS).transpose(3, 2, 1, 0).reshape(NS, 3, 8 * P)
    rs = o["rs_o"].reshape(2, 2, 64, 2, 2, 64)
    rs = np.stack([rs[:, q, :, :, q, :] for q in range(2)], 3).transpose(0, 2, 3, 4, 1)
    sst = o["sst_o"].reshape(2, 64, 4, NS, 64).transpose(3, 2, 0, 4, 1).reshape(NS, 8, 64, 64)
    cn = o["cn_o"].reshape(P, 4, 2 * P).transpose(1, 0, 2)
    rS = o["rS_o"].reshape(P, 4, 2, CDV).transpose(1, 2, 0, 3).reshape(4, CDK, CDV)
    rst = o["rst_o"].reshape(4, 4, 2, P, 2, CDV).transpose(0, 2, 1, 4, 3, 5).reshape(NS, 4, CDK, CDV)
    c = np.ascontiguousarray
    return (c(y[None, :TP]), c(y[TP:, None]),
            c(sho[None, 0:1]), c(rs.reshape(1, 1, 8, 64, 64)), c(cvo[None, None, 0:3]), c(cn[None, None, :, :, 0:P]),
            c(cn[None, None, :, :, P]), c(o["mo"][:, 0][None, None]), c(rS[None, None]),
            c(sho[None, 1:]), c(sst[None]), c(np.concatenate([conv[:, 1:], cvo[3:, None]], 1)[None]),
            c(o["cst_o"].reshape(P, 4, NS, P).transpose(2, 1, 0, 3)[None]),
            c(o["n_o"].reshape(P, 4, NS).transpose(2, 1, 0)[None]), c(o["mo"][:, 1:].T[None]), c(rst[None]))


def kernel(**inputs):
    import concourse.bacc as bacc
    from concourse.bass_utils import run_bass_kernel_spmd

    nc = bacc.Bacc("TRN2", target_bir_lowering=False, num_devices=1)
    arrays = {k: np.ascontiguousarray(a) for k, a in lay_out({k: np.asarray(a) for k, a in inputs.items()}).items()}
    dram = {k: nc.dram_tensor(f"in_{k}", s, F32, kind="ExternalInput").ap() for k, s in INS.items()}
    dram.update({k: nc.dram_tensor(f"out_{k}", s, F32, kind="ExternalOutput").ap() for k, s in OUTS.items()})
    program(nc, **dram)
    r = run_bass_kernel_spmd(nc, [{f"in_{k}": a for k, a in arrays.items()}], core_ids=[0])
    return unpack({k: np.asarray(r.results[0][f"out_{k}"]) for k in OUTS})
```
